# Optimizing a Trainium2 kernel written in Bass

```python
import functools
import jax, jax.numpy as jnp
from jax import lax
import numpy as np

D_MODEL = 1024
BATCH = 1
SEQ = 1024
DEPTH = 1
DEC_BATCH = 8
DEC_SEQ = 16
PAST_LEN = 512

CHUNK = 64
Q_BLOCK = 128
EPS = 1e-6
NEG = -1e30
A_HEADS = 8
A_HEAD_DIM = 64
A_WIDTH = A_HEADS * A_HEAD_DIM
FOX_FORGET_BIAS = 2.0
B_HEADS = 4
B_QK_DIM = 128
B_V_DIM = 128
B_WIDTH = B_HEADS * B_V_DIM
MLSTM_FORGET_BIAS = 3.0
P_HEADS = 8
P_KEYS = 128
P_EXPERTS = P_KEYS * P_KEYS
P_KEY_DIM = 128
P_HALF = P_KEY_DIM // 2
P_TOPK = 16
P_BLOCK = 256
IN_SIZES = (A_WIDTH, A_WIDTH, A_WIDTH, A_HEADS,
            B_HEADS * B_QK_DIM, B_HEADS * B_QK_DIM, B_WIDTH, B_HEADS, B_HEADS, B_WIDTH,
            D_MODEL, D_MODEL)
IN_WIDTH = 3 * A_WIDTH + A_HEADS + 2 * B_HEADS * B_QK_DIM + 2 * B_WIDTH + 2 * B_HEADS + 2 * D_MODEL

kernel_name = "fox_mlstm_peer_streaming_encoder_step"

def _col(i):
    start = sum(IN_SIZES[:i])
    return start, start + IN_SIZES[i]

def _split_points():
    pts, acc = [], 0
    for s in IN_SIZES[:-1]:
        acc += s
        pts.append(acc)
    return pts

def rms_norm(x):
    xf = x.astype(jnp.float32)
    return (xf * lax.rsqrt(jnp.mean(xf * xf, axis=-1, keepdims=True) + EPS)).astype(x.dtype)

def fox_attend(q, F_q, q_pos, k, v, F_k):
    s = jnp.einsum('blhd,bshd->bhls', q, k).astype(jnp.float32) * (A_HEAD_DIM ** -0.5)
    s = s + F_q[..., None] - F_k[:, :, None, :]
    mask = jnp.arange(k.shape[1])[None, :] <= q_pos[:, None]
    p = jax.nn.softmax(jnp.where(mask, s, NEG), axis=-1).astype(v.dtype)
    return jnp.einsum('bhls,bshd->blhd', p, v)

def fox_prompt(q, k, v, logf):
    b, s, h, d = q.shape
    F = jnp.cumsum(logf, axis=1).transpose(0, 2, 1)
    def block(i):
        start = i * Q_BLOCK
        qi = lax.dynamic_slice_in_dim(q, start, Q_BLOCK, axis=1)
        Fi = lax.dynamic_slice_in_dim(F, start, Q_BLOCK, axis=2)
        return fox_attend(qi, Fi, start + jnp.arange(Q_BLOCK), k, v, F)
    o = lax.map(block, jnp.arange(s // Q_BLOCK))
    return jnp.moveaxis(o, 0, 1).reshape(b, s, h * d)

def fox_sample(q, k, v, logf, ck, cv, clf):
    b, L, h, d = q.shape
    past = ck.shape[1]
    kk = jnp.concatenate([ck.astype(k.dtype), k], axis=1)
    vv = jnp.concatenate([cv.astype(v.dtype), v], axis=1)
    F = jnp.cumsum(jnp.concatenate([clf.astype(jnp.float32), logf], axis=1), axis=1).transpose(0, 2, 1)
    o = fox_attend(q, F[:, :, past:], past + jnp.arange(L), kk, vv, F)
    return o.reshape(b, L, h * d)

def mlstm_chunk(carry, inp):
    C0, n0, m0 = carry
    q, k, v, ig, lf = inp
    L = q.shape[1]
    bcum = jnp.cumsum(lf, axis=1).transpose(0, 2, 1)
    it = ig.transpose(0, 2, 1)
    causal = jnp.tril(jnp.ones((L, L), dtype=bool))
    dmat = jnp.where(causal, bcum[..., :, None] - bcum[..., None, :] + it[..., None, :], NEG)
    inter = m0[..., None] + bcum
    m = jnp.maximum(dmat.max(axis=-1), inter)
    w = jnp.exp(dmat - m[..., None])
    a = jnp.exp(inter - m)
    ws = w * jnp.einsum('bthd,bshd->bhts', q, k)
    num = jnp.einsum('bhts,bshv->bthv', ws, v) + jnp.einsum('bht,bthd,bhdv->bthv', a, q, C0)
    den = ws.sum(axis=-1) + a * jnp.einsum('bthd,bhd->bht', q, n0)
    h = num / jnp.maximum(jnp.abs(den), jnp.exp(-m)).transpose(0, 2, 1)[..., None]
    mL = m[..., -1]
    wL = jnp.exp(bcum[..., -1:] - bcum + it - mL[..., None])
    aL = jnp.exp(m0 + bcum[..., -1] - mL)
    C = aL[..., None, None] * C0 + jnp.einsum('bhs,bshd,bshv->bhdv', wL, k, v)
    n = aL[..., None] * n0 + jnp.einsum('bhs,bshd->bhd', wL, k)
    return (C, n, mL), h

def mlstm_prompt(q, k, v, ig, lf):
    b, s = q.shape[:2]
    nc = s // CHUNK
    def chunks(t):
        return jnp.swapaxes(t.reshape((b, nc, CHUNK) + t.shape[2:]), 0, 1)
    init = (jnp.zeros((b, B_HEADS, B_QK_DIM, B_V_DIM), jnp.float32),
            jnp.zeros((b, B_HEADS, B_QK_DIM), jnp.float32),
            jnp.zeros((b, B_HEADS), jnp.float32))
    state, h = lax.scan(mlstm_chunk, init, (chunks(q), chunks(k), chunks(v), chunks(ig), chunks(lf)))
    return jnp.swapaxes(h, 0, 1).reshape(b, s, B_HEADS, B_V_DIM), state

def prompt_mix(qa, ka, va, lfa, qb, kb, vb, ib, lfb):
    ha = fox_prompt(qa, ka, va, lfa)
    hb, (C, n, m) = mlstm_prompt(qb, kb, vb, ib, lfb)
    return ha, hb, (ka, va, lfa, C, n, m)

def sample_mix(ck, cv, clf, C0, n0, m0, qa, ka, va, lfa, qb, kb, vb, ib, lfb):
    ha = fox_sample(qa, ka, va, lfa, ck, cv, clf)
    carry = (C0.astype(jnp.float32), n0.astype(jnp.float32), m0.astype(jnp.float32))
    (C, n, m), hb = mlstm_chunk(carry, (qb, kb, vb, ib, lfb))
    return ha, hb, (ka, va, lfa, C, n, m)

def peer(x, w_pq, sub_keys, expert_u, expert_v):
    n = x.shape[0]
    pad = (-n) % P_BLOCK
    xb = jnp.pad(x, ((0, pad), (0, 0))).reshape(-1, P_BLOCK, D_MODEL)
    def blk(xi):
        q = (xi @ w_pq).reshape(P_BLOCK, P_HEADS, 2, P_HALF)
        s = jnp.einsum('thpd,hpkd->thpk', q, sub_keys).astype(jnp.float32)
        sv, si = lax.top_k(s, P_TOPK)
        cand = (sv[:, :, 0, :, None] + sv[:, :, 1, None, :]).reshape(P_BLOCK, P_HEADS, P_TOPK * P_TOPK)
        cidx = (si[:, :, 0, :, None] * P_KEYS + si[:, :, 1, None, :]).reshape(P_BLOCK, P_HEADS, P_TOPK * P_TOPK)
        fv, fi = lax.top_k(cand, P_TOPK)
        eidx = jnp.take_along_axis(cidx, fi, axis=-1)
        g = jax.nn.softmax(fv, axis=-1)
        act = jax.nn.gelu(jnp.einsum('thkd,td->thk', expert_u[eidx], xi).astype(jnp.float32), approximate=False)
        return jnp.einsum('thk,thkd->td', (g * act).astype(xi.dtype), expert_v[eidx])
    return lax.map(blk, xb).reshape(-1, D_MODEL)[:n]

def trunk_layer(x, c, token_mix, w_mod, b_mod, g_norm1, g_norm2, w_in, b_in, g_qa, g_ka, g_hb,
                w_pa, w_pb, w_o, w_pq, sub_keys, expert_u, expert_v):
    bsz, L, _ = x.shape
    f32 = jnp.float32
    sh1, sc1, gt1, sh2, sc2, gt2 = jnp.split((jax.nn.silu(c) @ w_mod + b_mod)[:, None, :], 6, axis=-1)
    h = rms_norm(x) * g_norm1 * (1.0 + sc1) + sh1
    z = h @ w_in + b_in
    aq, ak, av, af, bq, bk, bv, bi, bf, bo, ga, gb = jnp.split(z, _split_points(), axis=-1)
    qa = rms_norm(aq.reshape(bsz, L, A_HEADS, A_HEAD_DIM)) * g_qa
    ka = rms_norm(ak.reshape(bsz, L, A_HEADS, A_HEAD_DIM)) * g_ka
    va = av.reshape(bsz, L, A_HEADS, A_HEAD_DIM)
    lfa = jax.nn.log_sigmoid(af.astype(f32))
    qb = bq.reshape(bsz, L, B_HEADS, B_QK_DIM).astype(f32)
    kb = bk.reshape(bsz, L, B_HEADS, B_QK_DIM).astype(f32) * (B_QK_DIM ** -0.5)
    vb = bv.reshape(bsz, L, B_HEADS, B_V_DIM).astype(f32)
    ib = bi.astype(f32)
    lfb = jax.nn.log_sigmoid(bf.astype(f32))
    ha, hb, state = token_mix(qa, ka, va, lfa, qb, kb, vb, ib, lfb)
    hb = (rms_norm(hb) * g_hb).reshape(bsz, L, B_WIDTH).astype(x.dtype) * jax.nn.sigmoid(bo)
    merged = jax.nn.sigmoid(ga) * (ha @ w_pa) + jax.nn.sigmoid(gb) * (hb @ w_pb)
    x = x + gt1 * (merged @ w_o)
    h2 = rms_norm(x) * g_norm2 * (1.0 + sc2) + sh2
    y = peer(h2.reshape(bsz * L, D_MODEL), w_pq, sub_keys, expert_u, expert_v).reshape(bsz, L, D_MODEL)
    return x + gt2 * y, state

def setup_inputs(seed: int = 0) -> dict:
    key = jax.random.key(seed)
    ks = iter(jax.random.split(key, 32))
    def nrm(shape, scale):
        return jax.random.normal(next(ks), shape, jnp.float32) * scale
    D = D_MODEL
    x_prompt = nrm((BATCH, SEQ, D), 1.0)
    x_sample = nrm((DEC_BATCH, DEC_SEQ, D), 1.0)
    c_prompt = nrm((BATCH, D), 1.0)
    c_sample = nrm((DEC_BATCH, D), 1.0)
    cache_k = nrm((DEPTH, DEC_BATCH, PAST_LEN, A_HEADS, A_HEAD_DIM), 1.0)
    cache_v = nrm((DEPTH, DEC_BATCH, PAST_LEN, A_HEADS, A_HEAD_DIM), 1.0)
    cache_logf = jax.nn.log_sigmoid(FOX_FORGET_BIAS + nrm((DEPTH, DEC_BATCH, PAST_LEN, A_HEADS), 1.0))
    state_C = nrm((DEPTH, DEC_BATCH, B_HEADS, B_QK_DIM, B_V_DIM), 0.1)
    state_n = nrm((DEPTH, DEC_BATCH, B_HEADS, B_QK_DIM), 0.1)
    state_m = nrm((DEPTH, DEC_BATCH, B_HEADS), 1.0)
    w_mod = nrm((DEPTH, D, 6 * D), 0.3 * D ** -0.5)
    b_mod = nrm((DEPTH, 6 * D), 0.02)
    g_norm1 = 1.0 + nrm((DEPTH, D), 0.02)
    g_norm2 = 1.0 + nrm((DEPTH, D), 0.02)
    w_in = nrm((DEPTH, D, IN_WIDTH), D ** -0.5)
    fa0, fa1 = _col(3)
    fb0, fb1 = _col(8)
    b_in = nrm((DEPTH, IN_WIDTH), 0.02)
    b_in = b_in.at[:, fa0:fa1].add(FOX_FORGET_BIAS).at[:, fb0:fb1].add(MLSTM_FORGET_BIAS)
    g_qa = 1.0 + nrm((DEPTH, A_HEADS, A_HEAD_DIM), 0.02)
    g_ka = 1.0 + nrm((DEPTH, A_HEADS, A_HEAD_DIM), 0.02)
    g_hb = 1.0 + nrm((DEPTH, B_HEADS, B_V_DIM), 0.02)
    w_pa = nrm((DEPTH, A_WIDTH, D), A_WIDTH ** -0.5)
    w_pb = nrm((DEPTH, B_WIDTH, D), B_WIDTH ** -0.5)
    w_o = nrm((DEPTH, D, D), D ** -0.5)
    w_pq = nrm((DEPTH, D, P_HEADS * P_KEY_DIM), D ** -0.5)
    sub_keys = nrm((DEPTH, P_HEADS, 2, P_KEYS, P_HALF), P_HALF ** -0.5)
    expert_u = nrm((DEPTH, P_EXPERTS, D), D ** -0.5)
    expert_v = nrm((DEPTH, P_EXPERTS, D), P_HEADS ** -0.5)
    return {"x_prompt": x_prompt, "x_sample": x_sample, "c_prompt": c_prompt, "c_sample": c_sample,
            "cache_k": cache_k, "cache_v": cache_v, "cache_logf": cache_logf,
            "state_C": state_C, "state_n": state_n, "state_m": state_m,
            "w_mod": w_mod, "b_mod": b_mod, "g_norm1": g_norm1, "g_norm2": g_norm2,
            "w_in": w_in, "b_in": b_in, "g_qa": g_qa, "g_ka": g_ka, "g_hb": g_hb,
            "w_pa": w_pa, "w_pb": w_pb, "w_o": w_o, "w_pq": w_pq, "sub_keys": sub_keys,
            "expert_u": expert_u, "expert_v": expert_v}

def reference(x_prompt, x_sample, c_prompt, c_sample, cache_k, cache_v, cache_logf,
              state_C, state_n, state_m, w_mod, b_mod, g_norm1, g_norm2, w_in, b_in,
              g_qa, g_ka, g_hb, w_pa, w_pb, w_o, w_pq, sub_keys, expert_u, expert_v):
    y_p, y_s = x_prompt, x_sample
    new_p = [[] for _ in range(6)]
    new_s = [[] for _ in range(6)]
    for l in range(DEPTH):
        weights = (w_mod[l], b_mod[l], g_norm1[l], g_norm2[l], w_in[l], b_in[l], g_qa[l], g_ka[l], g_hb[l],
                   w_pa[l], w_pb[l], w_o[l], w_pq[l], sub_keys[l], expert_u[l], expert_v[l])
        y_p, st_p = trunk_layer(y_p, c_prompt, prompt_mix, *weights)
        mix_s = functools.partial(sample_mix, cache_k[l], cache_v[l], cache_logf[l],
                                  state_C[l], state_n[l], state_m[l])
        y_s, st_s = trunk_layer(y_s, c_sample, mix_s, *weights)
        for lst, arr in zip(new_p, st_p):
            lst.append(arr)
        for lst, arr in zip(new_s, st_s):
            lst.append(arr)
    return (y_p, y_s,
            jnp.stack(new_p[0]), jnp.stack(new_p[1]), jnp.stack(new_p[2]),
            jnp.stack(new_p[3]), jnp.stack(new_p[4]), jnp.stack(new_p[5]),
            jnp.stack(new_s[0]), jnp.stack(new_s[1]), jnp.stack(new_s[2]),
            jnp.stack(new_s[3]), jnp.stack(new_s[4]), jnp.stack(new_s[5]))


_drawn_inputs = setup_inputs


def setup_inputs(seed=0):
    import zlib

    import numpy as np

    out = dict(_drawn_inputs(seed))
    spreads = {}
    factors = {'cache_k': 4.179,
     'cache_v': 3.101,
     'cache_logf': 8.0,
     'g_norm2': 8.0,
     'g_qa': 8.0,
     'g_ka': 8.837,
     'g_hb': 24.249}
    for name, (base, spread) in spreads.items():
        noise = np.random.default_rng([zlib.crc32(name.encode()), seed]).standard_normal(out[name].shape)
        drawn = base * np.exp(spread * noise) if base else spread * noise
        out[name] = __import__('jax').numpy.asarray(drawn.astype(out[name].dtype))
    for name, factor in factors.items():
        out[name] = (out[name] * factor).astype(out[name].dtype)
    return out
```

```python
from contextlib import ExitStack

import numpy as np
import concourse.bass as bass
from concourse import mybir
from concourse.alu_op_type import AluOpType as ALU

ACT = mybir.ActivationFunctionType
AX = mybir.AxisListType
F32 = mybir.dt.float32
U32 = mybir.dt.uint32

P = 128
D = 1024
KD = D // P
SEQ = 1024
NB = 8
LS = 16
T = SEQ + NB * LS
NT = T // P
NPT = SEQ // P
NC = 3
TC = T // NC
FIRST = 3
PAST = 512
AH, AD = 8, 64
BH, BD = 4, 128
EPS = 1e-6
NEG = -1e30
PH, PK, PHALF, TOPK = 8, 128, 64, 16
BLK_Q, BLK_K, BLK_QB, BLK_KB, BLK_BO, BLK_GA, BLK_GB = 0, 4, 8, 12, 16, 20, 28
NBLK = 36
MOD_SHIFT1, MOD_SCALE1, MOD_GATE1, MOD_SHIFT2, MOD_SCALE2, MOD_GATE2 = range(0, 6 * KD, KD)
GATE_F, GATE_I, GATE_LF, GATE_W = 0, 32, 64, 96


class Steps:

    def __init__(self, eng, sem, base=0):
        self.eng, self.sem, self.base, self.n = eng, sem, base, 0

    def did(self, ins):
        ins.then_inc(self.sem, 1)
        self.n += 1
        return ins

    def settle(self):
        self.eng.wait_ge(self.sem, self.base + self.n)


class Mem:

    def __init__(self, nc, ctx):
        self.nc, self.ctx, self.signals = nc, ctx, []
        ctx.callback(self.clear)

    def clear(self):
        n = 0
        while n < len(self.signals):
            e = n
            while e + 1 < len(self.signals) and self.signals[e + 1] == self.signals[e] + 1:
                e += 1
            self.nc.gpsimd.sem_clear(range(self.signals[n], self.signals[e] + 1))
            n = e + 1

    def sb(self, name, shape, dt=F32):
        return self.ctx.enter_context(self.nc.sbuf_tensor(name, shape, dt))

    def ps(self, name, shape):
        return self.ctx.enter_context(self.nc.psum_tensor(name, shape, F32))

    def sem(self, name):
        handle = self.ctx.enter_context(self.nc.semaphore(name))
        self.signals.append(handle.num)
        return handle

    def credited(self, name):
        handle = self.sem(name)
        self.nc.gpsimd.sem_inc(handle, 1)
        return handle

    def credited_all(self, name, n):
        return [self.credited(f"{name}{i}") for i in range(n)]

    def sems(self, name, n):
        return [self.sem(f"{name}{i}") for i in range(n)]


def phase_constants(nc, src, name, consts):
    with ExitStack() as ctx:
        m = Mem(nc, ctx)
        loaded = m.sem(name + "_loaded")
        block = ctx.enter_context(nc.Block())

        @block.sync
        def _(sp):
            sp.dma_start(consts[:, :], src).then_inc(loaded, 16)
            sp.wait_ge(loaded, 16)


def phase_modulation(nc, io, modT, A1, A2, ident):
    NG, BPG, RING = 12, 4, 4
    NS = NB + 1
    with ExitStack() as ctx:
        m = Mem(nc, ctx)
        cT = m.sb("cT", [P, KD, NS])
        sig = m.sb("sig", [P, KD, NS])
        silu = m.sb("silu", [P, KD, NS])
        w = m.sb("w_mod_ring", [P, RING, KD, BPG * P])
        b = m.sb("b_mod", [P, NG * BPG])
        g12 = m.sb("g12", [P, 2, KD])
        row = m.sb("mod_rows", [P, 2, BPG * P])
        ps = m.ps("ps_mod", [P, 2, 512])
        ps_t = m.ps("ps_mod_turned", [P, 2, 512])
        small_loaded = m.sem("small_loaded")
        w_loaded = m.sems("w_loaded", RING)
        sig_done = m.sem("sig_done")
        rows_zeroed = m.sem("rows_zeroed")
        silu_ready = m.sem("silu_ready")
        mod_psum = m.credited_all("mod_psum", RING)
        row_ready = m.credited_all("mod_row", 2)
        turned = m.credited_all("mod_turned", 2)
        mod_taken = m.credited_all("mod_taken", 2)
        scaled = m.sem("scaled")
        block = ctx.enter_context(nc.Block())

        @block.sync
        def _(sp):
            sp.dma_start(cT[:, :, :], io["cT"]).then_inc(small_loaded, 16)
            sp.dma_start(b[:, :], io["b_mod"]).then_inc(small_loaded, 16)
            sp.dma_start(g12[:, :, :], io["g12"]).then_inc(small_loaded, 16)
            with sp.Fori(0, NG // RING) as i:
                for j in range(RING):
                    sp.wait_ge(mod_psum[j], i + 1)
                    sp.dma_start(w[:, j, :, :], io["w_mod"][i * RING + j]).then_inc(w_loaded[j], 16)

        @block.gpsimd
        def _(pool):
            pool.memset(row[:, :, :], 0.0).then_inc(rows_zeroed, 1)

        @block.scalar
        def _(act):
            act.wait_ge(small_loaded, 48)
            act.activation(sig[:, :, :], cT[:, :, :], ACT.Sigmoid).then_inc(sig_done, 1)
            act.wait_ge(rows_zeroed, 1)
            with act.Fori(0, NG // RING) as i:
                for j in range(RING):
                    e, n = j % 2, j // 2
                    act.wait_ge(mod_psum[j], i + 2)
                    act.wait_ge(turned[e], i * 2 + (n + 1))
                    act.activation(row[0:NS, e, :], ps[0:NS, e, :], ACT.Copy).then_inc(row_ready[e], 1)

        @block.tensor
        def _(pe):
            pe.wait_ge(silu_ready, 1)
            with pe.Fori(0, NG // RING) as i:
                for j in range(RING):
                    e, n = j % 2, j // 2
                    pe.wait_ge(w_loaded[j], i * 16 + 16)
                    pe.wait_ge(row_ready[e], i * 2 + (n + 1))
                    for k in range(KD):
                        mm = pe.matmul(ps[0:NS, e, :], silu[:, k, :], w[:, j, k, :], start=(k == 0), stop=(k == KD - 1))
                    mm.then_inc(mod_psum[j], 1)
                    pe.wait_ge(row_ready[e], i * 2 + (n + 2))
                    pe.wait_ge(mod_taken[e], i * 2 + (n + 1))
                    for q in range(BPG):
                        mm = pe.transpose(ps_t[:, e, q * P:(q + 1) * P], row[:, e, q * P:(q + 1) * P], ident)
                    mm.then_inc(turned[e], 1)

        @block.vector
        def _(dve):
            dve.wait_ge(sig_done, 1)
            dve.wait_ge(small_loaded, 48)
            dve.tensor_tensor(silu[:, :, :], sig[:, :, :], cT[:, :, :], ALU.mult).then_inc(silu_ready, 1)
            with dve.Fori(0, NG // 2) as i:
                for e in range(2):
                    dve.wait_ge(turned[e], i + 2)
                    first = (i * 2 + e) * BPG
                    dve.tensor_tensor(modT[:, bass.ds(first, BPG), :],
                                      ps_t[:, e, :].rearrange("p (q s) -> p q s", s=P)[:, :, 0:NS],
                                      b[:, bass.ds(first, BPG)].unsqueeze(2).to_broadcast([P, BPG, NS]),
                                      ALU.add).then_inc(mod_taken[e], 1)
            for e in range(2):
                dve.wait_ge(mod_taken[e], NG // 2 + 1)
            for n, (A, blk) in enumerate(((A1, MOD_SCALE1), (A2, MOD_SCALE2))):
                dve.scalar_tensor_tensor(A[:, :, :], modT[:, blk:blk + KD, :], 1.0,
                                         g12[:, n, :].unsqueeze(2).to_broadcast([P, KD, NS]),
                                         ALU.add, ALU.mult).then_inc(scaled, 1)
            dve.wait_ge(scaled, 2)


def phase_norm(nc, io, tag, src, dst, load, ones, A, modT, shift_blk, chunks=NC):
    prompt = min(chunks * TC, SEQ)
    with ExitStack() as ctx:
        m = Mem(nc, ctx)
        sq = m.sb("sq" + tag, [P, 2, KD, TC])
        rs = m.sb("rs" + tag, [P, T])
        ps = m.ps("ps_norm" + tag, [P, NC, 512])
        x_loaded = m.sems("x_loaded" + tag, NC)
        squared = m.sem("squared" + tag)
        summed = m.sem("summed" + tag)
        mean_ready = m.sem("mean_ready" + tag)
        root_ready = m.sem("root_ready" + tag)
        inv_ready = m.sem("inv_ready" + tag)
        normed = m.sem("normed" + tag)
        prompt_done = m.sem("prompt_done" + tag)
        sample_scaled = m.sem("sample_scaled" + tag)
        sample_done = m.sem("sample_done" + tag)
        block = ctx.enter_context(nc.Block())
        cut = [slice(c * TC, (c + 1) * TC) for c in range(chunks)]

        if load:
            @block.sync
            def _(sp):
                for c in range(chunks):
                    sp.dma_start(src[:, :, cut[c]], io["xT"][:, :, cut[c]]).then_inc(x_loaded[c], 16)

        @block.scalar
        def _(act):
            for c in range(chunks):
                if load:
                    act.wait_ge(x_loaded[c], 16)
                if c >= 2:
                    act.wait_ge(summed, c - 1)
                act.activation(sq[:, c % 2, :, :], src[:, :, cut[c]], ACT.Square).then_inc(squared, 1)
            for c in range(chunks):
                act.wait_ge(mean_ready, c + 1)
                act.activation(rs[:, cut[c]], rs[:, cut[c]], ACT.Sqrt).then_inc(root_ready, 1)
            act.wait_ge(normed, chunks)
            for k in range(KD):
                act.activation(dst[:, k, 0:prompt], dst[:, k, 0:prompt], ACT.Identity,
                               bias=modT[:, shift_blk + k, 0:1], scale=A[:, k, 0:1]).then_inc(prompt_done, 1)
            act.wait_ge(prompt_done, KD)

        @block.tensor
        def _(pe):
            for c in range(chunks):
                pe.wait_ge(squared, c + 1)
                for k in range(KD):
                    mm = pe.matmul(ps[:, c, 0:TC], ones, sq[:, c % 2, k, :], start=(k == 0), stop=(k == KD - 1))
                mm.then_inc(summed, 1)

        @block.vector
        def _(dve):
            for c in range(chunks):
                dve.wait_ge(summed, c + 1)
                dve.tensor_scalar(rs[:, cut[c]], ps[:, c, 0:TC], 1.0 / D, EPS, ALU.mult, ALU.add).then_inc(mean_ready, 1)
            for c in range(chunks):
                dve.wait_ge(root_ready, c + 1)
                dve.reciprocal(rs[:, cut[c]], rs[:, cut[c]]).then_inc(inv_ready, 1)
                dve.wait_ge(inv_ready, c + 1)
                if load:
                    dve.wait_ge(x_loaded[c], 16)
                dve.tensor_tensor(dst[:, :, cut[c]], src[:, :, cut[c]],
                                  rs[:, cut[c]].unsqueeze(1).to_broadcast([P, KD, TC]), ALU.mult).then_inc(normed, 1)
            dve.wait_ge(normed, chunks)
            if chunks < NC:
                return
            for k in range(KD):
                own = dst[:, k, SEQ:T].rearrange("p (b l) -> p b l", l=LS)
                dve.tensor_tensor(own, own, A[:, k, 1:NB + 1].unsqueeze(2).to_broadcast([P, NB, LS]),
                                  ALU.mult).then_inc(sample_scaled, 1)
            for k in range(KD):
                own = dst[:, k, SEQ:T].rearrange("p (b l) -> p b l", l=LS)
                dve.wait_ge(sample_scaled, k + 1)
                dve.tensor_tensor(own, own, modT[:, shift_blk + k, 1:NB + 1].unsqueeze(2).to_broadcast([P, NB, LS]),
                                  ALU.add).then_inc(sample_done, 1)
            dve.wait_ge(sample_done, KD)


def phase_project(nc, io, tag, first_blk, hT, qk, value_rows):
    NR = len(value_rows)
    with ExitStack() as ctx:
        m = Mem(nc, ctx)
        w = m.sb("w_ring" + tag, [P, 2, KD, P])
        wr = m.sb("w_rows" + tag, [P, KD, 512])
        bb = m.sb("b_blocks" + tag, [P, NBLK])
        br = m.sb("b_rows" + tag, [P, NR, 512])
        ps = m.ps("ps_blk" + tag, [P, 2, NC, 512])
        ps_row = m.ps("ps_row" + tag, [P, 2, 512])
        b_loaded = m.sem("b_loaded" + tag)
        wr_loaded = m.sem("wr_loaded" + tag)
        w_loaded = m.sems("w_loaded" + tag, 2)
        blk_psum = m.credited_all("blk_psum" + tag, 2)
        blk_taken = m.credited_all("blk_taken" + tag, 2)
        row_psum = m.sem("row_psum" + tag)
        row_taken = m.sem("row_taken" + tag)
        block = ctx.enter_context(nc.Block())

        @block.sync
        def _(sp):
            with sp.Fori(0, 4) as i:
                for j in range(2):
                    sp.wait_ge(blk_psum[j], i + 1)
                    sp.dma_start(w[:, j, :, :], io["w_blk"][i * 2 + (first_blk + j)]).then_inc(w_loaded[j], 16)

        @block.scalar
        def _(act):
            act.dma_start(bb[:, :], io["b_blk"]).then_inc(b_loaded, 16)
            for r, (n, _) in enumerate(value_rows):
                act.dma_start(br[:, r, :], io["b_row"][n:n + 1, :].to_broadcast([P, 512])).then_inc(b_loaded, 16)
            for r, (n, _) in enumerate(value_rows):
                if r:
                    act.wait_ge(row_psum, r * NT)
                act.dma_start(wr[:, :, :], io["w_row"][n]).then_inc(wr_loaded, 16)

        @block.tensor
        def _(pe):
            with pe.Fori(0, 4) as i:
                for j in range(2):
                    pe.wait_ge(w_loaded[j], i * 16 + 16)
                    pe.wait_ge(blk_taken[j], i * NC + 1)
                    for k in range(KD):
                        for c in range(NC):
                            mm = pe.matmul(ps[:, j, c, 0:TC], w[:, j, k, :], hT[:, k, c * TC:(c + 1) * TC],
                                           start=(k == 0), stop=(k == KD - 1))
                    mm.then_inc(blk_psum[j], 1)
            for r in range(NR):
                pe.wait_ge(wr_loaded, 16 * r + 16)
                for t in range(NT):
                    if r * NT + t >= 2:
                        pe.wait_ge(row_taken, r * NT + t - 1)
                    for k in range(KD):
                        mm = pe.matmul(ps_row[:, (r * NT + t) % 2, :], hT[:, k, t * P:(t + 1) * P], wr[:, k, :],
                                       start=(k == 0), stop=(k == KD - 1))
                    mm.then_inc(row_psum, 1)

        @block.vector
        def _(dve):
            dve.wait_ge(b_loaded, 16 + 16 * NR)
            with dve.Fori(0, 4) as i:
                for j in range(2):
                    dve.wait_ge(blk_psum[j], i + 2)
                    for c in range(NC):
                        dve.tensor_scalar(qk[:, bass.ds(i * 2 + j, 1), c * TC:(c + 1) * TC].rearrange("p o t -> p (o t)"),
                                          ps[:, j, c, 0:TC], bb[:, bass.ds(i * 2 + (first_blk + j), 1)], None,
                                          ALU.add).then_inc(blk_taken[j], 1)
            for r, (_, out) in enumerate(value_rows):
                for t in range(NT):
                    dve.wait_ge(row_psum, r * NT + t + 1)
                    a, b = ps_row[:, (r * NT + t) % 2, :], br[:, r, :]
                    if len(out.shape) == 4:
                        dve.tensor_tensor(out[:, t, :, 0:BD], a.rearrange("p (h d) -> p h d", h=BH),
                                          b.rearrange("p (h d) -> p h d", h=BH), ALU.add).then_inc(row_taken, 1)
                    else:
                        dve.tensor_tensor(out[:, t, :], a, b, ALU.add).then_inc(row_taken, 1)
            for j in range(2):
                dve.wait_ge(blk_taken[j], 4 * NC + 1)
            dve.wait_ge(row_taken, NR * NT)


def phase_gates(nc, io, hT, gates, va):
    with ExitStack() as ctx:
        m = Mem(nc, ctx)
        wg = m.sb("w_gates", [P, KD, GATE_W])
        bg = m.sb("b_gates", [GATE_W, 1])
        ps = m.ps("ps_gates", [P, NC, 512])
        loaded = m.sem("wg_loaded")
        gate_psum = m.sem("gate_psum")
        gate_taken = m.sem("gate_taken")
        stored = m.sem("new_v_stored")
        block = ctx.enter_context(nc.Block())

        @block.sync
        def _(sp):
            sp.dma_start(bg[:, :], io["b_gate"]).then_inc(loaded, 16)
            sp.dma_start(wg[:, :, :], io["w_gate"]).then_inc(loaded, 16)
            sp.dma_start(io["new_v"], va[:, :, :]).then_inc(stored, 16)
            sp.wait_ge(stored, 16)

        @block.tensor
        def _(pe):
            pe.wait_ge(loaded, 32)
            for c in range(NC):
                for k in range(KD):
                    mm = pe.matmul(ps[0:GATE_W, c, 0:TC], wg[:, k, :], hT[:, k, c * TC:(c + 1) * TC],
                                   start=(k == 0), stop=(k == KD - 1))
                mm.then_inc(gate_psum, 1)

        @block.vector
        def _(dve):
            dve.wait_ge(loaded, 32)
            for c in range(NC):
                dve.wait_ge(gate_psum, c + 1)
                dve.tensor_scalar(gates[:, c * TC:(c + 1) * TC], ps[0:GATE_W, c, 0:TC], bg[:, :], None,
                                  ALU.add).then_inc(gate_taken, 1)
            dve.wait_ge(gate_taken, NC)


def phase_head_norm(nc, io, qk, gqk, pair_ones):
    with ExitStack() as ctx:
        m = Mem(nc, ctx)
        sq = m.sb("head_sq", [P, 2, T])
        rs = m.sb("head_rs", [P, 2, T])
        ps = m.ps("ps_head", [P, 2, NC, 512])
        gains_loaded = m.sem("gains_loaded")
        squared = m.sems("head_squared", 2)
        summed = m.credited_all("head_summed", 2)
        mean_ready = m.credited_all("head_mean", 2)
        log_ready = m.sems("head_log", 2)
        inv_ready = m.sems("head_inv", 2)
        normed = m.credited_all("head_normed", 2)
        stored = m.sem("new_k_stored")
        block = ctx.enter_context(nc.Block())

        @block.sync
        def _(sp):
            sp.dma_start(gqk[:, :], io["g_qk"]).then_inc(gains_loaded, 16)
            for j in range(2):
                sp.wait_ge(normed[j], 4 + 1)
            sp.dma_start(io["new_kT"], qk[:, 4:8, :]).then_inc(stored, 16)
            sp.wait_ge(stored, 16)

        @block.scalar
        def _(act):
            with act.Fori(0, 4) as i:
                for j in range(2):
                    act.wait_ge(summed[j], i + 1)
                    act.activation(sq[:, j, :], qk[:, bass.ds(i * 2 + j, 1), :].rearrange("p o t -> p (o t)"),
                                   ACT.Square).then_inc(squared[j], 1)
                for j in range(2):
                    act.wait_ge(mean_ready[j], i + 2)
                    act.activation(rs[:, j, :], rs[:, j, :], ACT.Ln).then_inc(log_ready[j], 1)
                for j in range(2):
                    act.wait_ge(log_ready[j], i + 1)
                    act.activation(rs[:, j, :], rs[:, j, :], ACT.Exp, scale=-0.5).then_inc(inv_ready[j], 1)

        @block.tensor
        def _(pe):
            with pe.Fori(0, 4) as i:
                for j in range(2):
                    pe.wait_ge(squared[j], i + 1)
                    pe.wait_ge(mean_ready[j], i + 1)
                    for c in range(NC):
                        mm = pe.matmul(ps[:, j, c, 0:TC], pair_ones, sq[:, j, c * TC:(c + 1) * TC],
                                       start=True, stop=True)
                    mm.then_inc(summed[j], 1)

        @block.vector
        def _(dve):
            dve.wait_ge(gains_loaded, 16)
            with dve.Fori(0, 4) as i:
                for j in range(2):
                    dve.wait_ge(summed[j], i + 2)
                    dve.wait_ge(normed[j], i + 1)
                    dve.tensor_scalar(rs[:, j, :].rearrange("p (c t) -> p c t", c=NC), ps[:, j, :, 0:TC],
                                      1.0 / AD, EPS, ALU.mult, ALU.add).then_inc(mean_ready[j], 1)
                for j in range(2):
                    dve.wait_ge(inv_ready[j], i + 1)
                    own = qk[:, bass.ds(i * 2 + j, 1), :].rearrange("p o t -> p (o t)")
                    dve.scalar_tensor_tensor(own, own, gqk[:, bass.ds(i * 2 + j, 1)], rs[:, j, :],
                                             ALU.mult, ALU.mult).then_inc(normed[j], 1)
            for j in range(2):
                dve.wait_ge(normed[j], 4 + 1)


def phase_forget(nc, io, gates, lf, negF, negFc, negFn):
    with ExitStack() as ctx:
        m = Mem(nc, ctx)
        tmp = m.sb("softplus", [GATE_W, T])
        one = m.sb("one_row", [AH, SEQ])
        clf = m.sb("cache_logf", [AH, NB * PAST])
        cache_loaded = m.sem("cache_loaded")
        abs_ready = m.sem("abs_ready")
        ln_ready = m.sem("ln_ready")
        exp_ready = m.sem("exp_ready")
        lf_ready = m.sem("lf_ready")
        dve_done = m.sem("dve_done")
        stored = m.sem("logf_stored")
        block = ctx.enter_context(nc.Block())

        @block.sync
        def _(sp):
            sp.dma_start(clf[:, :], io["cache_logfT"]).then_inc(cache_loaded, 16)
            sp.wait_ge(lf_ready, 1)
            sp.dma_start(io["new_logfT"], lf[0:AH, :]).then_inc(stored, 16)
            sp.wait_ge(stored, 16)

        @block.scalar
        def _(act):
            act.activation(tmp[:, :], gates[:, :], ACT.Abs).then_inc(abs_ready, 1)
            act.wait_ge(abs_ready, 1)
            act.activation(tmp[:, :], tmp[:, :], ACT.Exp, scale=-1.0).then_inc(exp_ready, 1)
            act.wait_ge(exp_ready, 1)
            act.activation(tmp[:, :], tmp[:, :], ACT.Ln, bias=1.0).then_inc(ln_ready, 1)

        @block.vector
        def _(dve):
            s = Steps(dve, dve_done)
            s.did(dve.memset(one[:, :], 1.0))
            dve.wait_ge(ln_ready, 1)
            dve.scalar_tensor_tensor(lf[:, :], gates[:, :], 0.0, tmp[:, :], ALU.min, ALU.subtract).then_inc(lf_ready, 1)
            dve.wait_ge(lf_ready, 1)
            s.settle()
            s.did(dve.tensor_tensor_scan(negF[:, :], one[:, :], lf[0:AH, 0:SEQ], 0.0, ALU.mult, ALU.subtract))
            dve.wait_ge(cache_loaded, 16)
            for b in range(NB):
                s.did(dve.tensor_tensor_scan(negFc[:, b * PAST:(b + 1) * PAST], one[:, 0:PAST],
                                             clf[:, b * PAST:(b + 1) * PAST], 0.0, ALU.mult, ALU.subtract))
            s.settle()
            for b in range(NB):
                s.did(dve.tensor_tensor_scan(negFn[:, b * LS:(b + 1) * LS], one[:, 0:LS],
                                             lf[0:AH, SEQ + b * LS:SEQ + (b + 1) * LS],
                                             negFc[:, (b + 1) * PAST - 1:(b + 1) * PAST], ALU.mult, ALU.subtract))
            s.settle()


def phase_attend_prompt(nc, io, qk, va, negF, haT, ident, causal, head_rows):
    U = 2 * NPT
    BATCH = [(u % NPT) // 4 + 1 for u in range(U)]
    FIRST = [sum(BATCH[:u]) for u in range(U)]
    NBATCH = sum(BATCH)
    with ExitStack() as ctx:
        m = Mem(nc, ctx)
        qp = m.sb("q_pair", [P, SEQ])
        kp = m.sb("k_pair", [P, SEQ])
        vp = m.sb("v_pair", [P, NPT, P])
        sel = m.sb("sel_pair", [AH, 2, P])
        prob = m.sb("prob", [P, 2, SEQ])
        probT = m.sb("probT", [P, 2, 4 * P])
        nmax = m.sb("nmax", [P, 2])
        rsum = m.sb("rsum", [P, 2])
        rinv = m.sb("rinv", [P, 2])
        ps_s = m.ps("ps_s", [P, 2, 1024])
        ps_t = m.ps("ps_t", [P, 2, 512])
        ps_o = m.ps("ps_o", [P, 2, 512])
        staged_qk = m.sem("staged_qk")
        staged_v = m.sem("staged_v")
        staged_sel = m.sem("staged_sel")
        scores_ready = m.sem("scores_ready")
        nmax_ready = m.sem("nmax_ready")
        exp_done = m.sem("exp_done")
        rinv_ready = m.sem("rinv_ready")
        prob_ready = m.sem("prob_ready")
        turned = m.sem("turned")
        probT_ready = m.sem("probT_ready")
        out_ready = m.credited("out_ready")
        out_taken = m.sem("out_taken")
        block = ctx.enter_context(nc.Block())

        @block.gpsimd
        def _(pool):
            with pool.Fori(0, 4) as p:
                pool.wait_ge(out_ready, p * U + 1)
                pool.tensor_copy(sel[:, :, :], head_rows[0:AH, bass.ds(p * 2, 2), :]).then_inc(staged_sel, 1)

        @block.scalar
        def _(act):
            with act.Fori(0, 4) as p:
                act.wait_ge(out_ready, p * U + 1)
                act.activation(vp[:, :, :], va[:, 0:NPT, bass.ds(p * P, P)], ACT.Copy).then_inc(staged_v, 1)
                for u in range(U):
                    w = (u % NPT + 1) * P
                    act.wait_ge(nmax_ready, p * U + u + 1)
                    if u >= 2:
                        act.wait_ge(out_ready, p * U + u)
                    act.activation(prob[:, u % 2, 0:w], ps_s[:, u % 2, 0:w], ACT.Exp, bias=nmax[:, u % 2:u % 2 + 1],
                                   accum_out=rsum[:, u % 2:u % 2 + 1]).then_inc(exp_done, 1)
                    act.wait_ge(rinv_ready, p * U + u + 1)
                    act.activation(prob[:, u % 2, 0:w], prob[:, u % 2, 0:w], ACT.Copy,
                                   scale=rinv[:, u % 2:u % 2 + 1]).then_inc(prob_ready, 1)

        @block.tensor
        def _(pe):
            with pe.Fori(0, 4) as p:
                def scores(u):
                    hh, t = divmod(u, NPT)
                    if u >= 2:
                        pe.wait_ge(exp_done, p * U + u - 1)
                    rows = slice(hh * AD, (hh + 1) * AD)
                    for lo in range(0, (t + 1) * P, 512):
                        n = min(512, (t + 1) * P - lo)
                        last = lo + n == (t + 1) * P
                        pe.matmul(ps_s[:, u % 2, lo:lo + n], qp[rows, t * P:(t + 1) * P], kp[rows, lo:lo + n],
                                  start=True, stop=False)
                        mm = pe.matmul(ps_s[:, u % 2, lo:lo + n], sel[:, hh, :], negF[:, lo:lo + n],
                                       start=False, stop=not last)
                    mm = pe.matmul(ps_s[:, u % 2, t * P:(t + 1) * P], ident, causal, start=False, stop=True)
                    mm.then_inc(scores_ready, 1)

                pe.wait_ge(staged_qk, p * 2 + 2)
                pe.wait_ge(staged_sel, p + 1)
                pe.wait_ge(staged_v, p + 1)
                scores(0)
                for u in range(U):
                    if u + 1 < U:
                        scores(u + 1)
                    hh, t = divmod(u, NPT)
                    pe.wait_ge(prob_ready, p * U + u + 1)
                    for e in range(BATCH[u]):
                        g = FIRST[u] + e
                        if g >= 2:
                            pe.wait_ge(probT_ready, p * NBATCH + g - 1)
                        for k in range(4 * e, min(4 * e + 4, t + 1)):
                            mm = pe.transpose(ps_t[:, g % 2, (k % 4) * P:(k % 4 + 1) * P],
                                              prob[:, u % 2, k * P:(k + 1) * P], ident)
                        mm.then_inc(turned, 1)
                    if u >= 2:
                        pe.wait_ge(out_taken, p * U + u - 1)
                    for e in range(BATCH[u]):
                        g = FIRST[u] + e
                        pe.wait_ge(probT_ready, p * NBATCH + g + 1)
                        for k in range(4 * e, min(4 * e + 4, t + 1)):
                            mm = pe.matmul(ps_o[hh * AD:(hh + 1) * AD, u % 2, 0:P], vp[:, k, hh * AD:(hh + 1) * AD],
                                           probT[:, g % 2, (k % 4) * P:(k % 4 + 1) * P],
                                           start=(k == 0), stop=(k == t))
                    mm.then_inc(out_ready, 1)

        @block.vector
        def _(dve):
            with dve.Fori(0, 4) as p:
                dve.wait_ge(out_ready, p * U + 1)
                blk = lambda first: qk[:, bass.ds(p + first, 1), 0:SEQ].rearrange("p o t -> p (o t)")
                dve.tensor_scalar(qp[:, :], blk(0), AD ** -0.5, None, ALU.mult).then_inc(staged_qk, 1)
                dve.tensor_copy(kp[:, :], blk(4)).then_inc(staged_qk, 1)

                def row_max(u):
                    dve.wait_ge(scores_ready, p * U + u + 1)
                    dve.tensor_reduce(nmax[:, u % 2:u % 2 + 1], ps_s[:, u % 2, 0:(u % NPT + 1) * P], AX.X, ALU.max,
                                      negate=True).then_inc(nmax_ready, 1)

                row_max(0)
                for u in range(U):
                    hh, t = divmod(u, NPT)
                    dve.wait_ge(exp_done, p * U + u + 1)
                    dve.reciprocal(rinv[:, u % 2:u % 2 + 1], rsum[:, u % 2:u % 2 + 1]).then_inc(rinv_ready, 1)
                    if u + 1 < U:
                        row_max(u + 1)
                    for e in range(BATCH[u]):
                        g = FIRST[u] + e
                        n = min(4, t + 1 - 4 * e) * P
                        dve.wait_ge(turned, p * NBATCH + g + 1)
                        dve.tensor_copy(probT[:, g % 2, 0:n], ps_t[:, g % 2, 0:n]).then_inc(probT_ready, 1)
                    dve.wait_ge(out_ready, p * U + u + 2)
                    rows = slice(hh * AD, (hh + 1) * AD)
                    dve.tensor_copy(haT[rows, bass.ds(p, 1), t * P:(t + 1) * P].rearrange("p o t -> p (o t)"),
                                    ps_o[rows, u % 2, 0:P]).then_inc(out_taken, 1)
            dve.wait_ge(out_taken, 4 * U)


def phase_attend_streams(nc, io, qk, va, negFc, negFn, haT, spare, ident, stream_rows):
    W = PAST + P
    NP = AH // 2
    with ExitStack() as ctx:
        m = Mem(nc, ctx)
        masks = m.sb("stream_masks", [P, NB, P])
        kc = spare[:, 0:2 * NP * PAST].rearrange("p (j n t) -> p j n t", j=2, n=NP)
        vc = m.sb("v_cache", [P, 2, PAST // P, AH * AD])
        qbd = m.sb("q_diag", [P, 4 * (P + 2 * LS)])
        prob = m.sb("prob_s", [P, W])
        probT = m.sb("probT_s", [P, 5, P])
        nmax = m.sb("nmax_s", [P, 1])
        rsum = m.sb("rsum_s", [P, 1])
        rinv = m.sb("rinv_s", [P, 1])
        ps_s = m.ps("ps_ss", [P, 1024])
        ps_t = m.ps("ps_ts", [P, 5 * P])
        ps_o = m.ps("ps_os", [P, 4, 2 * LS])
        zeroed = m.sem("zeroed")
        masks_loaded = m.sem("masks_loaded")
        k_loaded = m.sems("k_loaded", 2)
        v_loaded = m.sems("v_loaded", 2)
        q_placed = m.sem("q_placed")
        scores_ready = m.credited("s_scores_ready")
        nmax_ready = m.sem("s_nmax_ready")
        exp_done = m.credited("s_exp_done")
        rinv_ready = m.sem("s_rinv_ready")
        prob_ready = m.sem("s_prob_ready")
        turned = m.credited("s_turned")
        probT_ready = m.credited("s_probT_ready")
        out_ready = m.credited("s_out_ready")
        out_taken = m.credited("s_out_taken")
        block = ctx.enter_context(nc.Block())

        @block.sync
        def _(sp):
            sp.dma_start(masks[:, :, :], io["stream_masks"]).then_inc(masks_loaded, 16)
            with sp.Fori(0, NB // 2) as i:
                for j in range(2):
                    sp.wait_ge(out_ready, i * 2 + j if j else i * 2 + 1)
                    sp.dma_start(kc[:, j, :, :], io["cache_kT"][i * 2 + j]).then_inc(k_loaded[j], 16)
                    sp.dma_start(vc[:, j, :, :], io["cache_v"][i * 2 + j]).then_inc(v_loaded[j], 16)

        @block.gpsimd
        def _(pool):
            pool.memset(qbd[:, :], 0.0).then_inc(zeroed, 1)

        @block.scalar
        def _(act):
            with act.Fori(0, NB) as b:
                act.wait_ge(nmax_ready, b + 1)
                act.wait_ge(turned, b + 1)
                act.activation(prob[:, :], ps_s[:, 0:W], ACT.Exp, bias=nmax[:, :], accum_out=rsum[:, :]).then_inc(exp_done, 1)

        @block.tensor
        def _(pe):
            pe.wait_ge(masks_loaded, 16)
            with pe.Fori(0, NB // 2) as i:
                for j in range(2):
                    b = i * 2 + j
                    pe.wait_ge(k_loaded[j], i * 16 + 16)
                    pe.wait_ge(q_placed, b * 2 + 2)
                    pe.wait_ge(exp_done, b + 1)
                    for n in range(NP):
                        pe.matmul(ps_s[:, 0:PAST], qbd[:, n * P:(n + 1) * P], kc[:, j, n, :], start=(n == 0), stop=False)
                    pe.matmul(ps_s[:, 0:PAST], stream_rows[0:AH, :], negFc[:, bass.ds(b * PAST, PAST)], start=False, stop=True)
                    for n in range(NP):
                        pe.matmul(ps_s[:, PAST:W], qbd[:, n * P:(n + 1) * P], qk[:, 4 + n, SEQ:T], start=(n == 0), stop=False)
                    pe.matmul(ps_s[:, PAST:W], stream_rows[0:AH, :], negFn[:, :], start=False, stop=False)
                    pe.matmul(ps_s[:, PAST:W], ident, masks[:, bass.ds(b, 1), :].rearrange("p o t -> p (o t)"),
                              start=False, stop=True).then_inc(scores_ready, 1)
                    pe.wait_ge(prob_ready, b + 1)
                    pe.wait_ge(probT_ready, b + 1)
                    for k in range(5):
                        mm = pe.transpose(ps_t[:, k * P:(k + 1) * P], prob[:, k * P:(k + 1) * P], ident)
                    mm.then_inc(turned, 1)
                    pe.wait_ge(v_loaded[j], i * 16 + 16)
                    pe.wait_ge(probT_ready, b + 2)
                    pe.wait_ge(out_taken, b * 2 + 1)
                    for n in range(NP):
                        for k in range(5):
                            v = vc[:, j, k, n * P:(n + 1) * P] if k < 4 else va[:, NT - 1, n * P:(n + 1) * P]
                            mm = pe.matmul(ps_o[:, n, :], v, probT[:, k, n * 2 * LS:(n + 1) * 2 * LS],
                                           start=(k == 0), stop=(k == 4))
                    mm.then_inc(out_ready, 1)

        @block.vector
        def _(dve):
            dve.wait_ge(zeroed, 1)
            with dve.Fori(0, NB) as b:
                dve.wait_ge(scores_ready, b + 1)
                for hh in range(2):
                    rows = slice(hh * AD, (hh + 1) * AD)
                    dve.tensor_scalar(qbd[rows, :].rearrange("p (n c) -> p n c", n=NP)[:, :, hh * LS:(hh + 1) * LS],
                                      qk[rows, 0:NP, bass.ds(b * LS + SEQ, LS)], AD ** -0.5, None,
                                      ALU.mult).then_inc(q_placed, 1)
                dve.wait_ge(scores_ready, b + 2)
                dve.tensor_reduce(nmax[:, :], ps_s[:, 0:W], AX.X, ALU.max, negate=True).then_inc(nmax_ready, 1)
                dve.wait_ge(exp_done, b + 2)
                dve.reciprocal(rinv[:, :], rsum[:, :]).then_inc(rinv_ready, 1)
                dve.wait_ge(rinv_ready, b + 1)
                dve.tensor_scalar(prob[:, :], prob[:, :], rinv[:, :], None, ALU.mult).then_inc(prob_ready, 1)
                dve.wait_ge(turned, b + 2)
                dve.tensor_copy(probT[:, :, :], ps_t[:, :].rearrange("p (k t) -> p k t", k=5)).then_inc(probT_ready, 1)
                dve.wait_ge(out_ready, b + 2)
                for hh in range(2):
                    rows = slice(hh * AD, (hh + 1) * AD)
                    dve.tensor_copy(haT[rows, :, bass.ds(b * LS + SEQ, LS)],
                                    ps_o[rows, :, hh * LS:(hh + 1) * LS]).then_inc(out_taken, 1)
            dve.wait_ge(out_taken, 2 * NB + 1)


def phase_mlstm_rows(nc, io, gates, lf, rows, cols):
    with ExitStack() as ctx:
        m = Mem(nc, ctx)
        scan_rows = m.sb("scan_rows", [BH, 2, T])
        m0s = m.sb("m0_streams", [BH, NB])
        small = lambda name: m.sb(name, [BH, T])
        lf4, u, start, d1, b, M, neg_m, u_end = (small("row_" + n) for n in ("lf", "u", "d0", "d1", "b", "M", "nm", "ue"))
        m0p = m.sb("m0_prompt", [BH, NPT])
        m_out = m.sb("m_out", [BH, NB + 1])
        ident = m.sb("ident4", [BH, BH])
        ps = m.ps("ps_cols", [P, NT, 3, BH])
        loaded = m.sem("rows_loaded")
        done = m.sem("rows_done")
        rows_ready = m.sem("rows_ready")
        turned = m.sem("cols_turned")
        cols_ready = m.sem("cols_ready")
        m_ready = m.sem("m_ready")
        stored = m.sem("m_stored")
        block = ctx.enter_context(nc.Block())
        chunks = lambda a: a[:, 0:SEQ].rearrange("p (c t) -> p c t", t=P)
        streams = lambda a: a[:, SEQ:T].rearrange("p (c t) -> p c t", t=LS)

        @block.sync
        def _(sp):
            sp.dma_start(scan_rows[:, :, :], io["scan_rows"]).then_inc(loaded, 16)
            sp.dma_start(m0s[:, :], io["state_mT"]).then_inc(loaded, 16)
            sp.dma_start(ident[:, :], io["consts"][0:BH, 0:BH]).then_inc(loaded, 16)
            sp.wait_ge(m_ready, 2)
            sp.dma_start(io["new_mT"], m_out[:, :]).then_inc(stored, 16)
            sp.wait_ge(stored, 16)

        @block.vector
        def _(dve):
            s = Steps(dve, done)
            s.did(dve.tensor_copy(lf4[:, :], lf[GATE_LF:GATE_LF + BH, :]))
            s.did(dve.tensor_copy(u[:, :], gates[GATE_I:GATE_I + BH, :]))
            s.did(dve.memset(m0p[:, 0:1], 0.0))
            dve.wait_ge(loaded, 48)
            s.settle()
            s.did(dve.tensor_tensor_scan(b[:, :], scan_rows[:, 0, :], lf4[:, :], 0.0, ALU.mult, ALU.add))
            s.settle()
            s.did(dve.tensor_tensor(u[:, :], u[:, :], b[:, :], ALU.subtract))
            s.did(dve.tensor_copy(start[:, :], scan_rows[:, 1, :]))
            s.settle()
            s.did(dve.tensor_copy(chunks(start)[:, 1:NPT, 0:1], chunks(b)[:, 0:NPT - 1, P - 1:P]))
            s.did(dve.tensor_copy(d1[:, :], u[:, :]))
            s.settle()
            s.did(dve.tensor_tensor(streams(d1)[:, :, 0:1], streams(u)[:, :, 0:1], m0s[:, :].unsqueeze(2), ALU.max))
            s.settle()
            s.did(dve.tensor_tensor_scan(M[:, :], start[:, :], d1[:, :], 0.0, ALU.add, ALU.max))
            s.settle()
            s.did(dve.scalar_tensor_tensor(neg_m[:, :], b[:, :], -1.0, M[:, :], ALU.mult, ALU.subtract))
            s.did(dve.tensor_scalar(rows[:, 0, :], M[:, :], -1.0, None, ALU.mult))
            s.did(dve.tensor_tensor(chunks(u_end), chunks(u), chunks(M)[:, :, P - 1:P].to_broadcast([BH, NPT, P]), ALU.subtract))
            s.did(dve.tensor_tensor(streams(u_end), streams(u), streams(M)[:, :, LS - 1:LS].to_broadcast([BH, NB, LS]), ALU.subtract))
            s.settle()
            s.did(dve.tensor_scalar(m0p[:, 1:NPT].unsqueeze(2), chunks(neg_m)[:, 0:NPT - 1, P - 1:P], -1.0, None, ALU.mult))
            dve.tensor_scalar(m_out[:, 0:1], neg_m[:, SEQ - 1:SEQ], -1.0, None, ALU.mult).then_inc(m_ready, 1)
            dve.tensor_scalar(m_out[:, 1:NB + 1].unsqueeze(2), streams(neg_m)[:, :, LS - 1:LS], -1.0, None, ALU.mult).then_inc(m_ready, 1)
            s.settle()
            s.did(dve.tensor_tensor(chunks(rows[:, 1, :]), m0p[:, :].unsqueeze(2).to_broadcast([BH, NPT, P]), chunks(M), ALU.subtract))
            s.did(dve.tensor_tensor(streams(rows[:, 1, :]), m0s[:, :].unsqueeze(2).to_broadcast([BH, NB, LS]), streams(M), ALU.subtract))
            s.settle()
            dve.wait_ge(m_ready, 2)
            dve.engine_nop().then_inc(rows_ready, 1)
            dve.wait_ge(cols_ready, 2)
            dve.tensor_copy(cols[:, 0, :, :], ps[:, :, 0, :]).then_inc(cols_ready, 1)
            dve.wait_ge(cols_ready, 3)

        @block.tensor
        def _(pe):
            pe.wait_ge(rows_ready, 1)
            for t in range(NT):
                for n, a in enumerate((u, u_end, neg_m)):
                    mm = pe.transpose(ps[:, t, n, :], a[:, t * P:(t + 1) * P], ident[:, :])
            mm.then_inc(turned, 1)

        @block.scalar
        def _(act):
            act.wait_ge(turned, 1)
            for n in (1, 2):
                act.activation(cols[:, n, :, :], ps[:, :, n, :], ACT.Exp).then_inc(cols_ready, 1)


def phase_ones(nc, vb):
    with ExitStack() as ctx:
        done = Mem(nc, ctx).sem("ones_set")
        block = ctx.enter_context(nc.Block())

        @block.vector
        def _(dve):
            dve.memset(vb[:, :, :, BD:BD + 1], 1.0).then_inc(done, 1)
            dve.wait_ge(done, 1)


def phase_mlstm(nc, io, qk, kb, vb, rows, cols, hbT, ident, causalT, head_rows):
    V1 = BD + 1
    KS = BD ** -0.5
    B3 = lambda b: (b // 3, (b % 3) * V1)
    with ExitStack() as ctx:
        m = Mem(nc, ctx)
        kT = m.sb("kT_head", [P, T])
        sel = m.sb("sel_head", [BH, P])
        smT = m.sb("stream_maskT", [P, P])
        own = m.sb("own_stream", [P, NB, P])
        own_rows = m.sb("own_rows", [P, NB])
        ghb = m.sb("g_hb", [P, BH])
        C = m.sb("state", [P, V1])
        Cs = m.sb("state_streams", [P, NB, V1])
        wT = m.sb("wT", [P, 2, P])
        aT = m.sb("aT", [P, 2, P])
        wsT = m.sb("wsT", [P, 2, P])
        qa = m.sb("qa", [P, 2, P])
        kw = m.sb("kw", [P, 2, P])
        qm = m.sb("q_streams", [P, NB, P])
        kwm = m.sb("kw_streams", [P, NB, P])
        hb = m.sb("h_rows", [P, NT, V1])
        sq = kT[:, :].rearrange("p (t d) -> p t d", d=BD)
        den = m.sb("den", [P, NT])
        inv = m.sb("inv", [P, NT])
        ps_a = m.ps("ps_a", [P, 2, 512])
        ps_n = m.ps("ps_n", [P, 2, 512])
        ps_u = m.ps("ps_u", [P, 3, 512])
        ps_h = m.ps("ps_h", [P, 512])
        consts_loaded = m.sem("m_consts_loaded")
        cs_loaded = m.sem("cs_loaded")
        staged = m.sem("m_staged")
        a_ready = m.credited("a_ready")
        w_ready = m.sem("w_ready")
        at_ready = m.sem("at_ready")
        ws_ready = m.sem("ws_ready")
        qa_ready = m.sem("qa_ready")
        kw_ready = m.sem("kw_ready")
        num_ready = m.sem("num_ready")
        num_taken = m.sem("num_taken")
        upd_ready = m.sem("upd_ready")
        state_ready = m.sem("state_ready")
        cs_ready = m.sem("cs_ready")
        dve_done = m.sem("m_dve_done")
        h_scaled = m.sem("h_scaled")
        h_squared = m.sem("h_squared")
        h_summed = m.sem("h_summed")
        mean_ready = m.sem("h_mean")
        log_ready = m.sem("h_log")
        inv_ready = m.sem("h_inv")
        h_normed = m.sem("h_normed")
        h_turned = m.sem("h_turned")
        hb_ready = m.sem("hb_ready")
        stored = m.credited("state_stored")
        block = ctx.enter_context(nc.Block())
        head = lambda a, h: a[:, bass.ds(h, 1), :].rearrange("p o t -> p (o t)")
        q_of = lambda h, tok: head(qk[:, :, tok], h)
        DONE = 5

        @block.sync
        def _(sp):
            sp.dma_start(smT[:, :], io["stream_maskT"]).then_inc(consts_loaded, 16)
            sp.dma_start(own[:, :, :], io["own_stream"]).then_inc(consts_loaded, 16)
            sp.dma_start(own_rows[:, :], io["own_rows"]).then_inc(consts_loaded, 16)
            sp.dma_start(ghb[:, :], io["g_hbT"]).then_inc(consts_loaded, 16)
            with sp.Fori(0, BH) as h:
                sp.wait_ge(stored, h * 32 + 1)
                sp.dma_start(Cs[:, :, :], io["state_C"][h]).then_inc(cs_loaded, 16)
                sp.wait_ge(state_ready, h * NPT + NPT)
                sp.dma_start(io["new_C_prompt"][h], C[:, :]).then_inc(stored, 16)
                sp.wait_ge(cs_ready, h * NB + NB)
                sp.dma_start(io["new_C_sample"][h], Cs[:, :, :]).then_inc(stored, 16)
            sp.wait_ge(stored, BH * 32 + 1)

        @block.gpsimd
        def _(pool):
            with pool.Fori(0, BH) as h:
                pool.wait_ge(a_ready, h * NT + 1)
                pool.tensor_copy(sel[:, :], head(head_rows[0:BH], h)).then_inc(staged, 1)

        @block.scalar
        def _(act):
            with act.Fori(0, BH) as h:
                for t in range(NT):
                    act.wait_ge(a_ready, h * NT + t + 2)
                    if t >= 2:
                        act.wait_ge(ws_ready, h * NT + t - 1)
                    act.activation(wT[:, t % 2, :], ps_a[:, t % 2, 0:P], ACT.Exp,
                                   bias=cols[:, 0, t, bass.ds(h, 1)]).then_inc(w_ready, 1)
                    if t >= 2:
                        act.wait_ge(state_ready, h * NPT + t - 1)
                    act.activation(aT[:, t % 2, :], ps_a[:, t % 2, P:2 * P], ACT.Exp).then_inc(at_ready, 1)
                    if t >= 1:
                        act.wait_ge(num_ready, h * NT + t)
                        act.activation(hb[:, t - 1, :], ps_n[:, (t - 1) % 2, 0:V1], ACT.Copy).then_inc(num_taken, 1)
                act.wait_ge(num_ready, h * NT + NT)
                act.activation(hb[:, NT - 1, :], ps_n[:, (NT - 1) % 2, 0:V1], ACT.Copy).then_inc(num_taken, 1)
                act.wait_ge(h_scaled, h + 1)
                act.activation(sq, hb[:, :, 0:BD], ACT.Square).then_inc(h_squared, 1)
                act.wait_ge(mean_ready, h + 1)
                act.activation(inv[:, :], inv[:, :], ACT.Ln).then_inc(log_ready, 1)
                act.wait_ge(log_ready, h + 1)
                act.activation(inv[:, :], inv[:, :], ACT.Exp, scale=-0.5).then_inc(inv_ready, 1)

        @block.tensor
        def _(pe):
            pe.wait_ge(consts_loaded, 64)
            with pe.Fori(0, BH) as h:
                def scores(t):
                    tok = slice(t * P, (t + 1) * P)
                    if t >= 2:
                        pe.wait_ge(at_ready, h * NT + t - 1)
                        pe.wait_ge(ws_ready, h * NT + t - 1)
                    pe.matmul(ps_a[:, t % 2, 0:P], sel[:, :], rows[:, 0, tok], start=True, stop=False)
                    pe.matmul(ps_a[:, t % 2, 0:P], ident, causalT if t < NPT else smT[:, :], start=False, stop=True)
                    pe.matmul(ps_a[:, t % 2, P:2 * P], sel[:, :], rows[:, 1, tok], start=True, stop=True)
                    pe.matmul(ps_a[:, t % 2, 2 * P:3 * P], kT[:, tok], q_of(h, tok), start=True, stop=True).then_inc(a_ready, 1)

                pe.wait_ge(staged, h * 3 + 3)
                scores(0)
                for t in range(NT):
                    if t + 1 < NT:
                        scores(t + 1)
                    v = head(vb[:, t], h)
                    pe.wait_ge(kw_ready, h * NT + t + 1)
                    if t < NPT:
                        if t >= 2:
                            pe.wait_ge(state_ready, h * NPT + t - 1)
                        pe.matmul(ps_u[:, t % 2, 0:V1], kw[:, t % 2, :], v, start=True, stop=True).then_inc(upd_ready, 1)
                    else:
                        pe.wait_ge(state_ready, h * NPT + NPT)
                        for b in range(NB):
                            bank, at = B3(b)
                            mm = pe.matmul(ps_u[:, bank, at:at + V1], kwm[:, b, :], v, start=True, stop=True)
                        mm.then_inc(upd_ready, 1)
                    pe.wait_ge(ws_ready, h * NT + t + 1)
                    pe.wait_ge(qa_ready, h * NT + t + 1)
                    if t >= 2:
                        pe.wait_ge(num_taken, h * NT + t - 1)
                    pe.matmul(ps_n[:, t % 2, 0:V1], wsT[:, t % 2, :], v, start=True, stop=False)
                    if t < NPT:
                        if t >= 1:
                            pe.wait_ge(state_ready, h * NPT + t)
                        mm = pe.matmul(ps_n[:, t % 2, 0:V1], qa[:, t % 2, :], C[:, :], start=False, stop=True)
                    else:
                        pe.wait_ge(cs_loaded, h * 16 + 16)
                        for b in range(NB):
                            mm = pe.matmul(ps_n[:, t % 2, 0:V1], qm[:, b, :], Cs[:, b, :], start=False, stop=(b == NB - 1))
                    mm.then_inc(num_ready, 1)
                pe.wait_ge(h_normed, h + 1)
                for e, (lo, hi) in enumerate(((0, 4), (4, 8), (8, 9))):
                    if e:
                        pe.wait_ge(hb_ready, h * 3 + e)
                    for t in range(lo, hi):
                        mm = pe.transpose(ps_h[:, (t - lo) * P:(t - lo + 1) * P], hb[:, t, 0:BD], ident)
                    mm.then_inc(h_turned, 1)

        @block.vector
        def _(dve):
            dve.wait_ge(consts_loaded, 64)
            with dve.Fori(0, BH) as h:
                s = Steps(dve, dve_done, h * DONE)
                dve.wait_ge(a_ready, h * NT + 1)
                dve.tensor_scalar(kT[:, :], head(qk, h + BH), KS, None, ALU.mult).then_inc(staged, 1)
                dve.wait_ge(stored, h * 32 + 1)
                dve.memset(C[:, :], 0.0).then_inc(staged, 1)
                for t in range(NT):
                    if t >= 2:
                        dve.wait_ge(upd_ready, h * NT + t - 1)
                        dve.wait_ge(num_ready, h * NT + t - 1)
                    dve.tensor_scalar(kw[:, t % 2, :], kb[:, t, bass.ds(h * BD, BD)], cols[:, 1, t, bass.ds(h, 1)], KS,
                                      ALU.mult, ALU.mult).then_inc(kw_ready if t < NPT else dve_done, 1)
                    if t == NT - 1:
                        s.n += 1
                        s.settle()
                        dve.tensor_tensor(kwm[:, :, :], kw[:, t % 2, :].unsqueeze(1).to_broadcast([P, NB, P]),
                                          own_rows[:, :].unsqueeze(2).to_broadcast([P, NB, P]), ALU.mult).then_inc(kw_ready, 1)
                    dve.wait_ge(w_ready, h * NT + t + 1)
                    dve.wait_ge(at_ready, h * NT + t + 1)
                    dve.tensor_tensor(wsT[:, t % 2, :], wT[:, t % 2, :], ps_a[:, t % 2, 2 * P:3 * P], ALU.mult).then_inc(ws_ready, 1)
                    dve.tensor_tensor(qa[:, t % 2, :], q_of(h, slice(t * P, (t + 1) * P)), aT[:, t % 2, :],
                                      ALU.mult).then_inc(qa_ready if t < NPT else dve_done, 1)
                    if t == NT - 1:
                        s.n += 1
                        s.settle()
                        dve.tensor_tensor(qm[:, :, :], qa[:, t % 2, :].unsqueeze(1).to_broadcast([P, NB, P]), own[:, :, :],
                                          ALU.mult).then_inc(qa_ready, 1)
                    dve.wait_ge(upd_ready, h * NT + t + 1)
                    dve.wait_ge(num_ready, h * NT + t + 1)
                    if t < NPT:
                        dve.scalar_tensor_tensor(C[:, :], C[:, :], aT[:, t % 2, P - 1:P], ps_u[:, t % 2, 0:V1],
                                                 ALU.mult, ALU.add).then_inc(state_ready, 1)
                        dve.wait_ge(state_ready, h * NPT + t + 1)
                    else:
                        for b in range(NB):
                            bank, at = B3(b)
                            dve.scalar_tensor_tensor(Cs[:, b, :], Cs[:, b, :], aT[:, t % 2, (b + 1) * LS - 1:(b + 1) * LS],
                                                     ps_u[:, bank, at:at + V1], ALU.mult, ALU.add).then_inc(cs_ready, 1)
                dve.wait_ge(num_taken, h * NT + NT)
                s.did(dve.scalar_tensor_tensor(den[:, :], hb[:, :, BD:V1].rearrange("p t o -> p (t o)"), -1.0,
                                               hb[:, :, BD:V1].rearrange("p t o -> p (t o)"), ALU.mult, ALU.max))
                s.settle()
                s.did(dve.tensor_tensor(den[:, :], den[:, :], cols[:, 2, :, bass.ds(h, 1)].rearrange("p t o -> p (t o)"), ALU.max))
                s.settle()
                s.did(dve.reciprocal(den[:, :], den[:, :]))
                s.settle()
                assert s.n == DONE
                dve.tensor_tensor(hb[:, :, 0:BD], hb[:, :, 0:BD], den[:, :].unsqueeze(2).to_broadcast([P, NT, BD]),
                                  ALU.mult).then_inc(h_scaled, 1)
                dve.wait_ge(h_squared, h + 1)
                dve.tensor_reduce(den[:, :], sq, AX.X, ALU.add).then_inc(h_summed, 1)
                dve.wait_ge(h_summed, h + 1)
                dve.tensor_scalar(inv[:, :], den[:, :], 1.0 / BD, EPS, ALU.mult, ALU.add).then_inc(mean_ready, 1)
                dve.wait_ge(inv_ready, h + 1)
                dve.tensor_tensor(hb[:, :, 0:BD], hb[:, :, 0:BD], inv[:, :].unsqueeze(2).to_broadcast([P, NT, BD]),
                                  ALU.mult).then_inc(h_normed, 1)
                for e, (lo, hi) in enumerate(((0, 4), (4, 8), (8, 9))):
                    dve.wait_ge(h_turned, h * 3 + e + 1)
                    dve.tensor_scalar(head(hbT[:, :, lo * P:hi * P], h), ps_h[:, 0:(hi - lo) * P],
                                      ghb[:, bass.ds(h, 1)], None, ALU.mult).then_inc(hb_ready, 1)
            dve.wait_ge(hb_ready, BH * 3)
            dve.wait_ge(cs_ready, BH * NB)


def phase_merge(nc, io, hT, haT, hbT, mT):
    with ExitStack() as ctx:
        m = Mem(nc, ctx)
        w = m.sb("w_gate_ring", [P, 2, KD, P])
        wp = m.sb("w_branch_ring", [P, 2, 4, P])
        bb = m.sb("b_blocks2", [P, NBLK])
        sg = m.sb("sig_ring", [P, 2, T])
        pr = m.sb("gated", [P, TC])
        ps_g = m.ps("ps_gate", [P, 2, NC, 512])
        ps_p = m.ps("ps_branch", [P, 2, 512])
        b_loaded = m.sem("b2_loaded")
        w_loaded = m.sems("wg_loaded", 2)
        wp_loaded = m.sems("wp_loaded", 2)
        gate_psum = m.credited_all("gate_psum2", 2)
        sig_ready = m.credited_all("sig_ready", 2)
        branch_psum = m.credited_all("branch_psum", 2)
        used = m.credited_all("gates_used", 2)
        merged = m.credited("merged")
        block = ctx.enter_context(nc.Block())
        BO = 2

        @block.sync
        def _(sp):
            sp.dma_start(bb[:, :], io["b_blk"]).then_inc(b_loaded, 16)
            with sp.Fori(0, BO) as i:
                for j in range(2):
                    sp.wait_ge(gate_psum[j], i + 1)
                    sp.dma_start(w[:, j, :, :], io["w_blk"][i * 2 + (BLK_BO + j)]).then_inc(w_loaded[j], 16)
            with sp.Fori(0, KD) as i:
                for j, (blk, wname) in enumerate(((BLK_GA, "w_paT"), (BLK_GB, "w_pbT"))):
                    sp.wait_ge(gate_psum[j], i + (BO + 1))
                    sp.dma_start(w[:, j, :, :], io["w_blk"][i + blk]).then_inc(w_loaded[j], 16)
                    sp.wait_ge(branch_psum[j], i + 1)
                    sp.dma_start(wp[:, j, :, :], io[wname][i]).then_inc(wp_loaded[j], 16)

        @block.tensor
        def _(pe):
            def gate(j, chunks):
                for k in range(KD):
                    for c in range(chunks):
                        mm = pe.matmul(ps_g[:, j, c, 0:TC], w[:, j, k, :], hT[:, k, c * TC:(c + 1) * TC],
                                       start=(k == 0), stop=(k == KD - 1))
                mm.then_inc(gate_psum[j], 1)

            with pe.Fori(0, BO) as i:
                for j in range(2):
                    pe.wait_ge(w_loaded[j], i * 16 + 16)
                    pe.wait_ge(sig_ready[j], i * NC + 1)
                    gate(j, NC)
            for j in range(2):
                pe.wait_ge(used[j], BO + 1)
            with pe.Fori(0, KD) as i:
                for j, src in enumerate((haT, hbT)):
                    pe.wait_ge(w_loaded[j], i * 16 + 16 * (BO + 1))
                    pe.wait_ge(sig_ready[j], i + (BO * NC + 1))
                    gate(j, 1)
                    pe.wait_ge(wp_loaded[j], i * 16 + 16)
                    pe.wait_ge(used[j], i + (BO + 1))
                    for k in range(4):
                        mm = pe.matmul(ps_p[:, j, 0:TC], wp[:, j, k, :], src[:, k, 0:TC], start=(k == 0), stop=(k == 3))
                    mm.then_inc(branch_psum[j], 1)

        @block.scalar
        def _(act):
            act.wait_ge(b_loaded, 16)
            with act.Fori(0, BO) as i:
                for j in range(2):
                    act.wait_ge(gate_psum[j], i + 2)
                    act.wait_ge(used[j], i + 1)
                    for c in range(NC):
                        act.activation(sg[:, j, c * TC:(c + 1) * TC], ps_g[:, j, c, 0:TC], ACT.Sigmoid,
                                       bias=bb[:, bass.ds(i * 2 + (BLK_BO + j), 1)]).then_inc(sig_ready[j], 1)
            with act.Fori(0, KD) as i:
                for j, blk in enumerate((BLK_GA, BLK_GB)):
                    act.wait_ge(gate_psum[j], i + (BO + 2))
                    act.wait_ge(used[j], i + (BO + 1))
                    act.activation(sg[:, j, 0:TC], ps_g[:, j, 0, 0:TC], ACT.Sigmoid,
                                   bias=bb[:, bass.ds(i + blk, 1)]).then_inc(sig_ready[j], 1)

        @block.vector
        def _(dve):
            with dve.Fori(0, BO) as i:
                for j in range(2):
                    dve.wait_ge(sig_ready[j], i * NC + (NC + 1))
                    own = hbT[:, bass.ds(i * 2 + j, 1), :].rearrange("p o t -> p (o t)")
                    dve.tensor_tensor(own, own, sg[:, j, :], ALU.mult).then_inc(used[j], 1)
            with dve.Fori(0, KD) as i:
                out = mT[:, bass.ds(i, 1), :].rearrange("p o t -> p (o t)")
                for j, dst in enumerate((pr[:, :], out)):
                    dve.wait_ge(sig_ready[j], i + (BO * NC + 2))
                    dve.wait_ge(branch_psum[j], i + 2)
                    if j == 0:
                        dve.wait_ge(merged, i + 1)
                    dve.tensor_tensor(dst, ps_p[:, j, 0:TC], sg[:, j, 0:TC], ALU.mult).then_inc(used[j], 1)
                for j in range(2):
                    dve.wait_ge(used[j], i + (BO + 2))
                dve.tensor_tensor(out, out, pr[:, :], ALU.add).then_inc(merged, 1)
            dve.wait_ge(merged, KD + 1)


def phase_out(nc, io, mT, modT, x1T):
    with ExitStack() as ctx:
        m = Mem(nc, ctx)
        w = m.sb("w_o_ring", [P, 2, KD, P])
        ps = m.ps("ps_o_proj", [P, 2, 512])
        x_loaded = m.sem("x_again_loaded")
        w_loaded = m.sems("wo_loaded", 2)
        psum_ready = m.credited_all("o_psum", 2)
        taken = m.credited_all("o_taken", 2)
        block = ctx.enter_context(nc.Block())

        @block.scalar
        def _(act):
            act.dma_start(x1T[:, :, 0:TC], io["xT"][:, :, 0:TC]).then_inc(x_loaded, 16)

        @block.sync
        def _(sp):
            with sp.Fori(0, KD // 2) as i:
                for j in range(2):
                    sp.wait_ge(psum_ready[j], i + 1)
                    sp.dma_start(w[:, j, :, :], io["w_oT"][i * 2 + j]).then_inc(w_loaded[j], 16)

        @block.tensor
        def _(pe):
            with pe.Fori(0, KD // 2) as i:
                for j in range(2):
                    pe.wait_ge(w_loaded[j], i * 16 + 16)
                    pe.wait_ge(taken[j], i + 1)
                    for k in range(KD):
                        mm = pe.matmul(ps[:, j, 0:TC], w[:, j, k, :], mT[:, k, :], start=(k == 0), stop=(k == KD - 1))
                    mm.then_inc(psum_ready[j], 1)

        @block.vector
        def _(dve):
            dve.wait_ge(x_loaded, 16)
            with dve.Fori(0, KD // 2) as i:
                for j in range(2):
                    dve.wait_ge(psum_ready[j], i + 2)
                    own = x1T[:, bass.ds(i * 2 + j, 1), 0:TC].rearrange("p o t -> p (o t)")
                    dve.scalar_tensor_tensor(own, ps[:, j, 0:TC],
                                             modT[:, bass.ds(i * 2 + (MOD_GATE1 + j), 1), 0:1].rearrange("p o t -> p (o t)"), own,
                                             ALU.mult, ALU.add).then_inc(taken[j], 1)
            for j in range(2):
                dve.wait_ge(taken[j], KD // 2 + 1)


def phase_turn(nc, x1T, h2T, modT, ident, x1_rows, h2_rows, g2_rows):
    with ExitStack() as ctx:
        m = Mem(nc, ctx)
        gate = m.sb("gate_tiles", [P, 2, KD, P])
        row = m.sb("row_ring", [P, 4, D])
        ps = m.ps("ps_turn", [P, 4, D])
        gate_ready = m.sem("gate_ready")
        turned = m.sem("tile_turned")
        row_ready = m.sem("row_ready")
        stored = m.sems("row_stored", 4)
        block = ctx.enter_context(nc.Block())
        units = [(x1T[:, :, t * P:(t + 1) * P], [x1_rows[t]]) for t in range(FIRST)]
        units += [(h2T[:, :, t * P:(t + 1) * P], [h2_rows[t]] + [h2_rows[NT]] * (t == 0)) for t in range(FIRST)]
        units += [(gate[:, 0], [g2_rows[t] for t in range(NPT)]), (gate[:, 1], [g2_rows[NPT]])]
        stores = [0] * 4
        until = []
        for n, (_, to) in enumerate(units):
            stores[n % 4] += len(to)
            until.append(stores[n % 4])

        @block.gpsimd
        def _(pool):
            pool.tensor_copy(gate[:, 0], modT[:, MOD_GATE2:MOD_GATE2 + KD, 0:1].to_broadcast([P, KD, P])).then_inc(gate_ready, 1)
            for b in range(NB):
                pool.tensor_copy(gate[:, 1, :, b * LS:(b + 1) * LS],
                                 modT[:, MOD_GATE2:MOD_GATE2 + KD, 1 + b:2 + b].to_broadcast([P, KD, LS])).then_inc(gate_ready, 1)

        @block.tensor
        def _(pe):
            for n, (src, _) in enumerate(units):
                if n == 2 * FIRST:
                    pe.wait_ge(gate_ready, 1 + NB)
                if n >= 4:
                    pe.wait_ge(row_ready, n - 3)
                for k in range(KD):
                    mm = pe.transpose(ps[:, n % 4, k * P:(k + 1) * P], src[:, k, :], ident)
                mm.then_inc(turned, 1)

        def take(eng, n, copy):
            eng.wait_ge(turned, n + 1)
            if n >= 1:
                eng.wait_ge(row_ready, n)
            if n >= 4:
                eng.wait_ge(stored[n % 4], 16 * until[n - 4])
            copy(n).then_inc(row_ready, 1)

        @block.vector
        def _(dve):
            for n in range(0, len(units), 2):
                take(dve, n, lambda n: dve.tensor_copy(row[:, n % 4, :], ps[:, n % 4, :]))

        @block.scalar
        def _(act):
            for n in range(1, len(units), 2):
                take(act, n, lambda n: act.activation(row[:, n % 4, :], ps[:, n % 4, :], ACT.Copy))

        @block.sync
        def _(sp):
            for n, (_, to) in enumerate(units):
                sp.wait_ge(row_ready, n + 1)
                for dst in to:
                    sp.dma_start(dst, row[:, n % 4, :]).then_inc(stored[n % 4], 16)
            for j in range(4):
                sp.wait_ge(stored[j], 16 * stores[j])


def phase_retrieval_scores(nc, io, h2T, score_rows):
    with ExitStack() as ctx:
        m = Mem(nc, ctx)
        w = m.sb("w_pq_ring", [P, 2, KD, P])
        keys = m.sb("sub_keys", [P, PH, PK])
        key = m.sb("head_keys", [P, 2, PK])
        q = m.sb("head_query", [P, 2, TC])
        row = m.sb("score_ring", [P, 2, FIRST, 2 * PK])
        ps_q = m.ps("ps_query", [P, 2, 512])
        ps_s = m.ps("ps_scores", [P, 2, 2, 512])
        keys_loaded = m.sem("keys_loaded")
        w_loaded = m.sems("wpq_loaded", 2)
        key_ready = m.sems("key_ready", 2)
        q_psum = m.credited_all("q_psum", 2)
        q_ready = m.credited_all("q_ready", 2)
        s_psum = m.credited_all("s_psum", 2)
        s_taken = m.credited_all("s_taken", 2)
        stored = m.credited_all("scores_stored", 2)
        block = ctx.enter_context(nc.Block())

        @block.sync
        def _(sp):
            sp.dma_start(keys[:, :, :], io["sub_keysT"]).then_inc(keys_loaded, 16)
            with sp.Fori(0, PH // 2) as i:
                for j in range(2):
                    sp.wait_ge(q_psum[j], i + 1)
                    sp.dma_start(w[:, j, :, :], io["w_pqT"][i * 2 + j]).then_inc(w_loaded[j], 16)

        @block.gpsimd
        def _(pool):
            pool.wait_ge(keys_loaded, 16)
            with pool.Fori(0, PH // 2) as i:
                for j in range(2):
                    pool.wait_ge(s_psum[j], i + 1)
                    pool.tensor_copy(key[:, j, :], keys[:, bass.ds(i * 2 + j, 1), :].rearrange("p o t -> p (o t)")
                                     ).then_inc(key_ready[j], 1)

        @block.tensor
        def _(pe):
            with pe.Fori(0, PH // 2) as i:
                for j in range(2):
                    pe.wait_ge(w_loaded[j], i * 16 + 16)
                    pe.wait_ge(q_ready[j], i + 1)
                    for k in range(KD):
                        mm = pe.matmul(ps_q[:, j, 0:TC], w[:, j, k, :], h2T[:, k, 0:TC], start=(k == 0), stop=(k == KD - 1))
                    mm.then_inc(q_psum[j], 1)
                for j in range(2):
                    pe.wait_ge(q_ready[j], i + 2)
                    pe.wait_ge(key_ready[j], i + 1)
                    pe.wait_ge(s_taken[j], i + 1)
                    for half in range(2):
                        rows = slice(half * PHALF, (half + 1) * PHALF)
                        for t in range(FIRST):
                            mm = pe.matmul(ps_s[:, j, half, t * PK:(t + 1) * PK],
                                           q[rows, j, t * P:(t + 1) * P], key[rows, j, :], start=True, stop=True)
                    mm.then_inc(s_psum[j], 1)

        @block.scalar
        def _(act):
            with act.Fori(0, PH // 2) as i:
                for j in range(2):
                    act.wait_ge(q_psum[j], i + 2)
                    act.wait_ge(s_psum[j], i + 1)
                    act.activation(q[:, j, :], ps_q[:, j, 0:TC], ACT.Copy).then_inc(q_ready[j], 1)
                for j in range(2):
                    act.wait_ge(s_taken[j], i + 2)
                    act.dma_start(score_rows[0:FIRST, bass.ds(i * 2 + j, 1), :, :].rearrange("t o p k -> p t (o k)"),
                                  row[:, j, :, :]).then_inc(stored[j], 16)
            for j in range(2):
                act.wait_ge(stored[j], 16 * PH // 2 + 1)
            act.dma_start(score_rows[NT, 0], row[:, 0, 0, :]).then_inc(stored[0], 16)
            act.wait_ge(stored[0], 16 * PH // 2 + 16 + 1)

        @block.vector
        def _(dve):
            with dve.Fori(0, PH // 2) as i:
                for j in range(2):
                    dve.wait_ge(stored[j], i * 16 + 1)
                    dve.wait_ge(s_psum[j], i + 2)
                    dve.tensor_copy(row[:, j, :, :].rearrange("p t (s k) -> p t s k", s=2),
                                    ps_s[:, j, :, 0:FIRST * PK].rearrange("p s (t k) -> p t s k", k=PK)).then_inc(s_taken[j], 1)
            for j in range(2):
                dve.wait_ge(s_taken[j], PH // 2 + 1)


class Rest:

    def __init__(self, nc, io, m, hT, branchT, modT, A2, ident, ones, x1_rows, h2_rows, score_rows):
        self.io, self.hT, self.branchT, self.modT, self.A2, self.ident, self.ones = io, hT, branchT, modT, A2, ident, ones
        self.x1_rows, self.h2_rows, self.score_rows = x1_rows, h2_rows, score_rows
        self.bb = m.sb("b_blocks3", [P, NBLK])
        side = m.sb("rest_scratch", [P, 3328])
        two = lambda a: a.rearrange("p (j t) -> p j t", j=2)
        self.w = side[:, 0:1024].rearrange("p (k c) -> p k c", k=KD)
        self.wp = side[:, 1024:1536].rearrange("p (k c) -> p k c", k=4)
        self.sg = self.xb = self.sq = two(side[:, 1536:3072])
        self.rs = side[:, 0:768]
        self.tmp = two(side[:, 1024:1280])
        self.row = two(side[:, 1024:3072])
        self.q, self.scores, self.key = side[:, 1024:1792], side[:, 1792:2560], two(side[:, 3072:3328])
        self.ps = m.ps("ps_rest", [P, 8, 512])
        self.loaded = m.sem("rest_bias_loaded")
        self.w_loaded, self.wp_loaded = m.sem("r_wg_loaded"), m.sem("r_wp_loaded")
        self.gate_psum, self.branch_psum = m.credited_all("r_gate_psum", 2), m.credited_all("r_branch_psum", 2)
        self.sig_ready, self.used = m.credited_all("r_sig_ready", 2), m.credited_all("r_used", 2)
        self.merged = m.credited("r_merged")
        self.wo_loaded, self.x_loaded = m.sem("r_wo_loaded"), m.sems("r_x_loaded", 2)
        self.o_psum, self.o_taken = m.credited_all("r_o_psum", 2), m.credited_all("r_o_taken", 2)
        self.o_scaled = m.sems("r_o_scaled", 2)
        self.squared, self.summed = m.sem("r_squared"), m.sem("r_summed")
        self.mean_ready, self.root_ready, self.inv_ready = m.sem("r_mean"), m.sem("r_root"), m.sem("r_inv")
        self.normed, self.affine, self.scaled, self.shifted = (m.sem("r_" + n) for n in ("normed", "affine", "scaled", "shifted"))
        self.turned, self.row_ready = m.sem("r_turned"), m.sem("r_row_ready")
        self.rows_stored = m.sems("r_rows_stored", 2)
        self.key_loaded, self.wq_loaded = m.sems("r_key_loaded", 2), m.sem("r_wq_loaded")
        self.q_psum, self.q_ready = m.credited_all("r_q_psum", 2), m.credited("r_q_ready")
        self.s_psum, self.s_taken = m.credited("r_s_psum"), m.credited("r_s_taken")
        self.scores_stored = m.credited("r_scores_stored")

    TILES = NT - FIRST
    COLS = slice(TC, T)
    UNITS = 2 * (NT - FIRST)

    def chunks(self, n, j):
        return self.ps[:, n + 2 * j:n + 2 * j + 2, 0:TC]

    def sync_start(self, sp, t):
        if t == 0:
            sp.dma_start(self.bb[:, :], self.io["b_blk"]).then_inc(self.loaded, 16)
        if t == 1:
            sp.wait_ge(self.gate_psum[1], KD + 1)
            sp.wait_ge(self.merged, 2 * KD + 1)
        if t == 2:
            sp.wait_ge(self.normed, 1)

    def sync_step(self, sp, t, i, j):
        b = i * 2 + j
        if t == 0:
            for e, (blk, wname) in enumerate(((BLK_GA, "w_paT"), (BLK_GB, "w_pbT"))):
                sp.wait_ge(self.gate_psum[1 - e], i * 2 + (j + e + 1))
                sp.dma_start(self.w, self.io["w_blk"][i * 2 + (blk + j)]).then_inc(self.w_loaded, 16)
                sp.wait_ge(self.branch_psum[1 - e], i * 2 + (j + e + 1))
                sp.dma_start(self.wp, self.io[wname][b]).then_inc(self.wp_loaded, 16)
        if t == 1:
            sp.wait_ge(self.o_psum[1 - j], i + (j + 1))
            sp.dma_start(self.w, self.io["w_oT"][b]).then_inc(self.wo_loaded, 16)
            sp.wait_ge(self.o_taken[j], i * 3 + 1)
            sp.dma_start(self.xb[:, j, :], self.io["xT"][:, bass.ds(b, 1), self.COLS].rearrange("p o t -> p (o t)")
                         ).then_inc(self.x_loaded[j], 16)
        if t == 2:
            sp.wait_ge(self.q_psum[1 - j], i + (j + 1))
            if j == 0:
                sp.wait_ge(self.scores_stored, i * 64 + 1)
            sp.dma_start(self.w, self.io["w_pqT"][b]).then_inc(self.wq_loaded, 16)
            sp.wait_ge(self.s_psum, i * 2 + (j + 1))
            sp.dma_start(self.key[:, j, :], self.io["sub_keysT"][:, bass.ds(b, 1), :].rearrange("p o t -> p (o t)")
                         ).then_inc(self.key_loaded[j], 16)

    def tensor(self, pe):
        hT, branchT, ps = self.hT, self.branchT, self.ps
        with pe.Fori(0, KD) as i:
            for j in range(2):
                pe.wait_ge(self.w_loaded, i * 32 + (16 * j + 16))
                pe.wait_ge(self.sig_ready[j], i + 1)
                for k in range(KD):
                    for c in range(2):
                        mm = pe.matmul(ps[:, 2 * j + c, 0:TC], self.w[:, k, :], hT[:, k, (c + 1) * TC:(c + 2) * TC],
                                       start=(k == 0), stop=(k == KD - 1))
                mm.then_inc(self.gate_psum[j], 1)
                pe.wait_ge(self.wp_loaded, i * 32 + (16 * j + 16))
                pe.wait_ge(self.used[j], i + 1)
                for k in range(4):
                    for c in range(2):
                        mm = pe.matmul(ps[:, 4 + 2 * j + c, 0:TC], self.wp[:, k, :],
                                       branchT[:, 4 * j + k, (c + 1) * TC:(c + 2) * TC], start=(k == 0), stop=(k == 3))
                mm.then_inc(self.branch_psum[j], 1)
        pe.wait_ge(self.merged, 2 * KD + 1)
        with pe.Fori(0, KD // 2) as i:
            for j in range(2):
                pe.wait_ge(self.wo_loaded, i * 32 + (16 * j + 16))
                pe.wait_ge(self.o_taken[j], i * 3 + 1)
                for k in range(KD):
                    for c, mT in enumerate((hT, branchT)):
                        mm = pe.matmul(ps[:, 2 * j + c, 0:TC], self.w[:, k, :], mT[:, k, 0:TC],
                                       start=(k == 0), stop=(k == KD - 1))
                mm.then_inc(self.o_psum[j], 1)
        for j in range(2):
            pe.wait_ge(self.o_taken[j], KD // 2 * 3 + 1)
        for k in range(KD):
            pe.wait_ge(self.squared, k + 1)
            for c in range(2):
                mm = pe.matmul(ps[:, c, 0:TC], self.ones, self.sq[:, k % 2, c * TC:(c + 1) * TC],
                               start=(k == 0), stop=(k == KD - 1))
            mm.then_inc(self.summed, 1)
        for n in range(self.UNITS):
            src, t = (branchT, hT)[n // self.TILES], FIRST + n % self.TILES
            if n == self.TILES:
                pe.wait_ge(self.affine, KD)
                pe.wait_ge(self.shifted, KD)
            if n >= 2:
                pe.wait_ge(self.row_ready, n - 1)
            for k in range(KD):
                at = 4 + 2 * (n % 2) + k // 4
                mm = pe.transpose(ps[:, at, k % 4 * P:(k % 4 + 1) * P], src[:, k, t * P:(t + 1) * P], self.ident)
            mm.then_inc(self.turned, 1)
        pe.wait_ge(self.row_ready, self.UNITS)
        pe.wait_ge(self.mean_ready, 1)
        with pe.Fori(0, PH // 2) as i:
            for j in range(2):
                pe.wait_ge(self.wq_loaded, i * 32 + (16 * j + 16))
                pe.wait_ge(self.q_ready, i * 2 + (j + 1))
                for k in range(KD):
                    for c in range(2):
                        mm = pe.matmul(ps[:, c, 0:TC], self.w[:, k, :], hT[:, k, (c + 1) * TC:(c + 2) * TC],
                                       start=(k == 0), stop=(k == KD - 1))
                mm.then_inc(self.q_psum[j], 1)
                pe.wait_ge(self.q_ready, i * 2 + (j + 2))
                pe.wait_ge(self.key_loaded[j], i * 16 + 16)
                pe.wait_ge(self.s_taken, i * 8 + (4 * j + 1))
                for half in range(2):
                    rows = slice(half * PHALF, (half + 1) * PHALF)
                    for t in range(self.TILES):
                        mm = pe.matmul(ps[:, 4 + 2 * half + t // 4, t % 4 * PK:(t % 4 + 1) * PK],
                                       self.q[rows, t * P:(t + 1) * P], self.key[rows, j, :], start=True, stop=True)
                mm.then_inc(self.s_psum, 1)

    def scalar_start(self, act, t):
        if t == 0:
            act.wait_ge(self.loaded, 16)
        if t == 2:
            for j in range(2):
                act.wait_ge(self.o_taken[j], KD // 2 * 3 + 1)
            for k in range(KD):
                if k >= 2:
                    act.wait_ge(self.summed, k - 1)
                act.activation(self.sq[:, k % 2, :], self.branchT[:, k, self.COLS], ACT.Square).then_inc(self.squared, 1)
            act.wait_ge(self.mean_ready, 1)
            act.activation(self.rs, self.rs, ACT.Sqrt).then_inc(self.root_ready, 1)
            act.wait_ge(self.normed, 1)
            for k in range(KD):
                own = self.hT[:, k, TC:SEQ]
                act.activation(own, own, ACT.Identity, bias=self.modT[:, MOD_SHIFT2 + k, 0:1],
                               scale=self.A2[:, k, 0:1]).then_inc(self.affine, 1)
            for n in range(self.UNITS):
                act.wait_ge(self.turned, n + 1)
                if n >= 2:
                    act.wait_ge(self.rows_stored[n % 2], n // 2 * 16)
                act.activation(self.row[:, n % 2, :].rearrange("p (b c) -> p b c", b=2),
                               self.ps[:, 4 + 2 * (n % 2):6 + 2 * (n % 2), :], ACT.Copy).then_inc(self.row_ready, 1)
                act.wait_ge(self.row_ready, n + 1)
                rows = (self.x1_rows, self.h2_rows)[n // self.TILES][FIRST + n % self.TILES]
                act.dma_start(rows, self.row[:, n % 2, :]).then_inc(self.rows_stored[n % 2], 16)
            for j in range(2):
                act.wait_ge(self.rows_stored[j], self.UNITS // 2 * 16)

    def scalar_step(self, act, t, i, j):
        if t == 0:
            for e, blk in enumerate((BLK_GA, BLK_GB)):
                act.wait_ge(self.gate_psum[e], i * 2 + (j + 2))
                act.wait_ge(self.merged, i * 4 + (2 * j + 1))
                act.activation(self.sg[:, e, :].rearrange("p (c t) -> p c t", c=2), self.chunks(0, e), ACT.Sigmoid,
                               bias=self.bb[:, bass.ds(i * 2 + (blk + j), 1)]).then_inc(self.sig_ready[e], 1)
        if t == 2:
            act.wait_ge(self.q_psum[j], i + 2)
            act.wait_ge(self.s_psum, i * 2 + (j + 1))
            act.activation(self.q.rearrange("p (c t) -> p c t", c=2), self.chunks(0, 0), ACT.Copy).then_inc(self.q_ready, 1)
            act.wait_ge(self.s_psum, i * 2 + (j + 2))
            HT = self.TILES // 2
            for e in range(2):
                act.wait_ge(self.scores_stored, i * 64 + (32 * j + 16 * e + 1))
                for half in range(2):
                    banks = self.ps[:, 4 + 2 * half:6 + 2 * half, :].rearrange("p b c -> p (b c)")
                    act.activation(self.scores.rearrange("p (t s k) -> p t s k", s=2, k=PK)[:, :, half, :],
                                   banks[:, e * HT * PK:(e + 1) * HT * PK].rearrange("p (t k) -> p t k", k=PK),
                                   ACT.Copy).then_inc(self.s_taken, 1)
                act.wait_ge(self.s_taken, i * 8 + (4 * j + 2 * e + 3))
                act.dma_start(self.score_rows[FIRST + e * HT:FIRST + (e + 1) * HT, bass.ds(i * 2 + j, 1), :, :]
                              .rearrange("t o p k -> p t (o k)"),
                              self.scores.rearrange("p (t k) -> p t k", k=2 * PK)).then_inc(self.scores_stored, 16)

    def vector_start(self, dve, t):
        if t != 2:
            return
        for j in range(2):
            dve.wait_ge(self.o_taken[j], KD // 2 * 3 + 1)
        dve.wait_ge(self.summed, KD)
        dve.tensor_scalar(self.rs.rearrange("p (c t) -> p c t", c=2), self.chunks(0, 0), 1.0 / D, EPS,
                          ALU.mult, ALU.add).then_inc(self.mean_ready, 1)
        dve.wait_ge(self.root_ready, 1)
        dve.reciprocal(self.rs, self.rs).then_inc(self.inv_ready, 1)
        dve.wait_ge(self.inv_ready, 1)
        dve.tensor_tensor(self.hT[:, :, self.COLS], self.branchT[:, :, self.COLS],
                          self.rs.unsqueeze(1).to_broadcast([P, KD, T - TC]), ALU.mult).then_inc(self.normed, 1)
        dve.wait_ge(self.normed, 1)
        for A, op, done in ((self.A2[:, :, 1:NB + 1], ALU.mult, self.scaled),
                            (self.modT[:, MOD_SHIFT2:MOD_SHIFT2 + KD, 1:NB + 1], ALU.add, self.shifted)):
            for k in range(KD):
                if done is self.shifted:
                    dve.wait_ge(self.scaled, k + 1)
                own = self.hT[:, k, SEQ:T].rearrange("p (b l) -> p b l", l=LS)
                dve.tensor_tensor(own, own, A[:, k, :].unsqueeze(2).to_broadcast([P, NB, LS]), op).then_inc(done, 1)

    def vector_step(self, dve, t, i, j):
        b = i * 2 + j
        if t == 0:
            three = lambda a: a.rearrange("p (c t) -> p c t", c=2)
            for e, dst in enumerate((self.sg[:, 0, :], self.sg[:, 1, :])):
                dve.wait_ge(self.sig_ready[e], i * 2 + (j + 2))
                dve.wait_ge(self.branch_psum[e], i * 2 + (j + 2))
                dve.tensor_tensor(three(dst), self.chunks(4, e), three(self.sg[:, e, :]), ALU.mult).then_inc(self.used[e], 1)
            for e in range(2):
                dve.wait_ge(self.used[e], i * 2 + (j + 2))
            for c, mT in enumerate((self.hT, self.branchT)):
                dve.tensor_tensor(mT[:, bass.ds(b, 1), 0:TC].rearrange("p o t -> p (o t)"), self.sg[:, 0, c * TC:(c + 1) * TC],
                                  self.sg[:, 1, c * TC:(c + 1) * TC], ALU.add).then_inc(self.merged, 1)
        if t == 1:
            dve.wait_ge(self.o_psum[j], i + 2)
            dve.wait_ge(self.x_loaded[j], i * 16 + 16)
            x1 = lambda lo, hi: self.branchT[:, bass.ds(b, 1), lo:hi].rearrange("p o t -> p (o t)")
            gate = lambda a, z: self.modT[:, bass.ds(i * 2 + (MOD_GATE1 + j), 1), a:z].rearrange("p o t -> p (o t)")
            for c, (lo, hi) in enumerate(((TC, 2 * TC), (2 * TC, SEQ))):
                dve.scalar_tensor_tensor(x1(lo, hi), self.ps[:, 2 * j + c, 0:hi - lo], gate(0, 1), self.xb[:, j, lo - TC:hi - TC],
                                         ALU.mult, ALU.add).then_inc(self.o_taken[j], 1)
            streams = lambda a: a.rearrange("p (b l) -> p b l", l=LS)
            dve.tensor_tensor(streams(self.tmp[:, j, :]), streams(self.ps[:, 2 * j + 1, SEQ - 2 * TC:TC]),
                              gate(1, NB + 1).unsqueeze(2).to_broadcast([P, NB, LS]), ALU.mult).then_inc(self.o_scaled[j], 1)
            dve.wait_ge(self.o_scaled[j], i + 1)
            dve.tensor_tensor(x1(SEQ, T), self.tmp[:, j, :], self.xb[:, j, SEQ - TC:T - TC], ALU.add).then_inc(self.o_taken[j], 1)


def phase_experts(nc, io, hT, branchT, modT, A2, ident, ones, score_rows, x1_rows, h2_rows, g2_rows):
    K = TOPK
    HALF = K // 2
    N1 = FIRST * PH

    def u_slot(first, n, k):
        if first:
            return k % HALF, n * 2 + k // HALF
        slot = (k + HALF) % K
        return slot, (n + N1 if slot < HALF else n - N1)

    with ExitStack() as ctx:
        m = Mem(nc, ctx)
        u = m.sb("u_rows", [P, HALF, D])
        v = m.sb("v_rows", [P, K, D])
        h2 = m.sb("h2_rows_sb", [P, D])
        g2 = m.sb("g2_rows_sb", [P, D])
        acc = m.sb("acc", [P, 2, D])
        more_u = hT.rearrange("p k t -> p (k t)")[:, 0:HALF * D].rearrange("p (s d) -> p s d", s=HALF)
        u_at = lambda slot: u[:, slot, :] if slot < HALF else more_u[:, slot - HALF, :]
        sc = m.sb("scores", [P, 2, 2, PK])
        iota = m.sb("iota16", [P, K])
        token = m.sb("token", [1, 1])
        sv = m.sb("half_best", [P, 2, K])
        si = m.sb("half_index", [P, 2, K], U32)
        sif = m.sb("half_index_f", [P, 2, K])
        cand = m.sb("cand", [P, K, K])
        fv = m.sb("best", [P, 2, K])
        fi = m.sb("best_at", [P, K], U32)
        ab = m.sb("best_pair", [P, 2, K], U32)
        hot = m.sb("hot", [P, 2, K, K])
        pick = m.sb("picked_f", [P, 2, K])
        pick_u = m.sb("picked", [P, 2, 2, K], U32)
        eidx = m.sb("expert_index", [P, 2, K], U32)
        neg = m.sb("neg_best", [P, 2])
        g = m.sb("gates16", [P, 2, K])
        gsum = m.sb("gates_sum", [P, 2])
        ginv = m.sb("gates_inv", [P, 2])
        dot = m.sb("dots", [P, 2, K])
        actv = m.sb("gelu", [P, 2, K])
        wgt = m.sb("weights", [P, 2, K])
        iota_loaded = m.sem("iota_loaded")
        tables_ready = m.sem("tables_ready")
        sc_loaded = m.sem("sc_loaded")
        u_loaded, v_loaded = m.sems("u_loaded", K), m.sems("v_loaded", K)
        u_used, v_used = m.credited_all("u_used", K), m.credited_all("v_used", K)
        chosen = m.sem("chosen")
        sc_used = m.credited("sc_used")
        best_ready = m.sem("best_ready")
        exp_ready = m.sem("exp_ready")
        g_ready = m.sem("g_ready")
        pick_ready = m.sem("pick_ready")
        idx_ready = m.sem("idx_ready")
        dots_ready = u_used[HALF - 1]
        dots_of = lambda first, units: (units * 2 if first else units + N1) + 1
        gelu_ready = m.sem("gelu_ready")
        wgt_ready = m.sem("wgt_ready")
        acc_zeroed = m.sem("acc_zeroed")
        h2_loaded = m.sem("h2_loaded")
        g2_loaded = m.sem("g2_loaded")
        joined = m.sem("joined")
        combined = m.credited("combined")
        stored = m.credited("y_stored")
        rest = Rest(nc, io, m, hT, branchT, modT, A2, ident, ones, x1_rows, h2_rows, score_rows)
        block = ctx.enter_context(nc.Block())
        nothing = lambda *_: None

        def over_units(eng, per_unit, tile_start=nothing, tile_end=nothing, rest_start=nothing, rest_step=nothing):
            for t in range(FIRST):
                tile_start(t, True)
                rest_start(eng, t)
                with eng.Fori(0, PH // 2) as i:
                    for j in range(2):
                        per_unit(True, t, i * 2 + (t * PH + j), j)
                        rest_step(eng, t, i, j)
                tile_end(t, True)
            with eng.Fori(0, NT - FIRST) as r:
                tile_start(r + FIRST, False)
                with eng.Fori(0, PH // 2) as i:
                    for j in range(2):
                        per_unit(False, r + FIRST, r * PH + i * 2 + (FIRST * PH + j), j)
                tile_end(r + FIRST, False)

        @block.tensor
        def _(pe):
            rest.tensor(pe)

        flat = score_rows.rearrange("t h p k -> (t h) p k")

        @block.sync
        def _(sp):
            sp.dma_start(iota[:, :], io["iota16"]).then_inc(iota_loaded, 16)
            sp.dma_start(h2[:, :], h2_rows[0]).then_inc(h2_loaded, 16)
            sp.dma_start(sc[:, 0, :, :], flat[0].rearrange("p (s k) -> p s k", s=2)).then_inc(sc_loaded, 16)

            def tile_start(t, first):
                sp.wait_ge(combined, t + 1)
                sp.dma_start(g2[:, :], g2_rows[t]).then_inc(g2_loaded, 16)

            def unit(first, t, n, j):
                sp.wait_ge(sc_used, n + 1)
                sp.wait_ge(sc_loaded, n * 16 + 16)
                sp.dma_start(sc[:, 1 - j, :, :], flat[n + 1].rearrange("p (s k) -> p s k", s=2)).then_inc(sc_loaded, 16)

            def tile_end(t, first):
                sp.wait_ge(dots_ready, dots_of(first, t * PH + PH))
                sp.dma_start(h2[:, :], x1_rows[t]).then_inc(h2_loaded, 16)
                if t is FIRST - 1:
                    for j in range(2):
                        sp.wait_ge(rest.rows_stored[j], rest.UNITS // 2 * 16)
                    sp.wait_ge(rest.scores_stored, PH * 32 + 1)
                sp.wait_ge(combined, t + 2)
                sp.dma_start(h2[:, :], h2_rows[t + 1]).then_inc(h2_loaded, 16)
                sp.dma_start(io["y"][t], acc[:, 0, :]).then_inc(stored, 16)

            over_units(sp, unit, tile_start, tile_end, rest.sync_start, rest.sync_step)
            sp.wait_ge(stored, NT * 16 + 1)
            sp.wait_ge(h2_loaded, NT * 32 + 16)

        @block.gpsimd
        def _(pool):
            pool.memset(token[:, :], 0.0).then_inc(tables_ready, 1)

            def unit(first, t, n, j):
                if not first:
                    pool.wait_ge(rest.s_psum, PH + 1)
                pool.wait_ge(v_used[0], n + 1)
                pool.wait_ge(dots_ready, dots_of(first, n))
                pool.wait_ge(pick_ready, n * 2 + 2)
                for e in range(2):
                    cut = slice(e * HALF, (e + 1) * HALF)
                    pool.tensor_tensor(eidx[:, j, cut], pick_u[:, j, 0, cut], pick_u[:, j, 1, cut], ALU.add).then_inc(idx_ready, 1)
                pool.wait_ge(tables_ready, 1)
                pool.wait_ge(idx_ready, n * 2 + 2)

                def gather(rows, table, k, loaded):
                    pool.indirect_dma_start(rows, None, io[table],
                                            bass.IndirectOffsetOnAxis(ap=eidx[:, j, k:k + 1], axis=0)).then_inc(loaded, 16)

                for k in range(K):
                    slot, _ = u_slot(first, n, k)
                    if first and k >= HALF and k % 2 == 0:
                        pool.wait_ge(tables_ready, 1)
                        pool.wait_ge(u_used[slot + 1], n * 2 + 2)
                    gather(u_at(slot), "expert_u", k, u_loaded[slot])
                for k in range(K):
                    if k % 4 == 0:
                        pool.wait_ge(tables_ready, 1)
                        pool.wait_ge(v_used[k + 3], n + 1)
                    gather(v[:, k, :], "expert_v", k, v_loaded[k])

            over_units(pool, unit)

        @block.scalar
        def _(act):
            def weigh(n, j):
                act.wait_ge(best_ready, n + 1)
                act.activation(g[:, j, :], fv[:, j, :], ACT.Exp, bias=neg[:, j:j + 1],
                               accum_out=gsum[:, j:j + 1]).then_inc(exp_ready, 1)

            def unit(first, t, n, j):
                act.wait_ge(dots_ready, dots_of(first, n + 1))
                act.activation(actv[:, j, :], dot[:, j, :], ACT.Gelu).then_inc(gelu_ready, 1)
                weigh(n + 1, 1 - j)

            weigh(0, 0)
            over_units(act, unit, nothing, nothing, rest.scalar_start, rest.scalar_step)

        @block.vector
        def _(dve):
            def choose(n, j):
                dve.sem_clear(chosen)
                s = Steps(dve, chosen)
                step = lambda ins: (s.did(ins), s.settle())
                dve.wait_ge(sc_loaded, n * 16 + 16)
                step(dve.tensor_copy(sif[:, :, :], sc[:, j, :, 0:K]))
                for half in range(2):
                    a = sc[:, j, half, :]
                    step(dve.max(sv[:, half, 0:8], a))
                    s.did(dve.max_index(si[:, half, 0:8], sv[:, half, 0:8], a))
                    step(dve.match_replace(a, sv[:, half, 0:8], a, -3e38))
                    step(dve.max(sv[:, half, 8:16], a))
                    step(dve.max_index(si[:, half, 8:16], sv[:, half, 8:16], a))
                s.did(dve.tensor_scalar(sif[:, 0, :], si[:, 0, :], float(PK), None, ALU.mult))
                step(dve.tensor_copy(sif[:, 1, :], si[:, 1, :]))
                dve.tensor_tensor(cand[:, :, :], sv[:, 0, :].unsqueeze(2).to_broadcast([P, K, K]),
                                  sv[:, 1, :].unsqueeze(1).to_broadcast([P, K, K]), ALU.add).then_inc(sc_used, 1)
                dve.wait_ge(sc_used, n + 2)
                step(dve.tensor_copy(neg[:, j:j + 1], cand[:, 0, 0:1]))
                c = cand[:, :, :].rearrange("p a b -> p (a b)")
                step(dve.max(fv[:, j, 0:8], c))
                s.did(dve.max_index(fi[:, 0:8], fv[:, j, 0:8], c))
                step(dve.match_replace(c, fv[:, j, 0:8], c, -3e38))
                step(dve.max(fv[:, j, 8:16], c))
                s.did(dve.max_index(fi[:, 8:16], fv[:, j, 8:16], c))
                dve.tensor_scalar(neg[:, j:j + 1], fv[:, j, 0:1], -1.0, None, ALU.mult).then_inc(best_ready, 1)
                s.settle()
                s.did(dve.tensor_scalar(ab[:, 0, :], fi[:, :], 4, None, ALU.logical_shift_right))
                step(dve.tensor_scalar(ab[:, 1, :], fi[:, :], 15, None, ALU.bitwise_and))
                for half in range(2):
                    s.did(dve.tensor_tensor(hot[:, half], ab[:, half, :].unsqueeze(2).to_broadcast([P, K, K]),
                                            iota[:, :].unsqueeze(1).to_broadcast([P, K, K]), ALU.is_equal))
                s.settle()
                for half in range(2):
                    s.did(dve.tensor_tensor(hot[:, half], hot[:, half],
                                            sif[:, half, :].unsqueeze(1).to_broadcast([P, K, K]), ALU.mult))
                s.settle()
                step(dve.tensor_reduce(pick[:, :, :], hot[:, :, :, :], AX.X, ALU.add))
                for half in range(2):
                    dve.tensor_copy(pick_u[:, j, half, :], pick[:, half, :]).then_inc(pick_ready, 1)
                dve.wait_ge(exp_ready, n + 1)
                step(dve.reciprocal(ginv[:, j:j + 1], gsum[:, j:j + 1]))
                dve.tensor_scalar(g[:, j, :], g[:, j, :], ginv[:, j:j + 1], None, ALU.mult).then_inc(g_ready, 1)

            def tile_start(t, first):
                dve.wait_ge(h2_loaded, t * 32 + 16)
                dve.wait_ge(combined, t + 1)
                dve.wait_ge(stored, t * 16 + 1)
                dve.memset(acc[:, :, :], 0.0).then_inc(acc_zeroed, 1)

            def unit(first, t, n, j):
                for k in range(K):
                    slot, before = u_slot(first, n, k)
                    dve.wait_ge(u_loaded[slot], before * 16 + 16)
                    dve.tensor_tensor_reduce(u_at(slot), u_at(slot), h2[:, :], 1.0, 0.0, ALU.mult, ALU.add,
                                             dot[:, j, k:k + 1]).then_inc(u_used[slot], 1)
                choose(n + 1, 1 - j)
                dve.wait_ge(gelu_ready, n + 1)
                dve.wait_ge(g_ready, n + 1)
                dve.tensor_tensor(wgt[:, j, :], actv[:, j, :], g[:, j, :], ALU.mult).then_inc(wgt_ready, 1)
                dve.wait_ge(wgt_ready, n + 1)
                dve.wait_ge(acc_zeroed, t + 1)
                for k in range(K):
                    dve.wait_ge(v_loaded[k], n * 16 + 16)
                    if k >= 2:
                        dve.wait_ge(v_used[k - 2], n + 2)
                    dve.scalar_tensor_tensor(acc[:, k % 2, :], v[:, k, :], wgt[:, j, k:k + 1], acc[:, k % 2, :],
                                             ALU.mult, ALU.add).then_inc(v_used[k], 1)
                for k in (K - 2, K - 1):
                    dve.wait_ge(v_used[k], n + 2)

            def tile_end(t, first):
                dve.tensor_tensor(acc[:, 0, :], acc[:, 0, :], acc[:, 1, :], ALU.add).then_inc(joined, 1)
                dve.wait_ge(g2_loaded, t * 16 + 16)
                dve.wait_ge(joined, t * 2 + 1)
                dve.tensor_tensor(acc[:, 0, :], acc[:, 0, :], g2[:, :], ALU.mult).then_inc(joined, 1)
                dve.wait_ge(joined, t * 2 + 2)
                dve.wait_ge(h2_loaded, t * 32 + 32)
                dve.tensor_tensor(acc[:, 0, :], acc[:, 0, :], h2[:, :], ALU.add).then_inc(combined, 1)

            dve.wait_ge(iota_loaded, 16)
            choose(0, 0)
            over_units(dve, unit, tile_start, tile_end, rest.vector_start, rest.vector_step)
            dve.wait_ge(combined, NT + 1)


def build(nc, io, upto=99):
    scratch = lambda name, shape: nc.dram_tensor(name, shape, F32).ap()
    x1_rows = scratch("x1_rows", (NT, P, D))
    h2_rows = scratch("h2_rows", (NT + 1, P, D))
    g2_rows = scratch("g2_rows", (NT, P, D))
    score_rows = scratch("score_rows", (NT + 1, PH, P, 2 * PK))
    with ExitStack() as whole:
        g = Mem(nc, whole)
        consts = g.sb("consts", [P, 2 * P])
        ident, ones = consts[:, 0:P], consts[:, P:2 * P]
        modT = g.sb("modT", [P, 6 * KD, NB + 1])
        A1 = g.sb("A1", [P, KD, NB + 1])
        A2 = g.sb("A2", [P, KD, NB + 1])
        phase_constants(nc, io["consts"][:, 0:2 * P], "constants", consts)
        phase_modulation(nc, io, modT, A1, A2, ident)
        if upto < 2:
            return
        hT = g.sb("hT", [P, KD, T])
        phase_norm(nc, io, "1", hT, hT, True, ones, A1, modT, 0)
        if upto < 3:
            return
        branchT = g.sb("branchT", [P, 8, T])
        haT, hbT = branchT[:, 0:4, :], branchT[:, 4:8, :]
        forget = ExitStack(); f = Mem(nc, forget)
        masks = f.sb("masks", [P, 12 * P])
        pair_ones, causal, causalT, stream_rows = (masks[:, n * P:(n + 1) * P] for n in range(4))
        head_rows = masks[:, 4 * P:12 * P].rearrange("p (h t) -> p h t", h=AH)
        phase_constants(nc, io["consts"][:, 2 * P:14 * P], "masks", masks)
        gates = f.sb("gates", [GATE_W, T])
        lf = f.sb("lf", [GATE_W, T])
        attn = ExitStack(); a = Mem(nc, attn)
        qk = a.sb("qkT", [P, 8, T])
        va = a.sb("va", [P, NT, AH * AD])
        phase_project(nc, io, "A", BLK_Q, hT, qk, [(0, va)])
        phase_gates(nc, io, hT, gates, va)
        gqk = a.sb("gqk", [P, 8])
        negF = a.sb("negF", [AH, SEQ])
        negFc = a.sb("negFc", [AH, NB * PAST])
        negFn = a.sb("negFn", [AH, NB * LS])
        phase_head_norm(nc, io, qk, gqk, pair_ones)
        phase_forget(nc, io, gates, lf, negF, negFc, negFn)
        phase_attend_prompt(nc, io, qk, va, negF, haT, ident, causal, head_rows)
        phase_attend_streams(nc, io, qk, va, negFc, negFn, haT, hbT.rearrange("p b t -> p (b t)"), ident, stream_rows)
        attn.close()
        mem = ExitStack(); b = Mem(nc, mem)
        rows = b.sb("mlstm_rows", [BH, 2, T])
        cols = b.sb("mlstm_cols", [P, 3, NT, BH])
        phase_mlstm_rows(nc, io, gates, lf, rows, cols)
        qkb = b.sb("qkbT", [P, 8, T])
        kb = b.sb("kb", [P, NT, BH * BD])
        vb = b.sb("vb", [P, NT, BH, BD + 1])
        phase_ones(nc, vb)
        phase_project(nc, io, "B", BLK_QB, hT, qkb, [(1, kb), (2, vb)])
        phase_mlstm(nc, io, qkb, kb, vb, rows, cols, hbT, ident, causalT, head_rows)
        mem.close()
        forget.close()
        first = ExitStack()
        mT = Mem(nc, first).sb("mergedT", [P, KD, TC])
        phase_merge(nc, io, hT, haT, hbT, mT)
        phase_out(nc, io, mT, modT, branchT)
        first.close()
        phase_norm(nc, io, "2", branchT, hT, False, ones, A2, modT, MOD_SHIFT2, 1)
        phase_turn(nc, branchT, hT, modT, ident, x1_rows, h2_rows, g2_rows)
        phase_retrieval_scores(nc, io, hT, score_rows)
        phase_experts(nc, io, hT, branchT, modT, A2, ident, ones, score_rows, x1_rows, h2_rows, g2_rows)


_DEV = 99
_OUTS = [("new_v", (P, NT, AH * AD)), ("new_kT", (P, 4, T)), ("new_logfT", (AH, T)),
         ("new_mT", (BH, NB + 1)), ("new_C_prompt", (BH, P, BD + 1)), ("new_C_sample", (BH, P, NB, BD + 1)),
         ("y", (NT, P, D))]


def kernel(**a):
    import concourse.bacc as bacc
    from concourse.bass_utils import run_bass_kernel_spmd

    def cols(w, n):
        k = w.shape[0] // P
        return w.reshape(k, P, n, P).transpose(2, 1, 0, 3).reshape(n, P, k * P)

    def on_rows(v):
        return v.reshape(-1, P).T

    f = {k: np.asarray(v) for k, v in a.items()}
    w_in, b_in = f["w_in"][0], f["b_in"][0]
    off = np.cumsum([0, 512, 512, 512, 8, 512, 512, 512, 4, 4, 512, 1024, 1024])
    cut = lambda i: slice(int(off[i]), int(off[i + 1]))
    x = np.concatenate([f["x_prompt"].reshape(SEQ, D), f["x_sample"].reshape(NB * LS, D)])
    c = np.concatenate([f["c_prompt"], f["c_sample"]])
    order = (0, 1, 4, 5, 9, 10, 11)
    w_blk = np.concatenate([w_in[:, cut(i)] for i in order], 1)
    b_blk = np.concatenate([b_in[cut(i)] for i in order])
    w_gate, b_gate = np.zeros((D, GATE_W), np.float32), np.zeros((GATE_W, 1), np.float32)
    for row, i in ((GATE_F, 3), (GATE_I, 7), (GATE_LF, 8)):
        w_gate[:, row:row + int(off[i + 1] - off[i])] = w_in[:, cut(i)]
        b_gate[row:row + int(off[i + 1] - off[i]), 0] = b_in[cut(i)]
    rows = lambda w: w.reshape(KD, P, -1).transpose(1, 0, 2)
    eye = np.eye(P, dtype=np.float32)
    pair = np.kron(np.eye(2), np.ones((AD, AD))).astype(np.float32)
    n = np.arange(P)
    causal = np.where(n[None, :] <= n[:, None], 0.0, NEG).astype(np.float32)
    stream_rows = (n[:, None] == n[None, :] // LS).astype(np.float32)
    head_rows = np.repeat(np.eye(P, AH, dtype=np.float32), P, 1)
    stream_masks = np.where((n[None, None, :] // LS == np.arange(NB)[None, :, None])
                            & (n[None, None, :] % LS <= n[:, None, None] % LS), 0.0, NEG).astype(np.float32)
    own = (n[None, :] // LS == np.arange(NB)[:, None]).astype(np.float32)
    start = np.array([t % P == 0 if t < SEQ else t % LS == 0 for t in range(T)], np.float32)
    arrays = {
        "consts": np.concatenate([eye, np.ones((P, P), np.float32), pair, causal, causal.T, stream_rows, head_rows], 1),
        "stream_masks": stream_masks,
        "stream_maskT": np.where((n[:, None] // LS == n[None, :] // LS) & (n[:, None] <= n[None, :]), 0.0, NEG).astype(np.float32),
        "own_stream": np.broadcast_to(own[None], (P, NB, P)),
        "own_rows": own.T,
        "scan_rows": np.broadcast_to(np.stack([1.0 - start, np.where(np.arange(T) >= SEQ, start * NEG, 0.0)]).astype(np.float32)[None], (BH, 2, T)),
        "state_mT": f["state_m"][0].T,
        "state_C": np.concatenate([f["state_C"][0].transpose(1, 2, 0, 3), f["state_n"][0].transpose(1, 2, 0)[..., None]], 3),
        "g_hbT": f["g_hb"][0].T,
        "w_oT": cols(f["w_o"][0], KD).reshape(KD, P, KD, P),
        "w_pqT": cols(f["w_pq"][0], PH).reshape(PH, P, KD, P),
        "sub_keysT": f["sub_keys"][0].transpose(1, 3, 0, 2).reshape(P, PH, PK),
        "iota16": np.broadcast_to(np.arange(TOPK, dtype=np.float32)[None], (P, TOPK)),
        "expert_u": f["expert_u"][0],
        "expert_v": f["expert_v"][0],
        "w_paT": cols(f["w_pa"][0], KD).reshape(KD, P, 4, P),
        "w_pbT": cols(f["w_pb"][0], KD).reshape(KD, P, 4, P),
        "g_qk": np.concatenate([on_rows(f["g_qa"].reshape(-1)), on_rows(f["g_ka"].reshape(-1))], 1),
        "cache_logfT": f["cache_logf"][0].transpose(2, 0, 1).reshape(AH, NB * PAST),
        "cache_kT": f["cache_k"][0].reshape(NB, PAST, 4, P).transpose(0, 3, 2, 1),
        "cache_v": f["cache_v"][0].reshape(NB, 4, P, AH * AD).transpose(0, 2, 1, 3),
        "cT": c.T.reshape(KD, P, NB + 1).transpose(1, 0, 2),
        "w_mod": f["w_mod"][0].reshape(KD, P, 12, 512).transpose(2, 1, 0, 3).reshape(12, P, KD, 512),
        "b_mod": on_rows(f["b_mod"][0]),
        "g12": np.stack([on_rows(f["g_norm1"][0]), on_rows(f["g_norm2"][0])], 1),
        "xT": x.T.reshape(KD, P, T).transpose(1, 0, 2),
        "w_blk": cols(w_blk, NBLK).reshape(NBLK, P, KD, P),
        "b_blk": on_rows(b_blk),
        "w_row": np.stack([rows(w_in[:, cut(i)]) for i in (2, 5, 6)]),
        "b_row": np.stack([b_in[cut(i)] for i in (2, 5, 6)]),
        "w_gate": rows(w_gate),
        "b_gate": b_gate,
    }
    nc = bacc.Bacc("TRN2", target_bir_lowering=False, num_devices=1)
    io, feed = {}, {}
    for name, v in arrays.items():
        v = np.ascontiguousarray(v)
        feed["in_" + name] = v
        io[name] = nc.dram_tensor("in_" + name, v.shape, mybir.dt.from_np(v.dtype), kind="ExternalInput").ap()
    for name, shape in _OUTS:
        io[name] = nc.dram_tensor("out_" + name, shape, F32, kind="ExternalOutput").ap()
    build(nc, io, _DEV)
    r = run_bass_kernel_spmd(nc, [feed], core_ids=[0]).results[0]
    got = {name: r["out_" + name] for name, _ in _OUTS}
    y = got["y"].reshape(T, D)
    k = got["new_kT"].transpose(2, 1, 0).reshape(T, AH, AD)
    v = got["new_v"].transpose(1, 0, 2).reshape(T, AH, AD)
    lf = got["new_logfT"].T
    st, ss, mm = got["new_C_prompt"], got["new_C_sample"].transpose(2, 0, 1, 3), got["new_mT"]
    whole = lambda a: np.ascontiguousarray(a[None])
    prompt = lambda a: whole(a[None, 0:SEQ])
    sample = lambda a: whole(a[SEQ:T].reshape((NB, LS) + a.shape[1:]))
    return (np.ascontiguousarray(y[None, 0:SEQ]), np.ascontiguousarray(y[SEQ:T].reshape(NB, LS, D)),
            prompt(k), prompt(v), prompt(lf), whole(st[None, :, :, 0:BD]), whole(st[None, :, :, BD]), whole(mm[:, 0][None]),
            sample(k), sample(v), sample(lf), whole(ss[..., 0:BD]), whole(ss[..., BD]), whole(mm[:, 1:].T))
```

```python
from contextlib import ExitStack

import numpy as np
import concourse.bass as bass
from concourse import mybir
from concourse.alu_op_type import AluOpType as ALU

ACT = mybir.ActivationFunctionType
AX = mybir.AxisListType
F32 = mybir.dt.float32
U32 = mybir.dt.uint32

P = 128
D = 1024
KD = D // P
SEQ = 1024
NB = 8
LS = 16
T = SEQ + NB * LS
NT = T // P
NPT = SEQ // P
NC = 3
TC = T // NC
FIRST = 3
PAST = 512
AH, AD = 8, 64
BH, BD = 4, 128
EPS = 1e-6
NEG = -1e30
PH, PK, PHALF, TOPK = 8, 128, 64, 16
BLK_Q, BLK_K, BLK_QB, BLK_KB, BLK_BO, BLK_GA, BLK_GB = 0, 4, 8, 12, 16, 20, 28
NBLK = 36
MOD_SHIFT1, MOD_SCALE1, MOD_GATE1, MOD_SHIFT2, MOD_SCALE2, MOD_GATE2 = range(0, 6 * KD, KD)
GATE_F, GATE_I, GATE_LF, GATE_W = 0, 32, 64, 96


class Steps:

    def __init__(self, eng, sem, base=0):
        self.eng, self.sem, self.base, self.n = eng, sem, base, 0

    def did(self, ins):
        ins.then_inc(self.sem, 1)
        self.n += 1
        return ins

    def settle(self):
        self.eng.wait_ge(self.sem, self.base + self.n)


class Mem:

    def __init__(self, nc, ctx):
        self.nc, self.ctx, self.signals = nc, ctx, []
        ctx.callback(self.clear)

    def clear(self):
        n = 0
        while n < len(self.signals):
            e = n
            while e + 1 < len(self.signals) and self.signals[e + 1] == self.signals[e] + 1:
                e += 1
            self.nc.gpsimd.sem_clear(range(self.signals[n], self.signals[e] + 1))
            n = e + 1

    def sb(self, name, shape, dt=F32):
        return self.ctx.enter_context(self.nc.sbuf_tensor(name, shape, dt))

    def ps(self, name, shape):
        return self.ctx.enter_context(self.nc.psum_tensor(name, shape, F32))

    def sem(self, name):
        handle = self.ctx.enter_context(self.nc.semaphore(name))
        self.signals.append(handle.num)
        return handle

    def credited(self, name):
        handle = self.sem(name)
        self.nc.gpsimd.sem_inc(handle, 1)
        return handle

    def credited_all(self, name, n):
        return [self.credited(f"{name}{i}") for i in range(n)]

    def sems(self, name, n):
        return [self.sem(f"{name}{i}") for i in range(n)]


def phase_constants(nc, src, name, consts):
    with ExitStack() as ctx:
        m = Mem(nc, ctx)
        loaded = m.sem(name + "_loaded")
        block = ctx.enter_context(nc.Block())

        @block.sync
        def _(sp):
            sp.dma_start(consts[:, :], src).then_inc(loaded, 16)
            sp.wait_ge(loaded, 16)


def phase_modulation(nc, io, modT, A1, A2, ident):
    NG, BPG, RING = 12, 4, 4
    NS = NB + 1
    with ExitStack() as ctx:
        m = Mem(nc, ctx)
        cT = m.sb("cT", [P, KD, NS])
        sig = m.sb("sig", [P, KD, NS])
        silu = m.sb("silu", [P, KD, NS])
        w = m.sb("w_mod_ring", [P, RING, KD, BPG * P])
        b = m.sb("b_mod", [P, NG * BPG])
        g12 = m.sb("g12", [P, 2, KD])
        row = m.sb("mod_rows", [P, 2, BPG * P])
        ps = m.ps("ps_mod", [P, 2, 512])
        ps_t = m.ps("ps_mod_turned", [P, 2, 512])
        small_loaded = m.sem("small_loaded")
        w_loaded = m.sems("w_loaded", RING)
        sig_done = m.sem("sig_done")
        rows_zeroed = m.sem("rows_zeroed")
        silu_ready = m.sem("silu_ready")
        mod_psum = m.credited_all("mod_psum", RING)
        row_ready = m.credited_all("mod_row", 2)
        turned = m.credited_all("mod_turned", 2)
        mod_taken = m.credited_all("mod_taken", 2)
        scaled = m.sem("scaled")
        block = ctx.enter_context(nc.Block())

        @block.sync
        def _(sp):
            sp.dma_start(cT[:, :, :], io["cT"]).then_inc(small_loaded, 16)
            sp.dma_start(b[:, :], io["b_mod"]).then_inc(small_loaded, 16)
            sp.dma_start(g12[:, :, :], io["g12"]).then_inc(small_loaded, 16)
            with sp.Fori(0, NG // RING) as i:
                for j in range(RING):
                    sp.wait_ge(mod_psum[j], i + 1)
                    sp.dma_start(w[:, j, :, :], io["w_mod"][i * RING + j]).then_inc(w_loaded[j], 16)

        @block.gpsimd
        def _(pool):
            pool.memset(row[:, :, :], 0.0).then_inc(rows_zeroed, 1)

        @block.scalar
        def _(act):
            act.wait_ge(small_loaded, 48)
            act.activation(sig[:, :, :], cT[:, :, :], ACT.Sigmoid).then_inc(sig_done, 1)
            act.wait_ge(rows_zeroed, 1)
            with act.Fori(0, NG // RING) as i:
                for j in range(RING):
                    e, n = j % 2, j // 2
                    act.wait_ge(mod_psum[j], i + 2)
                    act.wait_ge(turned[e], i * 2 + (n + 1))
                    act.activation(row[0:NS, e, :], ps[0:NS, e, :], ACT.Copy).then_inc(row_ready[e], 1)

        @block.tensor
        def _(pe):
            pe.wait_ge(silu_ready, 1)
            with pe.Fori(0, NG // RING) as i:
                for j in range(RING):
                    e, n = j % 2, j // 2
                    pe.wait_ge(w_loaded[j], i * 16 + 16)
                    pe.wait_ge(row_ready[e], i * 2 + (n + 1))
                    for k in range(KD):
                        mm = pe.matmul(ps[0:NS, e, :], silu[:, k, :], w[:, j, k, :], start=(k == 0), stop=(k == KD - 1))
                    mm.then_inc(mod_psum[j], 1)
                    pe.wait_ge(row_ready[e], i * 2 + (n + 2))
                    pe.wait_ge(mod_taken[e], i * 2 + (n + 1))
                    for q in range(BPG):
                        mm = pe.transpose(ps_t[:, e, q * P:(q + 1) * P], row[:, e, q * P:(q + 1) * P], ident)
                    mm.then_inc(turned[e], 1)

        @block.vector
        def _(dve):
            dve.wait_ge(sig_done, 1)
            dve.wait_ge(small_loaded, 48)
            dve.tensor_tensor(silu[:, :, :], sig[:, :, :], cT[:, :, :], ALU.mult).then_inc(silu_ready, 1)
            with dve.Fori(0, NG // 2) as i:
                for e in range(2):
                    dve.wait_ge(turned[e], i + 2)
                    first = (i * 2 + e) * BPG
                    dve.tensor_tensor(modT[:, bass.ds(first, BPG), :],
                                      ps_t[:, e, :].rearrange("p (q s) -> p q s", s=P)[:, :, 0:NS],
                                      b[:, bass.ds(first, BPG)].unsqueeze(2).to_broadcast([P, BPG, NS]),
                                      ALU.add).then_inc(mod_taken[e], 1)
            for e in range(2):
                dve.wait_ge(mod_taken[e], NG // 2 + 1)
            for n, (A, blk) in enumerate(((A1, MOD_SCALE1), (A2, MOD_SCALE2))):
                dve.scalar_tensor_tensor(A[:, :, :], modT[:, blk:blk + KD, :], 1.0,
                                         g12[:, n, :].unsqueeze(2).to_broadcast([P, KD, NS]),
                                         ALU.add, ALU.mult).then_inc(scaled, 1)
            dve.wait_ge(scaled, 2)


def phase_norm(nc, io, tag, src, dst, load, ones, A, modT, shift_blk, chunks=NC):
    prompt = min(chunks * TC, SEQ)
    with ExitStack() as ctx:
        m = Mem(nc, ctx)
        sq = m.sb("sq" + tag, [P, 2, KD, TC])
        rs = m.sb("rs" + tag, [P, T])
        ps = m.ps("ps_norm" + tag, [P, NC, 512])
        x_loaded = m.sems("x_loaded" + tag, NC)
        squared = m.sem("squared" + tag)
        summed = m.sem("summed" + tag)
        mean_ready = m.sem("mean_ready" + tag)
        root_ready = m.sem("root_ready" + tag)
        inv_ready = m.sem("inv_ready" + tag)
        normed = m.sem("normed" + tag)
        prompt_done = m.sem("prompt_done" + tag)
        sample_scaled = m.sem("sample_scaled" + tag)
        sample_done = m.sem("sample_done" + tag)
        block = ctx.enter_context(nc.Block())
        cut = [slice(c * TC, (c + 1) * TC) for c in range(chunks)]

        if load:
            @block.sync
            def _(sp):
                for c in range(chunks):
                    sp.dma_start(src[:, :, cut[c]], io["xT"][:, :, cut[c]]).then_inc(x_loaded[c], 16)

        @block.scalar
        def _(act):
            for c in range(chunks):
                if load:
                    act.wait_ge(x_loaded[c], 16)
                if c >= 2:
                    act.wait_ge(summed, c - 1)
                act.activation(sq[:, c % 2, :, :], src[:, :, cut[c]], ACT.Square).then_inc(squared, 1)
            for c in range(chunks):
                act.wait_ge(mean_ready, c + 1)
                act.activation(rs[:, cut[c]], rs[:, cut[c]], ACT.Sqrt).then_inc(root_ready, 1)
            act.wait_ge(normed, chunks)
            for k in range(KD):
                act.activation(dst[:, k, 0:prompt], dst[:, k, 0:prompt], ACT.Identity,
                               bias=modT[:, shift_blk + k, 0:1], scale=A[:, k, 0:1]).then_inc(prompt_done, 1)
            act.wait_ge(prompt_done, KD)

        @block.tensor
        def _(pe):
            for c in range(chunks):
                pe.wait_ge(squared, c + 1)
                for k in range(KD):
                    mm = pe.matmul(ps[:, c, 0:TC], ones, sq[:, c % 2, k, :], start=(k == 0), stop=(k == KD - 1))
                mm.then_inc(summed, 1)

        @block.vector
        def _(dve):
            for c in range(chunks):
                dve.wait_ge(summed, c + 1)
                dve.tensor_scalar(rs[:, cut[c]], ps[:, c, 0:TC], 1.0 / D, EPS, ALU.mult, ALU.add).then_inc(mean_ready, 1)
            for c in range(chunks):
                dve.wait_ge(root_ready, c + 1)
                dve.reciprocal(rs[:, cut[c]], rs[:, cut[c]]).then_inc(inv_ready, 1)
                dve.wait_ge(inv_ready, c + 1)
                if load:
                    dve.wait_ge(x_loaded[c], 16)
                dve.tensor_tensor(dst[:, :, cut[c]], src[:, :, cut[c]],
                                  rs[:, cut[c]].unsqueeze(1).to_broadcast([P, KD, TC]), ALU.mult).then_inc(normed, 1)
            dve.wait_ge(normed, chunks)
            if chunks < NC:
                return
            for k in range(KD):
                own = dst[:, k, SEQ:T].rearrange("p (b l) -> p b l", l=LS)
                dve.tensor_tensor(own, own, A[:, k, 1:NB + 1].unsqueeze(2).to_broadcast([P, NB, LS]),
                                  ALU.mult).then_inc(sample_scaled, 1)
            for k in range(KD):
                own = dst[:, k, SEQ:T].rearrange("p (b l) -> p b l", l=LS)
                dve.wait_ge(sample_scaled, k + 1)
                dve.tensor_tensor(own, own, modT[:, shift_blk + k, 1:NB + 1].unsqueeze(2).to_broadcast([P, NB, LS]),
                                  ALU.add).then_inc(sample_done, 1)
            dve.wait_ge(sample_done, KD)


def phase_project(nc, io, tag, first_blk, hT, qk, value_rows):
    NR = len(value_rows)
    with ExitStack() as ctx:
        m = Mem(nc, ctx)
        w = m.sb("w_ring" + tag, [P, 2, KD, P])
        wr = m.sb("w_rows" + tag, [P, KD, 512 if NR else 1])
        bb = m.sb("b_blocks" + tag, [P, NBLK])
        br = m.sb("b_rows" + tag, [P, max(NR, 1), 512])
        ps = m.ps("ps_blk" + tag, [P, 2, NC, 512])
        ps_row = m.ps("ps_row" + tag, [P, 2, 512])
        b_loaded = m.sem("b_loaded" + tag)
        wr_loaded = m.sem("wr_loaded" + tag)
        w_loaded = m.sems("w_loaded" + tag, 2)
        blk_psum = m.credited_all("blk_psum" + tag, 2)
        blk_taken = m.credited_all("blk_taken" + tag, 2)
        row_psum = m.sem("row_psum" + tag)
        row_taken = m.sem("row_taken" + tag)
        block = ctx.enter_context(nc.Block())

        @block.sync
        def _(sp):
            with sp.Fori(0, 4) as i:
                for j in range(2):
                    sp.wait_ge(blk_psum[j], i + 1)
                    sp.dma_start(w[:, j, :, :], io["w_blk"][i * 2 + (first_blk + j)]).then_inc(w_loaded[j], 16)

        @block.scalar
        def _(act):
            act.dma_start(bb[:, :], io["b_blk"]).then_inc(b_loaded, 16)
            for r, (n, _) in enumerate(value_rows):
                act.dma_start(br[:, r, :], io["b_row"][n:n + 1, :].to_broadcast([P, 512])).then_inc(b_loaded, 16)
            for r, (n, _) in enumerate(value_rows):
                if r:
                    act.wait_ge(row_psum, r * NT)
                act.dma_start(wr[:, :, :], io["w_row"][n]).then_inc(wr_loaded, 16)

        @block.tensor
        def _(pe):
            with pe.Fori(0, 4) as i:
                for j in range(2):
                    pe.wait_ge(w_loaded[j], i * 16 + 16)
                    pe.wait_ge(blk_taken[j], i * NC + 1)
                    for k in range(KD):
                        for c in range(NC):
                            mm = pe.matmul(ps[:, j, c, 0:TC], w[:, j, k, :], hT[:, k, c * TC:(c + 1) * TC],
                                           start=(k == 0), stop=(k == KD - 1))
                    mm.then_inc(blk_psum[j], 1)
            for r in range(NR):
                pe.wait_ge(wr_loaded, 16 * r + 16)
                for t in range(NT):
                    if r * NT + t >= 2:
                        pe.wait_ge(row_taken, r * NT + t - 1)
                    for k in range(KD):
                        mm = pe.matmul(ps_row[:, (r * NT + t) % 2, :], hT[:, k, t * P:(t + 1) * P], wr[:, k, :],
                                       start=(k == 0), stop=(k == KD - 1))
                    mm.then_inc(row_psum, 1)

        @block.vector
        def _(dve):
            dve.wait_ge(b_loaded, 16 + 16 * NR)
            with dve.Fori(0, 4) as i:
                for j in range(2):
                    dve.wait_ge(blk_psum[j], i + 2)
                    for c in range(NC):
                        dve.tensor_scalar(qk[:, bass.ds(i * 2 + j, 1), c * TC:(c + 1) * TC].rearrange("p o t -> p (o t)"),
                                          ps[:, j, c, 0:TC], bb[:, bass.ds(i * 2 + (first_blk + j), 1)], None,
                                          ALU.add).then_inc(blk_taken[j], 1)
            for r, (_, out) in enumerate(value_rows):
                for t in range(NT):
                    dve.wait_ge(row_psum, r * NT + t + 1)
                    a, b = ps_row[:, (r * NT + t) % 2, :], br[:, r, :]
                    if len(out.shape) == 4:
                        dve.tensor_tensor(out[:, t, :, 0:BD], a.rearrange("p (h d) -> p h d", h=BH),
                                          b.rearrange("p (h d) -> p h d", h=BH), ALU.add).then_inc(row_taken, 1)
                    else:
                        dve.tensor_tensor(out[:, t, :], a, b, ALU.add).then_inc(row_taken, 1)
            for j in range(2):
                dve.wait_ge(blk_taken[j], 4 * NC + 1)
            if NR:
                dve.wait_ge(row_taken, NR * NT)


def phase_values_gates_norms(nc, io, hT, qk, gqk, va, gates, lf, negF, negFc, negFn, pair_ones):
    NQ = 8
    with ExitStack() as ctx:
        m = Mem(nc, ctx)
        wr = m.sb("w_values", [P, KD, 512])
        br = m.sb("b_values", [P, 512])
        wg = m.sb("w_gates", [P, KD, GATE_W])
        bg = m.sb("b_gates", [GATE_W, 1])
        sq = m.sb("head_sq", [P, T])
        rs = m.sb("head_rs", [P, T])
        tmp = m.sb("softplus", [GATE_W, T])
        one = m.sb("one_row", [AH, SEQ])
        ps_g = m.ps("ps_gates", [P, NC, 512])
        ps_h = m.ps("ps_head", [P, NC, 512])
        ps_v = m.ps("ps_values", [P, 2, 512])
        gate_loaded = m.sem("wg_loaded")
        value_loaded = m.sem("w_values_loaded")
        gains_loaded = m.sem("gains_loaded")
        cache_loaded = m.sem("cache_loaded")
        gate_psum, gate_taken = m.sem("gate_psum"), m.sem("gate_taken")
        abs_ready, exp_ready, ln_ready, lf_ready = (m.sem(n) for n in ("abs_ready", "exp_ready", "ln_ready", "lf_ready"))
        value_psum, value_taken = m.sem("value_psum"), m.sem("value_taken")
        squared, summed, mean_ready = m.sem("head_squared"), m.sem("head_summed"), m.sem("head_mean")
        log_ready, inv_ready, normed = m.sem("head_log"), m.sem("head_inv"), m.sem("head_normed")
        summing = m.sem("running_sums")
        stored = m.sem("new_stored")
        block = ctx.enter_context(nc.Block())

        @block.sync
        def _(sp):
            sp.dma_start(bg[:, :], io["b_gate"]).then_inc(gate_loaded, 16)
            sp.dma_start(wg[:, :, :], io["w_gate"]).then_inc(gate_loaded, 16)
            sp.dma_start(wr[:, :, :], io["w_row"][0]).then_inc(value_loaded, 16)
            sp.dma_start(br[:, :], io["b_row"][0:1, :].to_broadcast([P, 512])).then_inc(value_loaded, 16)
            sp.dma_start(gqk[:, :], io["g_qk"]).then_inc(gains_loaded, 16)
            sp.dma_start(negFc[:, :], io["cache_logfT"]).then_inc(cache_loaded, 16)
            sp.wait_ge(lf_ready, 1)
            sp.dma_start(io["new_logfT"], lf[0:AH, :]).then_inc(stored, 16)
            sp.wait_ge(value_taken, NT)
            sp.dma_start(io["new_v"], va[:, :, :]).then_inc(stored, 16)
            sp.wait_ge(normed, NQ)
            sp.dma_start(io["new_kT"], qk[:, 4:8, :]).then_inc(stored, 16)
            sp.wait_ge(stored, 48)

        @block.tensor
        def _(pe):
            pe.wait_ge(gate_loaded, 32)
            for c in range(NC):
                for k in range(KD):
                    mm = pe.matmul(ps_g[0:GATE_W, c, 0:TC], wg[:, k, :], hT[:, k, c * TC:(c + 1) * TC],
                                   start=(k == 0), stop=(k == KD - 1))
                mm.then_inc(gate_psum, 1)
            pe.wait_ge(value_loaded, 32)
            for t in range(NT):
                if t >= 2:
                    pe.wait_ge(value_taken, t - 1)
                for k in range(KD):
                    mm = pe.matmul(ps_v[:, t % 2, :], hT[:, k, t * P:(t + 1) * P], wr[:, k, :],
                                   start=(k == 0), stop=(k == KD - 1))
                mm.then_inc(value_psum, 1)
                if t < NQ:
                    pe.wait_ge(squared, t + 1)
                    if t:
                        pe.wait_ge(mean_ready, t)
                    for c in range(NC):
                        mm = pe.matmul(ps_h[:, c, 0:TC], pair_ones, sq[:, c * TC:(c + 1) * TC], start=True, stop=True)
                    mm.then_inc(summed, 1)

        @block.scalar
        def _(act):
            act.activation(sq[:, :], qk[:, 0, :], ACT.Square).then_inc(squared, 1)
            act.wait_ge(gate_taken, NC)
            act.activation(tmp[:, :], gates[:, :], ACT.Abs).then_inc(abs_ready, 1)
            act.wait_ge(abs_ready, 1)
            act.activation(tmp[:, :], tmp[:, :], ACT.Exp, scale=-1.0).then_inc(exp_ready, 1)
            act.wait_ge(exp_ready, 1)
            act.activation(tmp[:, :], tmp[:, :], ACT.Ln, bias=1.0).then_inc(ln_ready, 1)
            for b in range(NQ):
                act.wait_ge(mean_ready, b + 1)
                if b + 1 < NQ:
                    act.activation(sq[:, :], qk[:, b + 1, :], ACT.Square).then_inc(squared, 1)
                act.activation(rs[:, :], rs[:, :], ACT.Ln).then_inc(log_ready, 1)
                act.wait_ge(log_ready, b + 1)
                act.activation(rs[:, :], rs[:, :], ACT.Exp, scale=-0.5).then_inc(inv_ready, 1)

        @block.vector
        def _(dve):
            s = Steps(dve, summing)
            s.did(dve.memset(one[:, :], 1.0))
            dve.wait_ge(gate_loaded, 32)
            for c in range(NC):
                dve.wait_ge(gate_psum, c + 1)
                dve.tensor_scalar(gates[:, c * TC:(c + 1) * TC], ps_g[0:GATE_W, c, 0:TC], bg[:, :], None,
                                  ALU.add).then_inc(gate_taken, 1)
            dve.wait_ge(gains_loaded, 16)
            dve.wait_ge(cache_loaded, 16)
            for t in range(NT):
                dve.wait_ge(value_psum, t + 1)
                if t == 0:
                    dve.wait_ge(value_loaded, 32)
                dve.tensor_tensor(va[:, t, :], ps_v[:, t % 2, :], br[:, :], ALU.add).then_inc(value_taken, 1)
                if t:
                    dve.wait_ge(inv_ready, t)
                    dve.scalar_tensor_tensor(qk[:, t - 1, :], qk[:, t - 1, :], gqk[:, t - 1:t], rs[:, :],
                                             ALU.mult, ALU.mult).then_inc(normed, 1)
                if t < NQ:
                    dve.wait_ge(summed, t + 1)
                    if t:
                        dve.wait_ge(normed, t)
                    dve.tensor_scalar(rs[:, :].rearrange("p (c t) -> p c t", c=NC), ps_h[:, :, 0:TC],
                                      1.0 / AD, EPS, ALU.mult, ALU.add).then_inc(mean_ready, 1)
                    if t == 0:
                        s.settle()
                    own = slice(t * PAST, (t + 1) * PAST)
                    s.did(dve.tensor_tensor_scan(negFc[:, own], one[:, 0:PAST], negFc[:, own], 0.0, ALU.mult, ALU.subtract))
                if t == 1:
                    dve.wait_ge(ln_ready, 1)
                    dve.scalar_tensor_tensor(lf[:, :], gates[:, :], 0.0, tmp[:, :], ALU.min, ALU.subtract).then_inc(lf_ready, 1)
                if t == 2:
                    dve.wait_ge(lf_ready, 1)
                    s.did(dve.tensor_tensor_scan(negF[:, :], one[:, :], lf[0:AH, 0:SEQ], 0.0, ALU.mult, ALU.subtract))
            s.settle()
            for b in range(NB):
                s.did(dve.tensor_tensor_scan(negFn[:, b * LS:(b + 1) * LS], one[:, 0:LS],
                                             lf[0:AH, SEQ + b * LS:SEQ + (b + 1) * LS],
                                             negFc[:, (b + 1) * PAST - 1:(b + 1) * PAST], ALU.mult, ALU.subtract))
            s.settle()
            dve.wait_ge(normed, NQ)
            dve.wait_ge(value_taken, NT)


def phase_attend_prompt(nc, io, qk, va, negF, haT, ident, causal, head_rows):
    U = 2 * NPT
    BATCH = [(u % NPT) // 4 + 1 for u in range(U)]
    FIRST = [sum(BATCH[:u]) for u in range(U)]
    NBATCH = sum(BATCH)
    with ExitStack() as ctx:
        m = Mem(nc, ctx)
        qp = m.sb("q_pair", [P, SEQ])
        kp = m.sb("k_pair", [P, SEQ])
        vp = m.sb("v_pair", [P, NPT, P])
        sel = m.sb("sel_pair", [AH, 2, P])
        prob = m.sb("prob", [P, 2, SEQ])
        probT = m.sb("probT", [P, 2, 4 * P])
        nmax = m.sb("nmax", [P, 2])
        rsum = m.sb("rsum", [P, 2])
        rinv = m.sb("rinv", [P, 2])
        ps_s = m.ps("ps_s", [P, 2, 1024])
        ps_t = m.ps("ps_t", [P, 2, 512])
        ps_o = m.ps("ps_o", [P, 2, 512])
        staged_qk = m.sem("staged_qk")
        staged_v = m.sem("staged_v")
        staged_sel = m.sem("staged_sel")
        scores_ready = m.sem("scores_ready")
        nmax_ready = m.sem("nmax_ready")
        exp_done = m.sem("exp_done")
        rinv_ready = m.sem("rinv_ready")
        prob_ready = m.sem("prob_ready")
        turned = m.sem("turned")
        probT_ready = m.sem("probT_ready")
        out_ready = m.credited("out_ready")
        out_taken = m.sem("out_taken")
        block = ctx.enter_context(nc.Block())

        @block.gpsimd
        def _(pool):
            with pool.Fori(0, 4) as p:
                pool.wait_ge(out_ready, p * U + 1)
                pool.tensor_copy(sel[:, :, :], head_rows[0:AH, bass.ds(p * 2, 2), :]).then_inc(staged_sel, 1)

        @block.scalar
        def _(act):
            with act.Fori(0, 4) as p:
                act.wait_ge(out_ready, p * U + 1)
                act.activation(vp[:, :, :], va[:, 0:NPT, bass.ds(p * P, P)], ACT.Copy).then_inc(staged_v, 1)
                for u in range(U):
                    w = (u % NPT + 1) * P
                    act.wait_ge(nmax_ready, p * U + u + 1)
                    if u >= 2:
                        act.wait_ge(out_ready, p * U + u)
                    act.activation(prob[:, u % 2, 0:w], ps_s[:, u % 2, 0:w], ACT.Exp, bias=nmax[:, u % 2:u % 2 + 1],
                                   accum_out=rsum[:, u % 2:u % 2 + 1]).then_inc(exp_done, 1)
                    act.wait_ge(rinv_ready, p * U + u + 1)
                    act.activation(prob[:, u % 2, 0:w], prob[:, u % 2, 0:w], ACT.Copy,
                                   scale=rinv[:, u % 2:u % 2 + 1]).then_inc(prob_ready, 1)

        @block.tensor
        def _(pe):
            with pe.Fori(0, 4) as p:
                def scores(u):
                    hh, t = divmod(u, NPT)
                    if u >= 2:
                        pe.wait_ge(exp_done, p * U + u - 1)
                    rows = slice(hh * AD, (hh + 1) * AD)
                    for lo in range(0, (t + 1) * P, 512):
                        n = min(512, (t + 1) * P - lo)
                        last = lo + n == (t + 1) * P
                        pe.matmul(ps_s[:, u % 2, lo:lo + n], qp[rows, t * P:(t + 1) * P], kp[rows, lo:lo + n],
                                  start=True, stop=False)
                        mm = pe.matmul(ps_s[:, u % 2, lo:lo + n], sel[:, hh, :], negF[:, lo:lo + n],
                                       start=False, stop=not last)
                    mm = pe.matmul(ps_s[:, u % 2, t * P:(t + 1) * P], ident, causal, start=False, stop=True)
                    mm.then_inc(scores_ready, 1)

                pe.wait_ge(staged_qk, p * 2 + 2)
                pe.wait_ge(staged_sel, p + 1)
                pe.wait_ge(staged_v, p + 1)
                scores(0)
                for u in range(U):
                    if u + 1 < U:
                        scores(u + 1)
                    hh, t = divmod(u, NPT)
                    pe.wait_ge(prob_ready, p * U + u + 1)
                    for e in range(BATCH[u]):
                        g = FIRST[u] + e
                        if g >= 2:
                            pe.wait_ge(probT_ready, p * NBATCH + g - 1)
                        for k in range(4 * e, min(4 * e + 4, t + 1)):
                            mm = pe.transpose(ps_t[:, g % 2, (k % 4) * P:(k % 4 + 1) * P],
                                              prob[:, u % 2, k * P:(k + 1) * P], ident)
                        mm.then_inc(turned, 1)
                    if u >= 2:
                        pe.wait_ge(out_taken, p * U + u - 1)
                    for e in range(BATCH[u]):
                        g = FIRST[u] + e
                        pe.wait_ge(probT_ready, p * NBATCH + g + 1)
                        for k in range(4 * e, min(4 * e + 4, t + 1)):
                            mm = pe.matmul(ps_o[hh * AD:(hh + 1) * AD, u % 2, 0:P], vp[:, k, hh * AD:(hh + 1) * AD],
                                           probT[:, g % 2, (k % 4) * P:(k % 4 + 1) * P],
                                           start=(k == 0), stop=(k == t))
                    mm.then_inc(out_ready, 1)

        @block.vector
        def _(dve):
            with dve.Fori(0, 4) as p:
                dve.wait_ge(out_ready, p * U + 1)
                blk = lambda first: qk[:, bass.ds(p + first, 1), 0:SEQ].rearrange("p o t -> p (o t)")
                dve.tensor_scalar(qp[:, :], blk(0), AD ** -0.5, None, ALU.mult).then_inc(staged_qk, 1)
                dve.tensor_copy(kp[:, :], blk(4)).then_inc(staged_qk, 1)

                def row_max(u):
                    dve.wait_ge(scores_ready, p * U + u + 1)
                    dve.tensor_reduce(nmax[:, u % 2:u % 2 + 1], ps_s[:, u % 2, 0:(u % NPT + 1) * P], AX.X, ALU.max,
                                      negate=True).then_inc(nmax_ready, 1)

                row_max(0)
                for u in range(U):
                    hh, t = divmod(u, NPT)
                    dve.wait_ge(exp_done, p * U + u + 1)
                    dve.reciprocal(rinv[:, u % 2:u % 2 + 1], rsum[:, u % 2:u % 2 + 1]).then_inc(rinv_ready, 1)
                    if u + 1 < U:
                        row_max(u + 1)
                    for e in range(BATCH[u]):
                        g = FIRST[u] + e
                        n = min(4, t + 1 - 4 * e) * P
                        dve.wait_ge(turned, p * NBATCH + g + 1)
                        dve.tensor_copy(probT[:, g % 2, 0:n], ps_t[:, g % 2, 0:n]).then_inc(probT_ready, 1)
                    dve.wait_ge(out_ready, p * U + u + 2)
                    rows = slice(hh * AD, (hh + 1) * AD)
                    dve.tensor_copy(haT[rows, bass.ds(p, 1), t * P:(t + 1) * P].rearrange("p o t -> p (o t)"),
                                    ps_o[rows, u % 2, 0:P]).then_inc(out_taken, 1)
            dve.wait_ge(out_taken, 4 * U)


def phase_attend_streams(nc, io, qk, va, negFc, negFn, haT, spare, ident, stream_rows):
    W = PAST + P
    NP = AH // 2
    with ExitStack() as ctx:
        m = Mem(nc, ctx)
        masks = m.sb("stream_masks", [P, NB, P])
        kc = spare[:, 0:2 * NP * PAST].rearrange("p (j n t) -> p j n t", j=2, n=NP)
        vc = m.sb("v_cache", [P, 2, PAST // P, AH * AD])
        qbd = m.sb("q_diag", [P, 2, 4 * (P + 2 * LS)])
        prob = m.sb("prob_s", [P, 2, W])
        probT = m.sb("probT_s", [P, 5, P])
        nmax = m.sb("nmax_s", [P, 2])
        rsum = m.sb("rsum_s", [P, 2])
        rinv = m.sb("rinv_s", [P, 2])
        ps_s = m.ps("ps_ss", [P, 2, 1024])
        ps_t = m.ps("ps_ts", [P, 5 * P])
        ps_o = m.ps("ps_os", [P, 4, 2 * LS])
        zeroed = m.sem("zeroed")
        masks_loaded = m.sem("masks_loaded")
        k_loaded = m.sems("k_loaded", 2)
        v_loaded = m.sems("v_loaded", 2)
        q_placed = m.sems("q_placed", 2)
        scores_ready = m.credited("s_scores_ready")
        nmax_ready = m.sem("s_nmax_ready")
        exp_done = m.credited("s_exp_done")
        rinv_ready = m.sem("s_rinv_ready")
        prob_ready = m.sem("s_prob_ready")
        turned = m.credited("s_turned")
        probT_ready = m.credited("s_probT_ready")
        out_ready = m.credited("s_out_ready")
        out_taken = m.credited("s_out_taken")
        block = ctx.enter_context(nc.Block())

        @block.sync
        def _(sp):
            sp.dma_start(masks[:, :, :], io["stream_masks"]).then_inc(masks_loaded, 16)
            for j in range(2):
                sp.dma_start(kc[:, j, :, :], io["cache_kT"][j]).then_inc(k_loaded[j], 16)
                sp.dma_start(vc[:, j, :, :], io["cache_v"][j]).then_inc(v_loaded[j], 16)
            with sp.Fori(0, NB // 2 - 1) as i:
                for j in range(2):
                    sp.wait_ge(scores_ready, i * 2 + (j + 2))
                    sp.dma_start(kc[:, j, :, :], io["cache_kT"][i * 2 + (j + 2)]).then_inc(k_loaded[j], 16)
                    sp.wait_ge(out_ready, i * 2 + (j + 2))
                    sp.dma_start(vc[:, j, :, :], io["cache_v"][i * 2 + (j + 2)]).then_inc(v_loaded[j], 16)

        @block.gpsimd
        def _(pool):
            pool.memset(qbd[:, :, :], 0.0).then_inc(zeroed, 1)

        @block.scalar
        def _(act):
            with act.Fori(0, NB // 2) as i:
                for j in range(2):
                    act.wait_ge(nmax_ready, i * 2 + (j + 1))
                    act.wait_ge(turned, i * 2 + (j + 1))
                    act.activation(prob[:, j, :], ps_s[:, j, 0:W], ACT.Exp, bias=nmax[:, j:j + 1],
                                   accum_out=rsum[:, j:j + 1]).then_inc(exp_done, 1)

        @block.tensor
        def _(pe):
            def scores(i, j, slot_new=False):
                b = i * 2 + j
                pe.wait_ge(k_loaded[j], i * 16 + 16)
                pe.wait_ge(q_placed[j], i * 2 + 2)
                if not slot_new:
                    pe.wait_ge(exp_done, i * 2 + j)
                for n in range(NP):
                    pe.matmul(ps_s[:, j, 0:PAST], qbd[:, j, n * P:(n + 1) * P], kc[:, j, n, :], start=(n == 0), stop=False)
                pe.matmul(ps_s[:, j, 0:PAST], stream_rows[0:AH, :], negFc[:, bass.ds(b * PAST, PAST)], start=False, stop=True)
                for n in range(NP):
                    pe.matmul(ps_s[:, j, PAST:W], qbd[:, j, n * P:(n + 1) * P], qk[:, 4 + n, SEQ:T], start=(n == 0), stop=False)
                pe.matmul(ps_s[:, j, PAST:W], stream_rows[0:AH, :], negFn[:, :], start=False, stop=False)
                pe.matmul(ps_s[:, j, PAST:W], ident, masks[:, bass.ds(b, 1), :].rearrange("p o t -> p (o t)"),
                          start=False, stop=True).then_inc(scores_ready, 1)

            def values(i, j):
                pe.wait_ge(prob_ready, i * 2 + (j + 1))
                pe.wait_ge(probT_ready, i * 2 + (j + 1))
                for k in range(5):
                    mm = pe.transpose(ps_t[:, k * P:(k + 1) * P], prob[:, j, k * P:(k + 1) * P], ident)
                mm.then_inc(turned, 1)
                pe.wait_ge(v_loaded[j], i * 16 + 16)
                pe.wait_ge(probT_ready, i * 2 + (j + 2))
                pe.wait_ge(out_taken, i * 4 + (2 * j + 1))
                for n in range(NP):
                    for k in range(5):
                        v = vc[:, j, k, n * P:(n + 1) * P] if k < 4 else va[:, NT - 1, n * P:(n + 1) * P]
                        mm = pe.matmul(ps_o[:, n, :], v, probT[:, k, n * 2 * LS:(n + 1) * 2 * LS],
                                       start=(k == 0), stop=(k == 4))
                mm.then_inc(out_ready, 1)

            pe.wait_ge(masks_loaded, 16)
            scores(0, 0, True)
            with pe.Fori(0, NB // 2 - 1) as i:
                scores(i, 1)
                values(i, 0)
                scores(i + 1, 0)
                values(i, 1)
            scores(NB // 2 - 1, 1)
            values(NB // 2 - 1, 0)
            values(NB // 2 - 1, 1)

        @block.vector
        def _(dve):
            def place_q(i, j):
                for hh in range(2):
                    rows = slice(hh * AD, (hh + 1) * AD)
                    dve.tensor_scalar(qbd[rows, j, :].rearrange("p (n c) -> p n c", n=NP)[:, :, hh * LS:(hh + 1) * LS],
                                      qk[rows, 0:NP, bass.ds(i * (2 * LS) + (j * LS + SEQ), LS)], AD ** -0.5, None,
                                      ALU.mult).then_inc(q_placed[j], 1)

            def stream(i, j, more):
                dve.wait_ge(scores_ready, i * 2 + (j + 2))
                dve.tensor_reduce(nmax[:, j:j + 1], ps_s[:, j, 0:W], AX.X, ALU.max, negate=True).then_inc(nmax_ready, 1)
                dve.wait_ge(exp_done, i * 2 + (j + 2))
                dve.reciprocal(rinv[:, j:j + 1], rsum[:, j:j + 1]).then_inc(rinv_ready, 1)
                dve.wait_ge(rinv_ready, i * 2 + (j + 1))
                dve.tensor_scalar(prob[:, j, :], prob[:, j, :], rinv[:, j:j + 1], None, ALU.mult).then_inc(prob_ready, 1)
                if more:
                    place_q(i + 1, j)
                dve.wait_ge(turned, i * 2 + (j + 2))
                dve.tensor_copy(probT[:, :, :], ps_t[:, :].rearrange("p (k t) -> p k t", k=5)).then_inc(probT_ready, 1)
                dve.wait_ge(out_ready, i * 2 + (j + 2))
                for hh in range(2):
                    rows = slice(hh * AD, (hh + 1) * AD)
                    dve.tensor_copy(haT[rows, :, bass.ds(i * (2 * LS) + (j * LS + SEQ), LS)],
                                    ps_o[rows, :, hh * LS:(hh + 1) * LS]).then_inc(out_taken, 1)

            dve.wait_ge(zeroed, 1)
            for j in range(2):
                place_q(0, j)
            with dve.Fori(0, NB // 2 - 1) as i:
                for j in range(2):
                    stream(i, j, True)
            for j in range(2):
                stream(NB // 2 - 1, j, False)
            dve.wait_ge(out_taken, 2 * NB + 1)


def phase_mlstm_rows(nc, io, gates, lf, rows, cols):
    with ExitStack() as ctx:
        m = Mem(nc, ctx)
        scan_rows = m.sb("scan_rows", [BH, 2, T])
        m0s = m.sb("m0_streams", [BH, NB])
        small = lambda name: m.sb(name, [BH, T])
        lf4, u, start, d1, b, M, neg_m, u_end = (small("row_" + n) for n in ("lf", "u", "d0", "d1", "b", "M", "nm", "ue"))
        m0p = m.sb("m0_prompt", [BH, NPT])
        m_out = m.sb("m_out", [BH, NB + 1])
        ident = m.sb("ident4", [BH, BH])
        ps = m.ps("ps_cols", [P, NT, 3, BH])
        loaded = m.sem("rows_loaded")
        done = m.sem("rows_done")
        rows_ready = m.sem("rows_ready")
        turned = m.sem("cols_turned")
        cols_ready = m.sem("cols_ready")
        m_ready = m.sem("m_ready")
        stored = m.sem("m_stored")
        block = ctx.enter_context(nc.Block())
        chunks = lambda a: a[:, 0:SEQ].rearrange("p (c t) -> p c t", t=P)
        streams = lambda a: a[:, SEQ:T].rearrange("p (c t) -> p c t", t=LS)

        @block.sync
        def _(sp):
            sp.dma_start(scan_rows[:, :, :], io["scan_rows"]).then_inc(loaded, 16)
            sp.dma_start(m0s[:, :], io["state_mT"]).then_inc(loaded, 16)
            sp.dma_start(ident[:, :], io["consts"][0:BH, 0:BH]).then_inc(loaded, 16)
            sp.wait_ge(m_ready, 2)
            sp.dma_start(io["new_mT"], m_out[:, :]).then_inc(stored, 16)
            sp.wait_ge(stored, 16)

        @block.vector
        def _(dve):
            s = Steps(dve, done)
            s.did(dve.tensor_copy(lf4[:, :], lf[GATE_LF:GATE_LF + BH, :]))
            s.did(dve.tensor_copy(u[:, :], gates[GATE_I:GATE_I + BH, :]))
            s.did(dve.memset(m0p[:, 0:1], 0.0))
            dve.wait_ge(loaded, 48)
            s.settle()
            s.did(dve.tensor_tensor_scan(b[:, :], scan_rows[:, 0, :], lf4[:, :], 0.0, ALU.mult, ALU.add))
            s.settle()
            s.did(dve.tensor_tensor(u[:, :], u[:, :], b[:, :], ALU.subtract))
            s.did(dve.tensor_copy(start[:, :], scan_rows[:, 1, :]))
            s.settle()
            s.did(dve.tensor_copy(chunks(start)[:, 1:NPT, 0:1], chunks(b)[:, 0:NPT - 1, P - 1:P]))
            s.did(dve.tensor_copy(d1[:, :], u[:, :]))
            s.settle()
            s.did(dve.tensor_tensor(streams(d1)[:, :, 0:1], streams(u)[:, :, 0:1], m0s[:, :].unsqueeze(2), ALU.max))
            s.settle()
            s.did(dve.tensor_tensor_scan(M[:, :], start[:, :], d1[:, :], 0.0, ALU.add, ALU.max))
            s.settle()
            s.did(dve.scalar_tensor_tensor(neg_m[:, :], b[:, :], -1.0, M[:, :], ALU.mult, ALU.subtract))
            s.did(dve.tensor_scalar(rows[:, 0, :], M[:, :], -1.0, None, ALU.mult))
            s.did(dve.tensor_tensor(chunks(u_end), chunks(u), chunks(M)[:, :, P - 1:P].to_broadcast([BH, NPT, P]), ALU.subtract))
            s.did(dve.tensor_tensor(streams(u_end), streams(u), streams(M)[:, :, LS - 1:LS].to_broadcast([BH, NB, LS]), ALU.subtract))
            s.settle()
            s.did(dve.tensor_scalar(m0p[:, 1:NPT].unsqueeze(2), chunks(neg_m)[:, 0:NPT - 1, P - 1:P], -1.0, None, ALU.mult))
            dve.tensor_scalar(m_out[:, 0:1], neg_m[:, SEQ - 1:SEQ], -1.0, None, ALU.mult).then_inc(m_ready, 1)
            dve.tensor_scalar(m_out[:, 1:NB + 1].unsqueeze(2), streams(neg_m)[:, :, LS - 1:LS], -1.0, None, ALU.mult).then_inc(m_ready, 1)
            s.settle()
            s.did(dve.tensor_tensor(chunks(rows[:, 1, :]), m0p[:, :].unsqueeze(2).to_broadcast([BH, NPT, P]), chunks(M), ALU.subtract))
            s.did(dve.tensor_tensor(streams(rows[:, 1, :]), m0s[:, :].unsqueeze(2).to_broadcast([BH, NB, LS]), streams(M), ALU.subtract))
            s.settle()
            dve.wait_ge(m_ready, 2)
            dve.engine_nop().then_inc(rows_ready, 1)
            dve.wait_ge(cols_ready, 2)
            dve.tensor_copy(cols[:, 0, :, :], ps[:, :, 0, :]).then_inc(cols_ready, 1)
            dve.wait_ge(cols_ready, 3)

        @block.tensor
        def _(pe):
            pe.wait_ge(rows_ready, 1)
            for t in range(NT):
                for n, a in enumerate((u, u_end, neg_m)):
                    mm = pe.transpose(ps[:, t, n, :], a[:, t * P:(t + 1) * P], ident[:, :])
            mm.then_inc(turned, 1)

        @block.scalar
        def _(act):
            act.wait_ge(turned, 1)
            for n in (1, 2):
                act.activation(cols[:, n, :, :], ps[:, :, n, :], ACT.Exp).then_inc(cols_ready, 1)


def phase_ones(nc, vb):
    with ExitStack() as ctx:
        done = Mem(nc, ctx).sem("ones_set")
        block = ctx.enter_context(nc.Block())

        @block.vector
        def _(dve):
            dve.memset(vb[:, :, :, BD:BD + 1], 1.0).then_inc(done, 1)
            dve.wait_ge(done, 1)


def phase_mlstm(nc, io, qk, kb, vb, rows, cols, hbT, ident, causalT, head_rows):
    V1 = BD + 1
    KS = BD ** -0.5
    B3 = lambda b: (b // 3, (b % 3) * V1)
    with ExitStack() as ctx:
        m = Mem(nc, ctx)
        kT = m.sb("kT_head", [P, T])
        sel = m.sb("sel_head", [BH, P])
        smT = m.sb("stream_maskT", [P, P])
        own = m.sb("own_stream", [P, NB, P])
        own_rows = m.sb("own_rows", [P, NB])
        ghb = m.sb("g_hb", [P, BH])
        C = m.sb("state", [P, V1])
        Cs = m.sb("state_streams", [P, NB, V1])
        wT = m.sb("wT", [P, 2, P])
        aT = m.sb("aT", [P, 2, P])
        wsT = m.sb("wsT", [P, 2, P])
        qa = m.sb("qa", [P, 2, P])
        kw = m.sb("kw", [P, 2, P])
        qm = m.sb("q_streams", [P, NB, P])
        kwm = m.sb("kw_streams", [P, NB, P])
        hb = m.sb("h_rows", [P, NT, V1])
        sq = kT[:, :].rearrange("p (t d) -> p t d", d=BD)
        den = m.sb("den", [P, NT])
        inv = m.sb("inv", [P, NT])
        ps_a = m.ps("ps_a", [P, 2, 512])
        ps_n = m.ps("ps_n", [P, 2, 512])
        ps_u = m.ps("ps_u", [P, 3, 512])
        ps_h = m.ps("ps_h", [P, 512])
        consts_loaded = m.sem("m_consts_loaded")
        cs_loaded = m.sem("cs_loaded")
        staged = m.sem("m_staged")
        a_ready = m.credited("a_ready")
        w_ready = m.sem("w_ready")
        at_ready = m.sem("at_ready")
        ws_ready = m.sem("ws_ready")
        qa_ready = m.sem("qa_ready")
        kw_ready = m.sem("kw_ready")
        num_ready = m.sem("num_ready")
        num_taken = m.sem("num_taken")
        upd_ready = m.sem("upd_ready")
        state_ready = m.sem("state_ready")
        cs_ready = m.sem("cs_ready")
        dve_done = m.sem("m_dve_done")
        h_scaled = m.sem("h_scaled")
        h_squared = m.sem("h_squared")
        h_summed = m.sem("h_summed")
        mean_ready = m.sem("h_mean")
        log_ready = m.sem("h_log")
        inv_ready = m.sem("h_inv")
        h_normed = m.sem("h_normed")
        h_turned = m.sem("h_turned")
        hb_ready = m.sem("hb_ready")
        stored = m.credited("state_stored")
        block = ctx.enter_context(nc.Block())
        head = lambda a, h: a[:, bass.ds(h, 1), :].rearrange("p o t -> p (o t)")
        q_of = lambda h, tok: head(qk[:, :, tok], h)
        DONE = 5

        @block.sync
        def _(sp):
            sp.dma_start(smT[:, :], io["stream_maskT"]).then_inc(consts_loaded, 16)
            sp.dma_start(own[:, :, :], io["own_stream"]).then_inc(consts_loaded, 16)
            sp.dma_start(own_rows[:, :], io["own_rows"]).then_inc(consts_loaded, 16)
            sp.dma_start(ghb[:, :], io["g_hbT"]).then_inc(consts_loaded, 16)
            with sp.Fori(0, BH) as h:
                sp.wait_ge(stored, h * 32 + 1)
                sp.dma_start(Cs[:, :, :], io["state_C"][h]).then_inc(cs_loaded, 16)
                sp.wait_ge(state_ready, h * NPT + NPT)
                sp.dma_start(io["new_C_prompt"][h], C[:, :]).then_inc(stored, 16)
                sp.wait_ge(cs_ready, h * NB + NB)
                sp.dma_start(io["new_C_sample"][h], Cs[:, :, :]).then_inc(stored, 16)
            sp.wait_ge(stored, BH * 32 + 1)

        @block.gpsimd
        def _(pool):
            with pool.Fori(0, BH) as h:
                pool.wait_ge(a_ready, h * NT + 1)
                pool.tensor_copy(sel[:, :], head(head_rows[0:BH], h)).then_inc(staged, 1)

        @block.scalar
        def _(act):
            with act.Fori(0, BH) as h:
                for t in range(NT):
                    act.wait_ge(a_ready, h * NT + t + 2)
                    if t >= 2:
                        act.wait_ge(ws_ready, h * NT + t - 1)
                    act.activation(wT[:, t % 2, :], ps_a[:, t % 2, 0:P], ACT.Exp,
                                   bias=cols[:, 0, t, bass.ds(h, 1)]).then_inc(w_ready, 1)
                    if t >= 2:
                        act.wait_ge(state_ready, h * NPT + t - 1)
                    act.activation(aT[:, t % 2, :], ps_a[:, t % 2, P:2 * P], ACT.Exp).then_inc(at_ready, 1)
                    if t >= 1:
                        act.wait_ge(num_ready, h * NT + t)
                        act.activation(hb[:, t - 1, :], ps_n[:, (t - 1) % 2, 0:V1], ACT.Copy).then_inc(num_taken, 1)
                act.wait_ge(num_ready, h * NT + NT)
                act.activation(hb[:, NT - 1, :], ps_n[:, (NT - 1) % 2, 0:V1], ACT.Copy).then_inc(num_taken, 1)
                act.wait_ge(h_scaled, h + 1)
                act.activation(sq, hb[:, :, 0:BD], ACT.Square).then_inc(h_squared, 1)
                act.wait_ge(mean_ready, h + 1)
                act.activation(inv[:, :], inv[:, :], ACT.Ln).then_inc(log_ready, 1)
                act.wait_ge(log_ready, h + 1)
                act.activation(inv[:, :], inv[:, :], ACT.Exp, scale=-0.5).then_inc(inv_ready, 1)

        @block.tensor
        def _(pe):
            pe.wait_ge(consts_loaded, 64)
            with pe.Fori(0, BH) as h:
                def scores(t):
                    tok = slice(t * P, (t + 1) * P)
                    if t >= 2:
                        pe.wait_ge(at_ready, h * NT + t - 1)
                        pe.wait_ge(ws_ready, h * NT + t - 1)
                    pe.matmul(ps_a[:, t % 2, 0:P], sel[:, :], rows[:, 0, tok], start=True, stop=False)
                    pe.matmul(ps_a[:, t % 2, 0:P], ident, causalT if t < NPT else smT[:, :], start=False, stop=True)
                    pe.matmul(ps_a[:, t % 2, P:2 * P], sel[:, :], rows[:, 1, tok], start=True, stop=True)
                    pe.matmul(ps_a[:, t % 2, 2 * P:3 * P], kT[:, tok], q_of(h, tok), start=True, stop=True).then_inc(a_ready, 1)

                pe.wait_ge(staged, h * 3 + 3)
                scores(0)
                for t in range(NT):
                    if t + 1 < NT:
                        scores(t + 1)
                    v = head(vb[:, t], h)
                    pe.wait_ge(kw_ready, h * NT + t + 1)
                    if t < NPT:
                        if t >= 2:
                            pe.wait_ge(state_ready, h * NPT + t - 1)
                        pe.matmul(ps_u[:, t % 2, 0:V1], kw[:, t % 2, :], v, start=True, stop=True).then_inc(upd_ready, 1)
                    else:
                        pe.wait_ge(state_ready, h * NPT + NPT)
                        for b in range(NB):
                            bank, at = B3(b)
                            mm = pe.matmul(ps_u[:, bank, at:at + V1], kwm[:, b, :], v, start=True, stop=True)
                        mm.then_inc(upd_ready, 1)
                    pe.wait_ge(ws_ready, h * NT + t + 1)
                    pe.wait_ge(qa_ready, h * NT + t + 1)
                    if t >= 2:
                        pe.wait_ge(num_taken, h * NT + t - 1)
                    pe.matmul(ps_n[:, t % 2, 0:V1], wsT[:, t % 2, :], v, start=True, stop=False)
                    if t < NPT:
                        if t >= 1:
                            pe.wait_ge(state_ready, h * NPT + t)
                        mm = pe.matmul(ps_n[:, t % 2, 0:V1], qa[:, t % 2, :], C[:, :], start=False, stop=True)
                    else:
                        pe.wait_ge(cs_loaded, h * 16 + 16)
                        for b in range(NB):
                            mm = pe.matmul(ps_n[:, t % 2, 0:V1], qm[:, b, :], Cs[:, b, :], start=False, stop=(b == NB - 1))
                    mm.then_inc(num_ready, 1)
                pe.wait_ge(h_normed, h + 1)
                for e, (lo, hi) in enumerate(((0, 4), (4, 8), (8, 9))):
                    if e:
                        pe.wait_ge(hb_ready, h * 3 + e)
                    for t in range(lo, hi):
                        mm = pe.transpose(ps_h[:, (t - lo) * P:(t - lo + 1) * P], hb[:, t, 0:BD], ident)
                    mm.then_inc(h_turned, 1)

        @block.vector
        def _(dve):
            dve.wait_ge(consts_loaded, 64)
            with dve.Fori(0, BH) as h:
                s = Steps(dve, dve_done, h * DONE)
                dve.wait_ge(a_ready, h * NT + 1)
                dve.tensor_scalar(kT[:, :], head(qk, h + BH), KS, None, ALU.mult).then_inc(staged, 1)
                dve.wait_ge(stored, h * 32 + 1)
                dve.memset(C[:, :], 0.0).then_inc(staged, 1)
                for t in range(NT):
                    if t >= 2:
                        dve.wait_ge(upd_ready, h * NT + t - 1)
                        dve.wait_ge(num_ready, h * NT + t - 1)
                    dve.tensor_scalar(kw[:, t % 2, :], kb[:, t, bass.ds(h * BD, BD)], cols[:, 1, t, bass.ds(h, 1)], KS,
                                      ALU.mult, ALU.mult).then_inc(kw_ready if t < NPT else dve_done, 1)
                    if t == NT - 1:
                        s.n += 1
                        s.settle()
                        dve.tensor_tensor(kwm[:, :, :], kw[:, t % 2, :].unsqueeze(1).to_broadcast([P, NB, P]),
                                          own_rows[:, :].unsqueeze(2).to_broadcast([P, NB, P]), ALU.mult).then_inc(kw_ready, 1)
                    dve.wait_ge(w_ready, h * NT + t + 1)
                    dve.wait_ge(at_ready, h * NT + t + 1)
                    dve.tensor_tensor(wsT[:, t % 2, :], wT[:, t % 2, :], ps_a[:, t % 2, 2 * P:3 * P], ALU.mult).then_inc(ws_ready, 1)
                    dve.tensor_tensor(qa[:, t % 2, :], q_of(h, slice(t * P, (t + 1) * P)), aT[:, t % 2, :],
                                      ALU.mult).then_inc(qa_ready if t < NPT else dve_done, 1)
                    if t == NT - 1:
                        s.n += 1
                        s.settle()
                        dve.tensor_tensor(qm[:, :, :], qa[:, t % 2, :].unsqueeze(1).to_broadcast([P, NB, P]), own[:, :, :],
                                          ALU.mult).then_inc(qa_ready, 1)
                    dve.wait_ge(upd_ready, h * NT + t + 1)
                    dve.wait_ge(num_ready, h * NT + t + 1)
                    if t < NPT:
                        dve.scalar_tensor_tensor(C[:, :], C[:, :], aT[:, t % 2, P - 1:P], ps_u[:, t % 2, 0:V1],
                                                 ALU.mult, ALU.add).then_inc(state_ready, 1)
                        dve.wait_ge(state_ready, h * NPT + t + 1)
                    else:
                        for b in range(NB):
                            bank, at = B3(b)
                            dve.scalar_tensor_tensor(Cs[:, b, :], Cs[:, b, :], aT[:, t % 2, (b + 1) * LS - 1:(b + 1) * LS],
                                                     ps_u[:, bank, at:at + V1], ALU.mult, ALU.add).then_inc(cs_ready, 1)
                dve.wait_ge(num_taken, h * NT + NT)
                s.did(dve.scalar_tensor_tensor(den[:, :], hb[:, :, BD:V1].rearrange("p t o -> p (t o)"), -1.0,
                                               hb[:, :, BD:V1].rearrange("p t o -> p (t o)"), ALU.mult, ALU.max))
                s.settle()
                s.did(dve.tensor_tensor(den[:, :], den[:, :], cols[:, 2, :, bass.ds(h, 1)].rearrange("p t o -> p (t o)"), ALU.max))
                s.settle()
                s.did(dve.reciprocal(den[:, :], den[:, :]))
                s.settle()
                assert s.n == DONE
                dve.tensor_tensor(hb[:, :, 0:BD], hb[:, :, 0:BD], den[:, :].unsqueeze(2).to_broadcast([P, NT, BD]),
                                  ALU.mult).then_inc(h_scaled, 1)
                dve.wait_ge(h_squared, h + 1)
                dve.tensor_reduce(den[:, :], sq, AX.X, ALU.add).then_inc(h_summed, 1)
                dve.wait_ge(h_summed, h + 1)
                dve.tensor_scalar(inv[:, :], den[:, :], 1.0 / BD, EPS, ALU.mult, ALU.add).then_inc(mean_ready, 1)
                dve.wait_ge(inv_ready, h + 1)
                dve.tensor_tensor(hb[:, :, 0:BD], hb[:, :, 0:BD], inv[:, :].unsqueeze(2).to_broadcast([P, NT, BD]),
                                  ALU.mult).then_inc(h_normed, 1)
                for e, (lo, hi) in enumerate(((0, 4), (4, 8), (8, 9))):
                    dve.wait_ge(h_turned, h * 3 + e + 1)
                    dve.tensor_scalar(head(hbT[:, :, lo * P:hi * P], h), ps_h[:, 0:(hi - lo) * P],
                                      ghb[:, bass.ds(h, 1)], None, ALU.mult).then_inc(hb_ready, 1)
            dve.wait_ge(hb_ready, BH * 3)
            dve.wait_ge(cs_ready, BH * NB)


def phase_merge(nc, io, hT, haT, hbT, mT):
    with ExitStack() as ctx:
        m = Mem(nc, ctx)
        w = m.sb("w_gate_ring", [P, 2, KD, P])
        wp = m.sb("w_branch_ring", [P, 2, 4, P])
        bb = m.sb("b_blocks2", [P, NBLK])
        sg = m.sb("sig_ring", [P, 2, T])
        pr = m.sb("gated", [P, TC])
        ps_g = m.ps("ps_gate", [P, 2, NC, 512])
        ps_p = m.ps("ps_branch", [P, 2, 512])
        b_loaded = m.sem("b2_loaded")
        w_loaded = m.sems("wg_loaded", 2)
        wp_loaded = m.sems("wp_loaded", 2)
        gate_psum = m.credited_all("gate_psum2", 2)
        sig_ready = m.credited_all("sig_ready", 2)
        branch_psum = m.credited_all("branch_psum", 2)
        used = m.credited_all("gates_used", 2)
        merged = m.credited("merged")
        block = ctx.enter_context(nc.Block())
        BO = 2

        @block.sync
        def _(sp):
            sp.dma_start(bb[:, :], io["b_blk"]).then_inc(b_loaded, 16)
            with sp.Fori(0, BO) as i:
                for j in range(2):
                    sp.wait_ge(gate_psum[j], i + 1)
                    sp.dma_start(w[:, j, :, :], io["w_blk"][i * 2 + (BLK_BO + j)]).then_inc(w_loaded[j], 16)
            with sp.Fori(0, KD) as i:
                for j, (blk, wname) in enumerate(((BLK_GA, "w_paT"), (BLK_GB, "w_pbT"))):
                    sp.wait_ge(gate_psum[j], i + (BO + 1))
                    sp.dma_start(w[:, j, :, :], io["w_blk"][i + blk]).then_inc(w_loaded[j], 16)
                    sp.wait_ge(branch_psum[j], i + 1)
                    sp.dma_start(wp[:, j, :, :], io[wname][i]).then_inc(wp_loaded[j], 16)

        @block.tensor
        def _(pe):
            def gate(j, chunks):
                for k in range(KD):
                    for c in range(chunks):
                        mm = pe.matmul(ps_g[:, j, c, 0:TC], w[:, j, k, :], hT[:, k, c * TC:(c + 1) * TC],
                                       start=(k == 0), stop=(k == KD - 1))
                mm.then_inc(gate_psum[j], 1)

            with pe.Fori(0, BO) as i:
                for j in range(2):
                    pe.wait_ge(w_loaded[j], i * 16 + 16)
                    pe.wait_ge(sig_ready[j], i * NC + 1)
                    gate(j, NC)
            for j in range(2):
                pe.wait_ge(used[j], BO + 1)
            with pe.Fori(0, KD) as i:
                for j, src in enumerate((haT, hbT)):
                    pe.wait_ge(w_loaded[j], i * 16 + 16 * (BO + 1))
                    pe.wait_ge(sig_ready[j], i + (BO * NC + 1))
                    gate(j, 1)
                    pe.wait_ge(wp_loaded[j], i * 16 + 16)
                    pe.wait_ge(used[j], i + (BO + 1))
                    for k in range(4):
                        mm = pe.matmul(ps_p[:, j, 0:TC], wp[:, j, k, :], src[:, k, 0:TC], start=(k == 0), stop=(k == 3))
                    mm.then_inc(branch_psum[j], 1)

        @block.scalar
        def _(act):
            act.wait_ge(b_loaded, 16)
            with act.Fori(0, BO) as i:
                for j in range(2):
                    act.wait_ge(gate_psum[j], i + 2)
                    act.wait_ge(used[j], i + 1)
                    for c in range(NC):
                        act.activation(sg[:, j, c * TC:(c + 1) * TC], ps_g[:, j, c, 0:TC], ACT.Sigmoid,
                                       bias=bb[:, bass.ds(i * 2 + (BLK_BO + j), 1)]).then_inc(sig_ready[j], 1)
            with act.Fori(0, KD) as i:
                for j, blk in enumerate((BLK_GA, BLK_GB)):
                    act.wait_ge(gate_psum[j], i + (BO + 2))
                    act.wait_ge(used[j], i + (BO + 1))
                    act.activation(sg[:, j, 0:TC], ps_g[:, j, 0, 0:TC], ACT.Sigmoid,
                                   bias=bb[:, bass.ds(i + blk, 1)]).then_inc(sig_ready[j], 1)

        @block.vector
        def _(dve):
            with dve.Fori(0, BO) as i:
                for j in range(2):
                    dve.wait_ge(sig_ready[j], i * NC + (NC + 1))
                    own = hbT[:, bass.ds(i * 2 + j, 1), :].rearrange("p o t -> p (o t)")
                    dve.tensor_tensor(own, own, sg[:, j, :], ALU.mult).then_inc(used[j], 1)
            with dve.Fori(0, KD) as i:
                out = mT[:, bass.ds(i, 1), :].rearrange("p o t -> p (o t)")
                for j, dst in enumerate((pr[:, :], out)):
                    dve.wait_ge(sig_ready[j], i + (BO * NC + 2))
                    dve.wait_ge(branch_psum[j], i + 2)
                    if j == 0:
                        dve.wait_ge(merged, i + 1)
                    dve.tensor_tensor(dst, ps_p[:, j, 0:TC], sg[:, j, 0:TC], ALU.mult).then_inc(used[j], 1)
                for j in range(2):
                    dve.wait_ge(used[j], i + (BO + 2))
                dve.tensor_tensor(out, out, pr[:, :], ALU.add).then_inc(merged, 1)
            dve.wait_ge(merged, KD + 1)


def phase_out(nc, io, mT, modT, x1T):
    with ExitStack() as ctx:
        m = Mem(nc, ctx)
        w = m.sb("w_o_ring", [P, 2, KD, P])
        ps = m.ps("ps_o_proj", [P, 2, 512])
        x_loaded = m.sem("x_again_loaded")
        w_loaded = m.sems("wo_loaded", 2)
        psum_ready = m.credited_all("o_psum", 2)
        taken = m.credited_all("o_taken", 2)
        block = ctx.enter_context(nc.Block())

        @block.scalar
        def _(act):
            act.dma_start(x1T[:, :, 0:TC], io["xT"][:, :, 0:TC]).then_inc(x_loaded, 16)

        @block.sync
        def _(sp):
            with sp.Fori(0, KD // 2) as i:
                for j in range(2):
                    sp.wait_ge(psum_ready[j], i + 1)
                    sp.dma_start(w[:, j, :, :], io["w_oT"][i * 2 + j]).then_inc(w_loaded[j], 16)

        @block.tensor
        def _(pe):
            with pe.Fori(0, KD // 2) as i:
                for j in range(2):
                    pe.wait_ge(w_loaded[j], i * 16 + 16)
                    pe.wait_ge(taken[j], i + 1)
                    for k in range(KD):
                        mm = pe.matmul(ps[:, j, 0:TC], w[:, j, k, :], mT[:, k, :], start=(k == 0), stop=(k == KD - 1))
                    mm.then_inc(psum_ready[j], 1)

        @block.vector
        def _(dve):
            dve.wait_ge(x_loaded, 16)
            with dve.Fori(0, KD // 2) as i:
                for j in range(2):
                    dve.wait_ge(psum_ready[j], i + 2)
                    own = x1T[:, bass.ds(i * 2 + j, 1), 0:TC].rearrange("p o t -> p (o t)")
                    dve.scalar_tensor_tensor(own, ps[:, j, 0:TC],
                                             modT[:, bass.ds(i * 2 + (MOD_GATE1 + j), 1), 0:1].rearrange("p o t -> p (o t)"), own,
                                             ALU.mult, ALU.add).then_inc(taken[j], 1)
            for j in range(2):
                dve.wait_ge(taken[j], KD // 2 + 1)


def phase_turn(nc, x1T, h2T, modT, ident, x1_rows, h2_rows, g2_rows):
    with ExitStack() as ctx:
        m = Mem(nc, ctx)
        gate = m.sb("gate_tiles", [P, 2, KD, P])
        row = m.sb("row_ring", [P, 4, D])
        ps = m.ps("ps_turn", [P, 4, D])
        gate_ready = m.sem("gate_ready")
        turned = m.sem("tile_turned")
        row_ready = m.sem("row_ready")
        stored = m.sems("row_stored", 4)
        block = ctx.enter_context(nc.Block())
        units = [(x1T[:, :, t * P:(t + 1) * P], [x1_rows[t]]) for t in range(FIRST)]
        units += [(h2T[:, :, t * P:(t + 1) * P], [h2_rows[t]] + [h2_rows[NT]] * (t == 0)) for t in range(FIRST)]
        units += [(gate[:, 0], [g2_rows[t] for t in range(NPT)]), (gate[:, 1], [g2_rows[NPT]])]
        stores = [0] * 4
        until = []
        for n, (_, to) in enumerate(units):
            stores[n % 4] += len(to)
            until.append(stores[n % 4])

        @block.gpsimd
        def _(pool):
            pool.tensor_copy(gate[:, 0], modT[:, MOD_GATE2:MOD_GATE2 + KD, 0:1].to_broadcast([P, KD, P])).then_inc(gate_ready, 1)
            for b in range(NB):
                pool.tensor_copy(gate[:, 1, :, b * LS:(b + 1) * LS],
                                 modT[:, MOD_GATE2:MOD_GATE2 + KD, 1 + b:2 + b].to_broadcast([P, KD, LS])).then_inc(gate_ready, 1)

        @block.tensor
        def _(pe):
            for n, (src, _) in enumerate(units):
                if n == 2 * FIRST:
                    pe.wait_ge(gate_ready, 1 + NB)
                if n >= 4:
                    pe.wait_ge(row_ready, n - 3)
                for k in range(KD):
                    mm = pe.transpose(ps[:, n % 4, k * P:(k + 1) * P], src[:, k, :], ident)
                mm.then_inc(turned, 1)

        def take(eng, n, copy):
            eng.wait_ge(turned, n + 1)
            if n >= 1:
                eng.wait_ge(row_ready, n)
            if n >= 4:
                eng.wait_ge(stored[n % 4], 16 * until[n - 4])
            copy(n).then_inc(row_ready, 1)

        @block.vector
        def _(dve):
            for n in range(0, len(units), 2):
                take(dve, n, lambda n: dve.tensor_copy(row[:, n % 4, :], ps[:, n % 4, :]))

        @block.scalar
        def _(act):
            for n in range(1, len(units), 2):
                take(act, n, lambda n: act.activation(row[:, n % 4, :], ps[:, n % 4, :], ACT.Copy))

        @block.sync
        def _(sp):
            for n, (_, to) in enumerate(units):
                sp.wait_ge(row_ready, n + 1)
                for dst in to:
                    sp.dma_start(dst, row[:, n % 4, :]).then_inc(stored[n % 4], 16)
            for j in range(4):
                sp.wait_ge(stored[j], 16 * stores[j])


def phase_retrieval_scores(nc, io, h2T, score_rows):
    with ExitStack() as ctx:
        m = Mem(nc, ctx)
        w = m.sb("w_pq_ring", [P, 2, KD, P])
        keys = m.sb("sub_keys", [P, PH, PK])
        key = m.sb("head_keys", [P, 2, PK])
        q = m.sb("head_query", [P, 2, TC])
        row = m.sb("score_ring", [P, 2, FIRST, 2 * PK])
        ps_q = m.ps("ps_query", [P, 2, 512])
        ps_s = m.ps("ps_scores", [P, 2, 2, 512])
        keys_loaded = m.sem("keys_loaded")
        w_loaded = m.sems("wpq_loaded", 2)
        key_ready = m.sems("key_ready", 2)
        q_psum = m.credited_all("q_psum", 2)
        q_ready = m.credited_all("q_ready", 2)
        s_psum = m.credited_all("s_psum", 2)
        s_taken = m.credited_all("s_taken", 2)
        stored = m.credited_all("scores_stored", 2)
        block = ctx.enter_context(nc.Block())

        @block.sync
        def _(sp):
            sp.dma_start(keys[:, :, :], io["sub_keysT"]).then_inc(keys_loaded, 16)
            with sp.Fori(0, PH // 2) as i:
                for j in range(2):
                    sp.wait_ge(q_psum[j], i + 1)
                    sp.dma_start(w[:, j, :, :], io["w_pqT"][i * 2 + j]).then_inc(w_loaded[j], 16)

        @block.gpsimd
        def _(pool):
            pool.wait_ge(keys_loaded, 16)
            with pool.Fori(0, PH // 2) as i:
                for j in range(2):
                    pool.wait_ge(s_psum[j], i + 1)
                    pool.tensor_copy(key[:, j, :], keys[:, bass.ds(i * 2 + j, 1), :].rearrange("p o t -> p (o t)")
                                     ).then_inc(key_ready[j], 1)

        @block.tensor
        def _(pe):
            with pe.Fori(0, PH // 2) as i:
                for j in range(2):
                    pe.wait_ge(w_loaded[j], i * 16 + 16)
                    pe.wait_ge(q_ready[j], i + 1)
                    for k in range(KD):
                        mm = pe.matmul(ps_q[:, j, 0:TC], w[:, j, k, :], h2T[:, k, 0:TC], start=(k == 0), stop=(k == KD - 1))
                    mm.then_inc(q_psum[j], 1)
                for j in range(2):
                    pe.wait_ge(q_ready[j], i + 2)
                    pe.wait_ge(key_ready[j], i + 1)
                    pe.wait_ge(s_taken[j], i + 1)
                    for half in range(2):
                        rows = slice(half * PHALF, (half + 1) * PHALF)
                        for t in range(FIRST):
                            mm = pe.matmul(ps_s[:, j, half, t * PK:(t + 1) * PK],
                                           q[rows, j, t * P:(t + 1) * P], key[rows, j, :], start=True, stop=True)
                    mm.then_inc(s_psum[j], 1)

        @block.scalar
        def _(act):
            with act.Fori(0, PH // 2) as i:
                for j in range(2):
                    act.wait_ge(q_psum[j], i + 2)
                    act.wait_ge(s_psum[j], i + 1)
                    act.activation(q[:, j, :], ps_q[:, j, 0:TC], ACT.Copy).then_inc(q_ready[j], 1)
                for j in range(2):
                    act.wait_ge(s_taken[j], i + 2)
                    act.dma_start(score_rows[0:FIRST, bass.ds(i * 2 + j, 1), :, :].rearrange("t o p k -> p t (o k)"),
                                  row[:, j, :, :]).then_inc(stored[j], 16)
            for j in range(2):
                act.wait_ge(stored[j], 16 * PH // 2 + 1)
            for h in range(2):
                act.dma_start(score_rows[NT, h], row[:, 0, 0, :]).then_inc(stored[0], 16)
            act.wait_ge(stored[0], 16 * PH // 2 + 32 + 1)

        @block.vector
        def _(dve):
            with dve.Fori(0, PH // 2) as i:
                for j in range(2):
                    dve.wait_ge(stored[j], i * 16 + 1)
                    dve.wait_ge(s_psum[j], i + 2)
                    dve.tensor_copy(row[:, j, :, :].rearrange("p t (s k) -> p t s k", s=2),
                                    ps_s[:, j, :, 0:FIRST * PK].rearrange("p s (t k) -> p t s k", k=PK)).then_inc(s_taken[j], 1)
            for j in range(2):
                dve.wait_ge(s_taken[j], PH // 2 + 1)


class Rest:

    def __init__(self, nc, io, m, hT, branchT, modT, A2, ident, ones, x1_rows, h2_rows, score_rows):
        self.io, self.hT, self.branchT, self.modT, self.A2, self.ident, self.ones = io, hT, branchT, modT, A2, ident, ones
        self.x1_rows, self.h2_rows, self.score_rows = x1_rows, h2_rows, score_rows
        self.bb = m.sb("b_blocks3", [P, NBLK])
        side = m.sb("rest_scratch", [P, 3328])
        two = lambda a: a.rearrange("p (j t) -> p j t", j=2)
        self.w = side[:, 0:1024].rearrange("p (k c) -> p k c", k=KD)
        self.wp = side[:, 1024:1536].rearrange("p (k c) -> p k c", k=4)
        self.sg = self.xb = self.sq = two(side[:, 1536:3072])
        self.rs = side[:, 0:768]
        self.tmp = two(side[:, 1024:1280])
        self.row = two(side[:, 1024:3072])
        self.q, self.scores, self.key = side[:, 1024:1792], side[:, 1792:2560], two(side[:, 3072:3328])
        self.ps = m.ps("ps_rest", [P, 8, 512])
        self.loaded = m.sem("rest_bias_loaded")
        self.w_loaded, self.wp_loaded = m.sem("r_wg_loaded"), m.sem("r_wp_loaded")
        self.gate_psum, self.branch_psum = m.credited_all("r_gate_psum", 2), m.credited_all("r_branch_psum", 2)
        self.sig_ready, self.used = m.credited_all("r_sig_ready", 2), m.credited_all("r_used", 2)
        self.merged = m.credited("r_merged")
        self.wo_loaded, self.x_loaded = m.sem("r_wo_loaded"), m.sems("r_x_loaded", 2)
        self.o_psum, self.o_taken = m.credited_all("r_o_psum", 2), m.credited_all("r_o_taken", 2)
        self.o_scaled = m.sems("r_o_scaled", 2)
        self.squared, self.summed = m.sem("r_squared"), m.sem("r_summed")
        self.mean_ready, self.root_ready, self.inv_ready = m.sem("r_mean"), m.sem("r_root"), m.sem("r_inv")
        self.normed, self.affine, self.scaled, self.shifted = (m.sem("r_" + n) for n in ("normed", "affine", "scaled", "shifted"))
        self.turned, self.row_ready = m.sem("r_turned"), m.sem("r_row_ready")
        self.rows_stored = m.sems("r_rows_stored", 2)
        self.key_loaded, self.wq_loaded = m.sems("r_key_loaded", 2), m.sem("r_wq_loaded")
        self.q_psum, self.q_ready = m.credited_all("r_q_psum", 2), m.credited("r_q_ready")
        self.s_psum, self.s_taken = m.credited("r_s_psum"), m.credited("r_s_taken")
        self.scores_stored = m.credited("r_scores_stored")

    TILES = NT - FIRST
    COLS = slice(TC, T)
    UNITS = 2 * (NT - FIRST)

    def chunks(self, n, j):
        return self.ps[:, n + 2 * j:n + 2 * j + 2, 0:TC]

    def sync_start(self, sp, t):
        if t == 0:
            sp.dma_start(self.bb[:, :], self.io["b_blk"]).then_inc(self.loaded, 16)
        if t == 1:
            sp.wait_ge(self.gate_psum[1], KD + 1)
            sp.wait_ge(self.merged, 2 * KD + 1)
        if t == 2:
            sp.wait_ge(self.normed, 1)

    def sync_step(self, sp, t, i, j):
        b = i * 2 + j
        if t == 0:
            for e, (blk, wname) in enumerate(((BLK_GA, "w_paT"), (BLK_GB, "w_pbT"))):
                sp.wait_ge(self.gate_psum[1 - e], i * 2 + (j + e + 1))
                sp.dma_start(self.w, self.io["w_blk"][i * 2 + (blk + j)]).then_inc(self.w_loaded, 16)
                sp.wait_ge(self.branch_psum[1 - e], i * 2 + (j + e + 1))
                sp.dma_start(self.wp, self.io[wname][b]).then_inc(self.wp_loaded, 16)
        if t == 1:
            sp.wait_ge(self.o_psum[1 - j], i + (j + 1))
            sp.dma_start(self.w, self.io["w_oT"][b]).then_inc(self.wo_loaded, 16)
            sp.wait_ge(self.o_taken[j], i * 3 + 1)
            sp.dma_start(self.xb[:, j, :], self.io["xT"][:, bass.ds(b, 1), self.COLS].rearrange("p o t -> p (o t)")
                         ).then_inc(self.x_loaded[j], 16)
        if t == 2:
            sp.wait_ge(self.q_psum[1 - j], i + (j + 1))
            if j == 0:
                sp.wait_ge(self.scores_stored, i * 64 + 1)
            sp.dma_start(self.w, self.io["w_pqT"][b]).then_inc(self.wq_loaded, 16)
            sp.wait_ge(self.s_psum, i * 2 + (j + 1))
            sp.dma_start(self.key[:, j, :], self.io["sub_keysT"][:, bass.ds(b, 1), :].rearrange("p o t -> p (o t)")
                         ).then_inc(self.key_loaded[j], 16)

    def tensor(self, pe):
        hT, branchT, ps = self.hT, self.branchT, self.ps
        with pe.Fori(0, KD) as i:
            for j in range(2):
                pe.wait_ge(self.w_loaded, i * 32 + (16 * j + 16))
                pe.wait_ge(self.sig_ready[j], i + 1)
                for k in range(KD):
                    for c in range(2):
                        mm = pe.matmul(ps[:, 2 * j + c, 0:TC], self.w[:, k, :], hT[:, k, (c + 1) * TC:(c + 2) * TC],
                                       start=(k == 0), stop=(k == KD - 1))
                mm.then_inc(self.gate_psum[j], 1)
                pe.wait_ge(self.wp_loaded, i * 32 + (16 * j + 16))
                pe.wait_ge(self.used[j], i + 1)
                for k in range(4):
                    for c in range(2):
                        mm = pe.matmul(ps[:, 4 + 2 * j + c, 0:TC], self.wp[:, k, :],
                                       branchT[:, 4 * j + k, (c + 1) * TC:(c + 2) * TC], start=(k == 0), stop=(k == 3))
                mm.then_inc(self.branch_psum[j], 1)
        pe.wait_ge(self.merged, 2 * KD + 1)
        with pe.Fori(0, KD // 2) as i:
            for j in range(2):
                pe.wait_ge(self.wo_loaded, i * 32 + (16 * j + 16))
                pe.wait_ge(self.o_taken[j], i * 3 + 1)
                for k in range(KD):
                    for c, mT in enumerate((hT, branchT)):
                        mm = pe.matmul(ps[:, 2 * j + c, 0:TC], self.w[:, k, :], mT[:, k, 0:TC],
                                       start=(k == 0), stop=(k == KD - 1))
                mm.then_inc(self.o_psum[j], 1)
        for j in range(2):
            pe.wait_ge(self.o_taken[j], KD // 2 * 3 + 1)
        for k in range(KD):
            pe.wait_ge(self.squared, k + 1)
            for c in range(2):
                mm = pe.matmul(ps[:, c, 0:TC], self.ones, self.sq[:, k % 2, c * TC:(c + 1) * TC],
                               start=(k == 0), stop=(k == KD - 1))
            mm.then_inc(self.summed, 1)

        def turn(src, units):
            for n in units:
                t = FIRST + n % self.TILES
                if n >= 2:
                    pe.wait_ge(self.row_ready, n - 1)
                for k in range(KD):
                    at = 4 + 2 * (n % 2) + k // 4
                    mm = pe.transpose(ps[:, at, k % 4 * P:(k % 4 + 1) * P], src[:, k, t * P:(t + 1) * P], self.ident)
                mm.then_inc(self.turned, 1)

        pe.wait_ge(self.affine, KD)
        pe.wait_ge(self.shifted, KD)
        turn(hT, range(self.TILES))
        pe.wait_ge(self.row_ready, self.TILES)
        pe.wait_ge(self.mean_ready, 1)
        with pe.Fori(0, PH // 2) as i:
            for j in range(2):
                pe.wait_ge(self.wq_loaded, i * 32 + (16 * j + 16))
                pe.wait_ge(self.q_ready, i * 2 + (j + 1))
                for k in range(KD):
                    for c in range(2):
                        mm = pe.matmul(ps[:, c, 0:TC], self.w[:, k, :], hT[:, k, (c + 1) * TC:(c + 2) * TC],
                                       start=(k == 0), stop=(k == KD - 1))
                mm.then_inc(self.q_psum[j], 1)
                pe.wait_ge(self.q_ready, i * 2 + (j + 2))
                pe.wait_ge(self.key_loaded[j], i * 16 + 16)
                pe.wait_ge(self.s_taken, i * 8 + (4 * j + 1))
                for half in range(2):
                    rows = slice(half * PHALF, (half + 1) * PHALF)
                    for t in range(self.TILES):
                        mm = pe.matmul(ps[:, 4 + 2 * half + t // 4, t % 4 * PK:(t % 4 + 1) * PK],
                                       self.q[rows, t * P:(t + 1) * P], self.key[rows, j, :], start=True, stop=True)
                mm.then_inc(self.s_psum, 1)
        pe.wait_ge(self.s_taken, 4 * PH + 1)
        turn(branchT, range(self.TILES, self.UNITS))

    def scalar_start(self, act, t):
        if t == 0:
            act.wait_ge(self.loaded, 16)
        if t == 2:
            for j in range(2):
                act.wait_ge(self.o_taken[j], KD // 2 * 3 + 1)
            for k in range(KD):
                if k >= 2:
                    act.wait_ge(self.summed, k - 1)
                act.activation(self.sq[:, k % 2, :], self.branchT[:, k, self.COLS], ACT.Square).then_inc(self.squared, 1)
            act.wait_ge(self.mean_ready, 1)
            act.activation(self.rs, self.rs, ACT.Sqrt).then_inc(self.root_ready, 1)
            act.wait_ge(self.normed, 1)
            for k in range(KD):
                own = self.hT[:, k, TC:SEQ]
                act.activation(own, own, ACT.Identity, bias=self.modT[:, MOD_SHIFT2 + k, 0:1],
                               scale=self.A2[:, k, 0:1]).then_inc(self.affine, 1)
            self.scalar_turn(act, self.h2_rows, range(self.TILES))

    def scalar_turn(self, act, to, units):
        for n in units:
            act.wait_ge(self.turned, n + 1)
            if n >= 2:
                act.wait_ge(self.rows_stored[n % 2], n // 2 * 16)
            act.activation(self.row[:, n % 2, :].rearrange("p (b c) -> p b c", b=2),
                           self.ps[:, 4 + 2 * (n % 2):6 + 2 * (n % 2), :], ACT.Copy).then_inc(self.row_ready, 1)
            act.wait_ge(self.row_ready, n + 1)
            act.dma_start(to[FIRST + n % self.TILES], self.row[:, n % 2, :]).then_inc(self.rows_stored[n % 2], 16)
        for j in range(2):
            act.wait_ge(self.rows_stored[j], (units[-1] + 1) // 2 * 16)

    def scalar_end(self, act, t):
        if t == FIRST - 1:
            act.wait_ge(self.scores_stored, PH * 32 + 1)
            self.scalar_turn(act, self.x1_rows, range(self.TILES, self.UNITS))

    def scalar_step(self, act, t, i, j):
        if t == 0:
            for e, blk in enumerate((BLK_GA, BLK_GB)):
                act.wait_ge(self.gate_psum[e], i * 2 + (j + 2))
                act.wait_ge(self.merged, i * 4 + (2 * j + 1))
                act.activation(self.sg[:, e, :].rearrange("p (c t) -> p c t", c=2), self.chunks(0, e), ACT.Sigmoid,
                               bias=self.bb[:, bass.ds(i * 2 + (blk + j), 1)]).then_inc(self.sig_ready[e], 1)
        if t == 2:
            act.wait_ge(self.q_psum[j], i + 2)
            act.wait_ge(self.s_psum, i * 2 + (j + 1))
            act.activation(self.q.rearrange("p (c t) -> p c t", c=2), self.chunks(0, 0), ACT.Copy).then_inc(self.q_ready, 1)
            act.wait_ge(self.s_psum, i * 2 + (j + 2))
            HT = self.TILES // 2
            for e in range(2):
                act.wait_ge(self.scores_stored, i * 64 + (32 * j + 16 * e + 1))
                for half in range(2):
                    banks = self.ps[:, 4 + 2 * half:6 + 2 * half, :].rearrange("p b c -> p (b c)")
                    act.activation(self.scores.rearrange("p (t s k) -> p t s k", s=2, k=PK)[:, :, half, :],
                                   banks[:, e * HT * PK:(e + 1) * HT * PK].rearrange("p (t k) -> p t k", k=PK),
                                   ACT.Copy).then_inc(self.s_taken, 1)
                act.wait_ge(self.s_taken, i * 8 + (4 * j + 2 * e + 3))
                act.dma_start(self.score_rows[FIRST + e * HT:FIRST + (e + 1) * HT, bass.ds(i * 2 + j, 1), :, :]
                              .rearrange("t o p k -> p t (o k)"),
                              self.scores.rearrange("p (t k) -> p t k", k=2 * PK)).then_inc(self.scores_stored, 16)

    def vector_start(self, dve, t):
        if t != 2:
            return
        for j in range(2):
            dve.wait_ge(self.o_taken[j], KD // 2 * 3 + 1)
        dve.wait_ge(self.summed, KD)
        dve.tensor_scalar(self.rs.rearrange("p (c t) -> p c t", c=2), self.chunks(0, 0), 1.0 / D, EPS,
                          ALU.mult, ALU.add).then_inc(self.mean_ready, 1)
        dve.wait_ge(self.root_ready, 1)
        dve.reciprocal(self.rs, self.rs).then_inc(self.inv_ready, 1)
        dve.wait_ge(self.inv_ready, 1)
        dve.tensor_tensor(self.hT[:, :, self.COLS], self.branchT[:, :, self.COLS],
                          self.rs.unsqueeze(1).to_broadcast([P, KD, T - TC]), ALU.mult).then_inc(self.normed, 1)
        dve.wait_ge(self.normed, 1)
        for A, op, done in ((self.A2[:, :, 1:NB + 1], ALU.mult, self.scaled),
                            (self.modT[:, MOD_SHIFT2:MOD_SHIFT2 + KD, 1:NB + 1], ALU.add, self.shifted)):
            for k in range(KD):
                if done is self.shifted:
                    dve.wait_ge(self.scaled, k + 1)
                own = self.hT[:, k, SEQ:T].rearrange("p (b l) -> p b l", l=LS)
                dve.tensor_tensor(own, own, A[:, k, :].unsqueeze(2).to_broadcast([P, NB, LS]), op).then_inc(done, 1)

    def vector_step(self, dve, t, i, j):
        b = i * 2 + j
        if t == 0:
            three = lambda a: a.rearrange("p (c t) -> p c t", c=2)
            for e, dst in enumerate((self.sg[:, 0, :], self.sg[:, 1, :])):
                dve.wait_ge(self.sig_ready[e], i * 2 + (j + 2))
                dve.wait_ge(self.branch_psum[e], i * 2 + (j + 2))
                dve.tensor_tensor(three(dst), self.chunks(4, e), three(self.sg[:, e, :]), ALU.mult).then_inc(self.used[e], 1)
            for e in range(2):
                dve.wait_ge(self.used[e], i * 2 + (j + 2))
            for c, mT in enumerate((self.hT, self.branchT)):
                dve.tensor_tensor(mT[:, bass.ds(b, 1), 0:TC].rearrange("p o t -> p (o t)"), self.sg[:, 0, c * TC:(c + 1) * TC],
                                  self.sg[:, 1, c * TC:(c + 1) * TC], ALU.add).then_inc(self.merged, 1)
        if t == 1:
            dve.wait_ge(self.o_psum[j], i + 2)
            dve.wait_ge(self.x_loaded[j], i * 16 + 16)
            x1 = lambda lo, hi: self.branchT[:, bass.ds(b, 1), lo:hi].rearrange("p o t -> p (o t)")
            gate = lambda a, z: self.modT[:, bass.ds(i * 2 + (MOD_GATE1 + j), 1), a:z].rearrange("p o t -> p (o t)")
            for c, (lo, hi) in enumerate(((TC, 2 * TC), (2 * TC, SEQ))):
                dve.scalar_tensor_tensor(x1(lo, hi), self.ps[:, 2 * j + c, 0:hi - lo], gate(0, 1), self.xb[:, j, lo - TC:hi - TC],
                                         ALU.mult, ALU.add).then_inc(self.o_taken[j], 1)
            streams = lambda a: a.rearrange("p (b l) -> p b l", l=LS)
            dve.tensor_tensor(streams(self.tmp[:, j, :]), streams(self.ps[:, 2 * j + 1, SEQ - 2 * TC:TC]),
                              gate(1, NB + 1).unsqueeze(2).to_broadcast([P, NB, LS]), ALU.mult).then_inc(self.o_scaled[j], 1)
            dve.wait_ge(self.o_scaled[j], i + 1)
            dve.tensor_tensor(x1(SEQ, T), self.tmp[:, j, :], self.xb[:, j, SEQ - TC:T - TC], ALU.add).then_inc(self.o_taken[j], 1)


def phase_experts(nc, io, hT, branchT, modT, A2, ident, ones, score_rows, x1_rows, h2_rows, g2_rows):
    K = TOPK
    HALF = K // 2
    with ExitStack() as ctx:
        m = Mem(nc, ctx)
        u = m.sb("u_rows", [P, HALF, D])
        v = m.sb("v_rows", [P, K, D])
        h2 = m.sb("h2_rows_sb", [P, D])
        g2 = m.sb("g2_rows_sb", [P, D])
        acc = m.sb("acc", [P, 2, D])
        sc = m.sb("scores", [P, 2, 2, PK])
        iota = m.sb("iota16", [P, K])
        token = m.sb("token", [1, 1])
        zero = m.sb("zero", [P, 1])
        sv = m.sb("half_best", [P, 2, K])
        si = m.sb("half_index", [P, 2, K], U32)
        sif = m.sb("half_index_f", [P, 2, K])
        cand = m.sb("cand", [P, K, K])
        fv = m.sb("best", [P, 2, K])
        fi = m.sb("best_at", [P, K], U32)
        ab = m.sb("best_pair", [P, 2, K], U32)
        hot = m.sb("hot", [P, 2, K, K])
        pick = m.sb("picked_f", [P, 2, K])
        pick_u = m.sb("picked", [P, 2, 2, K], U32)
        eidx = m.sb("expert_index", [P, 2, K], U32)
        neg = m.sb("neg_best", [P, 2])
        g = m.sb("gates16", [P, 2, K])
        gsum = m.sb("gates_sum", [P, 2])
        ginv = m.sb("gates_inv", [P, 2])
        dot = m.sb("dots", [P, 2, K])
        actv = m.sb("gelu", [P, 2, K])
        wgt = m.sb("weights", [P, 2, K])
        iota_loaded = m.sem("iota_loaded")
        tables_ready = m.sem("tables_ready")
        zero_set = m.sem("zero_set")
        sc_loaded = m.sem("sc_loaded")
        u_loaded, v_loaded = m.sems("u_loaded", HALF), m.sems("v_loaded", K)
        u_used, v_used = m.credited_all("u_used", HALF), m.credited_all("v_used", K)
        chosen = m.sem("chosen")
        sc_used = m.credited("sc_used")
        best_ready = m.sem("best_ready")
        exp_ready = m.sem("exp_ready")
        ginv_ready = m.sem("ginv_ready")
        g_ready = m.sem("g_ready")
        pick_ready = m.sem("pick_ready")
        idx_ready = m.sem("idx_ready")
        dots_ready = u_used[HALF - 1]
        dots_of = lambda units: units * 2 + 1
        gelu_ready = m.sem("gelu_ready")
        wgt_ready = m.sem("wgt_ready")
        acc_zeroed = m.sem("acc_zeroed")
        h2_loaded = m.sem("h2_loaded")
        g2_loaded = m.sem("g2_loaded")
        joined = m.sem("joined")
        combined = m.credited("combined")
        stored = m.credited("y_stored")
        rest = Rest(nc, io, m, hT, branchT, modT, A2, ident, ones, x1_rows, h2_rows, score_rows)
        block = ctx.enter_context(nc.Block())
        nothing = lambda *_: None

        def over_units(eng, per_unit, tile_start=nothing, tile_end=nothing, rest_start=nothing, rest_step=nothing,
                       rest_end=nothing):
            for t in range(FIRST):
                rest_start(eng, t)
                tile_start(t)
                with eng.Fori(0, PH // 2) as i:
                    for j in range(2):
                        per_unit(t, i * 2 + (t * PH + j), j)
                        rest_step(eng, t, i, j)
                rest_end(eng, t)
                tile_end(t)
            with eng.Fori(0, NT - FIRST) as r:
                tile_start(r + FIRST)
                with eng.Fori(0, PH // 2) as i:
                    for j in range(2):
                        per_unit(r + FIRST, r * PH + i * 2 + (FIRST * PH + j), j)
                tile_end(r + FIRST)

        @block.tensor
        def _(pe):
            rest.tensor(pe)

        flat = score_rows.rearrange("t h p k -> (t h) p k")

        @block.sync
        def _(sp):
            sp.dma_start(iota[:, :], io["iota16"]).then_inc(iota_loaded, 16)
            sp.dma_start(h2[:, :], h2_rows[0]).then_inc(h2_loaded, 16)
            for n in range(2):
                if n:
                    sp.wait_ge(sc_loaded, 16)
                sp.dma_start(sc[:, n, :, :], flat[n].rearrange("p (s k) -> p s k", s=2)).then_inc(sc_loaded, 16)

            def tile_start(t):
                sp.wait_ge(combined, t + 1)
                sp.dma_start(g2[:, :], g2_rows[t]).then_inc(g2_loaded, 16)

            def unit(t, n, j):
                sp.wait_ge(sc_used, n + 2)
                sp.wait_ge(sc_loaded, n * 16 + 32)
                sp.dma_start(sc[:, j, :, :], flat[n + 2].rearrange("p (s k) -> p s k", s=2)).then_inc(sc_loaded, 16)

            def tile_end(t):
                sp.wait_ge(dots_ready, dots_of(t * PH + PH))
                sp.dma_start(h2[:, :], x1_rows[t]).then_inc(h2_loaded, 16)
                if t is FIRST - 1:
                    for j in range(2):
                        sp.wait_ge(rest.rows_stored[j], rest.TILES // 2 * 16)
                    sp.wait_ge(rest.scores_stored, PH * 32 + 1)
                sp.wait_ge(combined, t + 2)
                sp.dma_start(h2[:, :], h2_rows[t + 1]).then_inc(h2_loaded, 16)
                sp.dma_start(io["y"][t], acc[:, 0, :]).then_inc(stored, 16)
                if t is FIRST - 1:
                    for j in range(2):
                        sp.wait_ge(rest.rows_stored[j], rest.UNITS // 2 * 16)

            over_units(sp, unit, tile_start, tile_end, rest.sync_start, rest.sync_step)
            sp.wait_ge(stored, NT * 16 + 1)
            sp.wait_ge(h2_loaded, NT * 32 + 16)
            sp.wait_ge(sc_loaded, NT * PH * 16 + 32)

        @block.gpsimd
        def _(pool):
            pool.memset(token[:, :], 0.0).then_inc(tables_ready, 1)

            def unit(t, n, j):
                pool.wait_ge(best_ready, n + 1)
                pool.wait_ge(u_used[0], dots_of(n))
                pool.wait_ge(pick_ready, n * 2 + 2)
                for e in range(2):
                    cut = slice(e * HALF, (e + 1) * HALF)
                    pool.tensor_tensor(eidx[:, j, cut], pick_u[:, j, 0, cut], pick_u[:, j, 1, cut], ALU.add).then_inc(idx_ready, 1)
                pool.wait_ge(tables_ready, 1)
                pool.wait_ge(idx_ready, n * 2 + 2)

                def gather(rows, table, k, loaded):
                    pool.indirect_dma_start(rows, None, io[table],
                                            bass.IndirectOffsetOnAxis(ap=eidx[:, j, k:k + 1], axis=0)).then_inc(loaded, 16)

                for half in range(2):
                    for k in range(half * HALF, (half + 1) * HALF):
                        slot = k % HALF
                        if k % 2 == 0:
                            pool.wait_ge(tables_ready, 1)
                            pool.wait_ge(u_used[slot + 1], n * 2 + (half + 1))
                        gather(u[:, slot, :], "expert_u", k, u_loaded[slot])
                    for k in range(half * HALF, (half + 1) * HALF):
                        if k % 4 == 0:
                            pool.wait_ge(tables_ready, 1)
                            pool.wait_ge(v_used[k + 3], n + 1)
                        gather(v[:, k, :], "expert_v", k, v_loaded[k])

            over_units(pool, unit)

        @block.scalar
        def _(act):
            def weigh(n, j):
                act.wait_ge(best_ready, n + 1)
                act.activation(g[:, j, :], fv[:, j, :], ACT.Exp, bias=neg[:, j:j + 1],
                               accum_out=gsum[:, j:j + 1]).then_inc(exp_ready, 1)

            def tile_start(t):
                act.wait_ge(combined, t + 1)
                act.wait_ge(stored, t * 16 + 1)
                act.activation(acc[:, :, :].rearrange("p a d -> p (a d)"), zero[:, :].to_broadcast([P, 2 * D]),
                               ACT.Copy).then_inc(acc_zeroed, 1)

            def unit(t, n, j):
                weigh(n + 1, 1 - j)
                act.wait_ge(dots_ready, dots_of(n + 1))
                act.activation(actv[:, j, :], dot[:, j, :], ACT.Gelu).then_inc(gelu_ready, 1)

            act.wait_ge(zero_set, 1)
            weigh(0, 0)
            over_units(act, unit, tile_start, nothing, rest.scalar_start, rest.scalar_step, rest.scalar_end)

        @block.vector
        def _(dve):
            def choose(n, j):
                s = Steps(dve, chosen)
                step = lambda ins: (s.did(ins), s.settle())
                dve.wait_ge(sc_loaded, n * 16 + 16)
                step(dve.tensor_copy(sif[:, :, :], sc[:, j, :, 0:K]))
                for half in range(2):
                    a = sc[:, j, half, :]
                    step(dve.max(sv[:, half, 0:8], a))
                    s.did(dve.max_index(si[:, half, 0:8], sv[:, half, 0:8], a))
                    step(dve.match_replace(a, sv[:, half, 0:8], a, -3e38))
                    step(dve.max(sv[:, half, 8:16], a))
                    step(dve.max_index(si[:, half, 8:16], sv[:, half, 8:16], a))
                s.did(dve.tensor_scalar(sif[:, 0, :], si[:, 0, :], float(PK), None, ALU.mult))
                step(dve.tensor_copy(sif[:, 1, :], si[:, 1, :]))
                dve.tensor_tensor(cand[:, :, :], sv[:, 0, :].unsqueeze(2).to_broadcast([P, K, K]),
                                  sv[:, 1, :].unsqueeze(1).to_broadcast([P, K, K]), ALU.add).then_inc(sc_used, 1)
                dve.wait_ge(sc_used, n + 2)
                step(dve.tensor_copy(neg[:, j:j + 1], cand[:, 0, 0:1]))
                c = cand[:, :, :].rearrange("p a b -> p (a b)")
                step(dve.max(fv[:, j, 0:8], c))
                s.did(dve.max_index(fi[:, 0:8], fv[:, j, 0:8], c))
                step(dve.match_replace(c, fv[:, j, 0:8], c, -3e38))
                step(dve.max(fv[:, j, 8:16], c))
                s.did(dve.max_index(fi[:, 8:16], fv[:, j, 8:16], c))
                dve.tensor_scalar(neg[:, j:j + 1], fv[:, j, 0:1], -1.0, None, ALU.mult).then_inc(best_ready, 1)
                s.settle()
                s.did(dve.tensor_scalar(ab[:, 0, :], fi[:, :], 4, None, ALU.logical_shift_right))
                step(dve.tensor_scalar(ab[:, 1, :], fi[:, :], 15, None, ALU.bitwise_and))
                for half in range(2):
                    s.did(dve.tensor_tensor(hot[:, half], ab[:, half, :].unsqueeze(2).to_broadcast([P, K, K]),
                                            iota[:, :].unsqueeze(1).to_broadcast([P, K, K]), ALU.is_equal))
                s.settle()
                for half in range(2):
                    s.did(dve.tensor_tensor(hot[:, half], hot[:, half],
                                            sif[:, half, :].unsqueeze(1).to_broadcast([P, K, K]), ALU.mult))
                s.settle()
                step(dve.tensor_reduce(pick[:, :, :], hot[:, :, :, :], AX.X, ALU.add))
                for half in range(2):
                    dve.tensor_copy(pick_u[:, j, half, :], pick[:, half, :]).then_inc(pick_ready, 1)
                s.settle()

            def normalise(n, j):
                dve.wait_ge(exp_ready, n + 1)
                dve.reciprocal(ginv[:, j:j + 1], gsum[:, j:j + 1]).then_inc(ginv_ready, 1)
                dve.wait_ge(ginv_ready, n + 1)
                dve.tensor_scalar(g[:, j, :], g[:, j, :], ginv[:, j:j + 1], None, ALU.mult).then_inc(g_ready, 1)

            def unit(t, n, j):
                choose(n + 1, 1 - j)
                dve.wait_ge(h2_loaded, t * 32 + 16)
                for k in range(K):
                    half, slot = divmod(k, HALF)
                    dve.wait_ge(u_loaded[slot], n * 32 + (half * 16 + 16))
                    dve.tensor_tensor_reduce(u[:, slot, :], u[:, slot, :], h2[:, :], 1.0, 0.0, ALU.mult, ALU.add,
                                             dot[:, j, k:k + 1]).then_inc(u_used[slot], 1)
                dve.sem_clear(chosen)
                normalise(n + 1, 1 - j)
                dve.wait_ge(gelu_ready, n + 1)
                dve.wait_ge(g_ready, n + 1)
                dve.tensor_tensor(wgt[:, j, :], actv[:, j, :], g[:, j, :], ALU.mult).then_inc(wgt_ready, 1)
                dve.wait_ge(wgt_ready, n + 1)
                dve.wait_ge(acc_zeroed, t + 1)
                for k in range(K):
                    dve.wait_ge(v_loaded[k], n * 16 + 16)
                    if k >= 2:
                        dve.wait_ge(v_used[k - 2], n + 2)
                    dve.scalar_tensor_tensor(acc[:, k % 2, :], v[:, k, :], wgt[:, j, k:k + 1], acc[:, k % 2, :],
                                             ALU.mult, ALU.add).then_inc(v_used[k], 1)
                for k in (K - 2, K - 1):
                    dve.wait_ge(v_used[k], n + 2)

            def tile_end(t):
                dve.tensor_tensor(acc[:, 0, :], acc[:, 0, :], acc[:, 1, :], ALU.add).then_inc(joined, 1)
                dve.wait_ge(g2_loaded, t * 16 + 16)
                dve.wait_ge(joined, t * 2 + 1)
                dve.tensor_tensor(acc[:, 0, :], acc[:, 0, :], g2[:, :], ALU.mult).then_inc(joined, 1)
                dve.wait_ge(joined, t * 2 + 2)
                dve.wait_ge(h2_loaded, t * 32 + 32)
                dve.tensor_tensor(acc[:, 0, :], acc[:, 0, :], h2[:, :], ALU.add).then_inc(combined, 1)

            dve.wait_ge(iota_loaded, 16)
            dve.memset(zero[:, :], 0.0).then_inc(zero_set, 1)
            choose(0, 0)
            dve.sem_clear(chosen)
            normalise(0, 0)
            over_units(dve, unit, nothing, tile_end, rest.vector_start, rest.vector_step)
            dve.wait_ge(combined, NT + 1)


def build(nc, io, upto=99):
    scratch = lambda name, shape: nc.dram_tensor(name, shape, F32).ap()
    x1_rows = scratch("x1_rows", (NT, P, D))
    h2_rows = scratch("h2_rows", (NT + 1, P, D))
    g2_rows = scratch("g2_rows", (NT, P, D))
    score_rows = scratch("score_rows", (NT + 1, PH, P, 2 * PK))
    with ExitStack() as whole:
        g = Mem(nc, whole)
        consts = g.sb("consts", [P, 2 * P])
        ident, ones = consts[:, 0:P], consts[:, P:2 * P]
        modT = g.sb("modT", [P, 6 * KD, NB + 1])
        A1 = g.sb("A1", [P, KD, NB + 1])
        A2 = g.sb("A2", [P, KD, NB + 1])
        phase_constants(nc, io["consts"][:, 0:2 * P], "constants", consts)
        phase_modulation(nc, io, modT, A1, A2, ident)
        if upto < 2:
            return
        hT = g.sb("hT", [P, KD, T])
        phase_norm(nc, io, "1", hT, hT, True, ones, A1, modT, 0)
        if upto < 3:
            return
        branchT = g.sb("branchT", [P, 8, T])
        haT, hbT = branchT[:, 0:4, :], branchT[:, 4:8, :]
        forget = ExitStack(); f = Mem(nc, forget)
        masks = f.sb("masks", [P, 12 * P])
        pair_ones, causal, causalT, stream_rows = (masks[:, n * P:(n + 1) * P] for n in range(4))
        head_rows = masks[:, 4 * P:12 * P].rearrange("p (h t) -> p h t", h=AH)
        phase_constants(nc, io["consts"][:, 2 * P:14 * P], "masks", masks)
        gates = f.sb("gates", [GATE_W, T])
        lf = f.sb("lf", [GATE_W, T])
        attn = ExitStack(); a = Mem(nc, attn)
        qk = a.sb("qkT", [P, 8, T])
        va = a.sb("va", [P, NT, AH * AD])
        gqk = a.sb("gqk", [P, 8])
        negF = a.sb("negF", [AH, SEQ])
        negFc = a.sb("negFc", [AH, NB * PAST])
        negFn = a.sb("negFn", [AH, NB * LS])
        phase_project(nc, io, "A", BLK_Q, hT, qk, [])
        phase_values_gates_norms(nc, io, hT, qk, gqk, va, gates, lf, negF, negFc, negFn, pair_ones)
        phase_attend_prompt(nc, io, qk, va, negF, haT, ident, causal, head_rows)
        phase_attend_streams(nc, io, qk, va, negFc, negFn, haT, hbT.rearrange("p b t -> p (b t)"), ident, stream_rows)
        attn.close()
        mem = ExitStack(); b = Mem(nc, mem)
        rows = b.sb("mlstm_rows", [BH, 2, T])
        cols = b.sb("mlstm_cols", [P, 3, NT, BH])
        phase_mlstm_rows(nc, io, gates, lf, rows, cols)
        qkb = b.sb("qkbT", [P, 8, T])
        kb = b.sb("kb", [P, NT, BH * BD])
        vb = b.sb("vb", [P, NT, BH, BD + 1])
        phase_ones(nc, vb)
        phase_project(nc, io, "B", BLK_QB, hT, qkb, [(1, kb), (2, vb)])
        phase_mlstm(nc, io, qkb, kb, vb, rows, cols, hbT, ident, causalT, head_rows)
        mem.close()
        forget.close()
        first = ExitStack()
        mT = Mem(nc, first).sb("mergedT", [P, KD, TC])
        phase_merge(nc, io, hT, haT, hbT, mT)
        phase_out(nc, io, mT, modT, branchT)
        first.close()
        phase_norm(nc, io, "2", branchT, hT, False, ones, A2, modT, MOD_SHIFT2, 1)
        phase_turn(nc, branchT, hT, modT, ident, x1_rows, h2_rows, g2_rows)
        phase_retrieval_scores(nc, io, hT, score_rows)
        phase_experts(nc, io, hT, branchT, modT, A2, ident, ones, score_rows, x1_rows, h2_rows, g2_rows)


_DEV = 99
_OUTS = [("new_v", (P, NT, AH * AD)), ("new_kT", (P, 4, T)), ("new_logfT", (AH, T)),
         ("new_mT", (BH, NB + 1)), ("new_C_prompt", (BH, P, BD + 1)), ("new_C_sample", (BH, P, NB, BD + 1)),
         ("y", (NT, P, D))]


def kernel(**a):
    import concourse.bacc as bacc
    from concourse.bass_utils import run_bass_kernel_spmd

    def cols(w, n):
        k = w.shape[0] // P
        return w.reshape(k, P, n, P).transpose(2, 1, 0, 3).reshape(n, P, k * P)

    def on_rows(v):
        return v.reshape(-1, P).T

    f = {k: np.asarray(v) for k, v in a.items()}
    w_in, b_in = f["w_in"][0], f["b_in"][0]
    off = np.cumsum([0, 512, 512, 512, 8, 512, 512, 512, 4, 4, 512, 1024, 1024])
    cut = lambda i: slice(int(off[i]), int(off[i + 1]))
    x = np.concatenate([f["x_prompt"].reshape(SEQ, D), f["x_sample"].reshape(NB * LS, D)])
    c = np.concatenate([f["c_prompt"], f["c_sample"]])
    order = (0, 1, 4, 5, 9, 10, 11)
    w_blk = np.concatenate([w_in[:, cut(i)] for i in order], 1)
    b_blk = np.concatenate([b_in[cut(i)] for i in order])
    w_gate, b_gate = np.zeros((D, GATE_W), np.float32), np.zeros((GATE_W, 1), np.float32)
    for row, i in ((GATE_F, 3), (GATE_I, 7), (GATE_LF, 8)):
        w_gate[:, row:row + int(off[i + 1] - off[i])] = w_in[:, cut(i)]
        b_gate[row:row + int(off[i + 1] - off[i]), 0] = b_in[cut(i)]
    rows = lambda w: w.reshape(KD, P, -1).transpose(1, 0, 2)
    eye = np.eye(P, dtype=np.float32)
    pair = np.kron(np.eye(2), np.ones((AD, AD))).astype(np.float32)
    n = np.arange(P)
    causal = np.where(n[None, :] <= n[:, None], 0.0, NEG).astype(np.float32)
    stream_rows = (n[:, None] == n[None, :] // LS).astype(np.float32)
    head_rows = np.repeat(np.eye(P, AH, dtype=np.float32), P, 1)
    stream_masks = np.where((n[None, None, :] // LS == np.arange(NB)[None, :, None])
                            & (n[None, None, :] % LS <= n[:, None, None] % LS), 0.0, NEG).astype(np.float32)
    own = (n[None, :] // LS == np.arange(NB)[:, None]).astype(np.float32)
    start = np.array([t % P == 0 if t < SEQ else t % LS == 0 for t in range(T)], np.float32)
    arrays = {
        "consts": np.concatenate([eye, np.ones((P, P), np.float32), pair, causal, causal.T, stream_rows, head_rows], 1),
        "stream_masks": stream_masks,
        "stream_maskT": np.where((n[:, None] // LS == n[None, :] // LS) & (n[:, None] <= n[None, :]), 0.0, NEG).astype(np.float32),
        "own_stream": np.broadcast_to(own[None], (P, NB, P)),
        "own_rows": own.T,
        "scan_rows": np.broadcast_to(np.stack([1.0 - start, np.where(np.arange(T) >= SEQ, start * NEG, 0.0)]).astype(np.float32)[None], (BH, 2, T)),
        "state_mT": f["state_m"][0].T,
        "state_C": np.concatenate([f["state_C"][0].transpose(1, 2, 0, 3), f["state_n"][0].transpose(1, 2, 0)[..., None]], 3),
        "g_hbT": f["g_hb"][0].T,
        "w_oT": cols(f["w_o"][0], KD).reshape(KD, P, KD, P),
        "w_pqT": cols(f["w_pq"][0], PH).reshape(PH, P, KD, P),
        "sub_keysT": f["sub_keys"][0].transpose(1, 3, 0, 2).reshape(P, PH, PK),
        "iota16": np.broadcast_to(np.arange(TOPK, dtype=np.float32)[None], (P, TOPK)),
        "expert_u": f["expert_u"][0],
        "expert_v": f["expert_v"][0],
        "w_paT": cols(f["w_pa"][0], KD).reshape(KD, P, 4, P),
        "w_pbT": cols(f["w_pb"][0], KD).reshape(KD, P, 4, P),
        "g_qk": np.concatenate([on_rows(f["g_qa"].reshape(-1)), on_rows(f["g_ka"].reshape(-1))], 1),
        "cache_logfT": f["cache_logf"][0].transpose(2, 0, 1).reshape(AH, NB * PAST),
        "cache_kT": f["cache_k"][0].reshape(NB, PAST, 4, P).transpose(0, 3, 2, 1),
        "cache_v": f["cache_v"][0].reshape(NB, 4, P, AH * AD).transpose(0, 2, 1, 3),
        "cT": c.T.reshape(KD, P, NB + 1).transpose(1, 0, 2),
        "w_mod": f["w_mod"][0].reshape(KD, P, 12, 512).transpose(2, 1, 0, 3).reshape(12, P, KD, 512),
        "b_mod": on_rows(f["b_mod"][0]),
        "g12": np.stack([on_rows(f["g_norm1"][0]), on_rows(f["g_norm2"][0])], 1),
        "xT": x.T.reshape(KD, P, T).transpose(1, 0, 2),
        "w_blk": cols(w_blk, NBLK).reshape(NBLK, P, KD, P),
        "b_blk": on_rows(b_blk),
        "w_row": np.stack([rows(w_in[:, cut(i)]) for i in (2, 5, 6)]),
        "b_row": np.stack([b_in[cut(i)] for i in (2, 5, 6)]),
        "w_gate": rows(w_gate),
        "b_gate": b_gate,
    }
    nc = bacc.Bacc("TRN2", target_bir_lowering=False, num_devices=1)
    io, feed = {}, {}
    for name, v in arrays.items():
        v = np.ascontiguousarray(v)
        feed["in_" + name] = v
        io[name] = nc.dram_tensor("in_" + name, v.shape, mybir.dt.from_np(v.dtype), kind="ExternalInput").ap()
    for name, shape in _OUTS:
        io[name] = nc.dram_tensor("out_" + name, shape, F32, kind="ExternalOutput").ap()
    build(nc, io, _DEV)
    r = run_bass_kernel_spmd(nc, [feed], core_ids=[0]).results[0]
    got = {name: r["out_" + name] for name, _ in _OUTS}
    y = got["y"].reshape(T, D)
    k = got["new_kT"].transpose(2, 1, 0).reshape(T, AH, AD)
    v = got["new_v"].transpose(1, 0, 2).reshape(T, AH, AD)
    lf = got["new_logfT"].T
    st, ss, mm = got["new_C_prompt"], got["new_C_sample"].transpose(2, 0, 1, 3), got["new_mT"]
    whole = lambda a: np.ascontiguousarray(a[None])
    prompt = lambda a: whole(a[None, 0:SEQ])
    sample = lambda a: whole(a[SEQ:T].reshape((NB, LS) + a.shape[1:]))
    return (np.ascontiguousarray(y[None, 0:SEQ]), np.ascontiguousarray(y[SEQ:T].reshape(NB, LS, D)),
            prompt(k), prompt(v), prompt(lf), whole(st[None, :, :, 0:BD]), whole(st[None, :, :, BD]), whole(mm[:, 0][None]),
            sample(k), sample(v), sample(lf), whole(ss[..., 0:BD]), whole(ss[..., BD]), whole(mm[:, 1:].T))
```
